# Optimizing a Trainium2 kernel written in Bass

```python
import math
import jax, jax.numpy as jnp
from jax import lax
import numpy as np

D_MODEL = 1024
BATCH = 1
SEQ = 512
DEPTH = 2
DEC_BATCH = 8
DEC_SEQ = 1
PAST_LEN = 512
PAGE_SIZE = 128

N_EVEN = (DEPTH + 1) // 2
N_ODD = DEPTH // 2
RMS_EPS = 1e-6
NEG = -1e30

HEAD_DIM = 64
A_HEADS = 8
A_WIDTH = A_HEADS * HEAD_DIM
A_BRANCHES = ((128, 1), (512, 4), (2048, 16))
A_MAX_WINDOW = 2048
A_KEYS = 128
A_BLOCK = 128

POOL_WINDOWS = (2, 4, 8, 16)
POOL_GROUPS = 4
POOL_WIDTH = D_MODEL - A_WIDTH
POOL_GROUP_DIM = POOL_WIDTH // POOL_GROUPS
POOL_HIST = max(POOL_WINDOWS) - 1
EVEN_IN = 3 * A_WIDTH + POOL_WIDTH
EVEN_MIX = A_WIDTH + POOL_WIDTH

GDN_HEADS = 8
GDN_DK = 128
GDN_DV = 128
GDN_QK = GDN_HEADS * GDN_DK
GDN_VW = GDN_HEADS * GDN_DV
GDN_CONV_CH = 2 * GDN_QK + GDN_VW
CONV_WIDTH = 4
GDN_CHUNK = 64
ODD_IN = GDN_CONV_CH + GDN_VW + 2 * GDN_HEADS

FFN_HIDDEN = -(-8 * D_MODEL // (3 * 256)) * 256

kernel_name = 'hybrid_dilated_pool_gdn_decoder_step'

F32 = jnp.float32

def _rmsnorm(x, g):
    xf = x.astype(F32)
    y = xf * lax.rsqrt(jnp.mean(xf * xf, axis=-1, keepdims=True) + RMS_EPS)
    return (y * g.astype(F32)).astype(x.dtype)

def _l2norm(x):
    return x * lax.rsqrt(jnp.sum(x * x, axis=-1, keepdims=True) + 1e-6)

def _alibi_slopes(n):
    return jnp.exp2(-8.0 * (jnp.arange(n, dtype=F32) + 1.0) / n)

def _swiglu(h, wg, wu, wd):
    return (jax.nn.silu(h @ wg) * (h @ wu)) @ wd

def _dilated_branch_prompt(q, k, v, dil, slopes):
    b, s, h, dh = q.shape
    span = dil * A_BLOCK
    s_pad = -(-s // span) * span
    L = s_pad // dil
    nb = L // A_BLOCK

    def res_blocks(a):
        a = jnp.pad(a, ((0, 0), (0, s_pad - s), (0, 0), (0, 0)))
        a = a.reshape(b, L, dil, h, dh).transpose(0, 2, 1, 3, 4)
        return a.reshape(b * dil, nb, A_BLOCK, h, dh)

    def with_prev(a):
        prev = jnp.pad(a, ((0, 0), (1, 0), (0, 0), (0, 0), (0, 0)))[:, :-1]
        return jnp.concatenate([prev, a], axis=2)

    qb = res_blocks(q).astype(F32)
    kk = with_prev(res_blocks(k)).astype(F32)
    vv = with_prev(res_blocks(v)).astype(F32)
    scores = jnp.einsum('znqhd,znkhd->znhqk', qb, kk) * (HEAD_DIM ** -0.5)
    rel = jnp.arange(A_BLOCK)[:, None] + A_BLOCK - jnp.arange(2 * A_BLOCK)[None, :]
    band = (rel >= 0) & (rel <= A_KEYS)
    key_idx = jnp.arange(nb)[:, None] * A_BLOCK - A_BLOCK + jnp.arange(2 * A_BLOCK)[None, :]
    mask = band[None] & (key_idx >= 0)[:, None, :]
    bias = -slopes[:, None, None] * (rel * dil).astype(F32)[None]
    scores = jnp.where(mask[None, :, None], scores + bias[None, None], NEG)
    m = jnp.max(scores, axis=-1, keepdims=True)
    p = jnp.exp(scores - m)
    l = jnp.sum(p, axis=-1, keepdims=True)
    o = jnp.einsum('znhqk,znkhd->znhqd', p, vv) / l
    lse = (m + jnp.log(l))[..., 0]
    o = o.transpose(0, 1, 3, 2, 4).reshape(b, dil, L, h, dh).transpose(0, 2, 1, 3, 4)
    o = o.reshape(b, s_pad, h, dh)[:, :s]
    lse = lse.transpose(0, 1, 3, 2).reshape(b, dil, L, h).transpose(0, 2, 1, 3)
    lse = lse.reshape(b, s_pad, h)[:, :s]
    return o, lse

def _dilated_branch_decode(q, kx, vx, n_hist, dil, slopes):
    t = q.shape[1]
    j = jnp.arange(A_KEYS + 1)
    idx = n_hist + jnp.arange(t)[:, None] - dil * j[None, :]
    valid = idx >= 0
    idx = jnp.maximum(idx, 0)
    kg = kx[:, idx].astype(F32)
    vg = vx[:, idx].astype(F32)
    scores = jnp.einsum('bthd,btjhd->bthj', q.astype(F32), kg) * (HEAD_DIM ** -0.5)
    scores = scores - slopes[:, None] * (dil * j).astype(F32)[None, :]
    scores = jnp.where(valid[None, :, None, :], scores, NEG)
    m = jnp.max(scores, axis=-1, keepdims=True)
    p = jnp.exp(scores - m)
    l = jnp.sum(p, axis=-1, keepdims=True)
    o = jnp.einsum('bthj,btjhd->bthd', p, vg) / l
    lse = (m + jnp.log(l))[..., 0]
    return o, lse

def _mix_dilations(res):
    o = jnp.stack([r[0] for r in res], axis=0)
    lse = jnp.stack([r[1] for r in res], axis=0)
    w = jax.nn.softmax(lse, axis=0)
    return jnp.einsum('rbth,rbthd->bthd', w, o)

def _pool_mixer(u, hist, pos0, w_pool, scale):
    b, t, c = u.shape
    ux = jnp.concatenate([hist, u], axis=1)
    uf = ux.astype(F32)
    cs = jnp.concatenate([jnp.zeros((b, 1, c), F32), jnp.cumsum(uf, axis=1)], axis=1)
    end = cs[:, POOL_HIST + 1:]
    cur = uf[:, POOL_HIST:]
    pos = pos0 + jnp.arange(t)
    outs = []
    for g, w in enumerate(POOL_WINDOWS):
        sl = slice(g * POOL_GROUP_DIM, (g + 1) * POOL_GROUP_DIM)
        start = cs[:, POOL_HIST + 1 - w:POOL_HIST + 1 - w + t, sl]
        cnt = jnp.minimum(pos + 1, w).astype(F32)[None, :, None]
        pooled = (end[..., sl] - start) / cnt - cur[..., sl]
        outs.append(jnp.einsum('btc,cd->btd', pooled, w_pool[g].astype(F32)))
    y = jnp.concatenate(outs, axis=-1) * scale.astype(F32)
    return y, ux[:, -POOL_HIST:]

def _even_mixer(h, k_buf, v_buf, pool_hist, pos0, w_in, w_out, w_pool, scale, slopes):
    b, t, _ = h.shape
    z = h @ w_in
    q = z[..., :A_WIDTH].reshape(b, t, A_HEADS, HEAD_DIM)
    k = z[..., A_WIDTH:2 * A_WIDTH].reshape(b, t, A_HEADS, HEAD_DIM)
    v = z[..., 2 * A_WIDTH:3 * A_WIDTH].reshape(b, t, A_HEADS, HEAD_DIM)
    u = z[..., 3 * A_WIDTH:]
    if k_buf is None:
        res = [_dilated_branch_prompt(q, k, v, dil, slopes) for _, dil in A_BRANCHES]
        keep = min(A_MAX_WINDOW, t)
        new_k, new_v = k[:, t - keep:], v[:, t - keep:]
    else:
        n_hist = k_buf.shape[1]
        kx = jnp.concatenate([k_buf, k], axis=1)
        vx = jnp.concatenate([v_buf, v], axis=1)
        res = [_dilated_branch_decode(q, kx, vx, n_hist, dil, slopes) for _, dil in A_BRANCHES]
        keep = min(A_MAX_WINDOW, n_hist + t)
        new_k, new_v = kx[:, n_hist + t - keep:], vx[:, n_hist + t - keep:]
    attn = _mix_dilations(res).reshape(b, t, A_WIDTH)
    pooled, new_pool = _pool_mixer(u, pool_hist, pos0, w_pool, scale)
    y = jnp.concatenate([attn, pooled], axis=-1).astype(h.dtype) @ w_out
    return y, new_k, new_v, new_pool

def _short_conv(xr, hist, w):
    xx = jnp.concatenate([hist, xr], axis=1)
    y = lax.conv_general_dilated(xx, w[:, None, :], window_strides=(1,), padding='VALID',
                                 dimension_numbers=('NWC', 'WIO', 'NWC'),
                                 feature_group_count=xr.shape[-1])
    return jax.nn.silu(y), xx[:, -(CONV_WIDTH - 1):]

def _gated_delta_chunked(q, k, v, g, beta, s0):
    b, t, h, dk = q.shape
    dv = v.shape[-1]
    c = min(GDN_CHUNK, t)
    tp = -(-t // c) * c
    n = tp // c

    def chunks(a):
        a = jnp.pad(a, ((0, 0), (0, tp - t)) + ((0, 0),) * (a.ndim - 2))
        a = a.reshape((b, n, c) + a.shape[2:])
        return a.transpose(1, 0, 3, 2, 4) if a.ndim == 5 else a.transpose(1, 0, 3, 2)

    qc, kc, vc = chunks(q), chunks(k), chunks(v)
    gc = jnp.cumsum(chunks(g), axis=-1)
    bc = chunks(beta)
    kb = kc * bc[..., None]
    vb = vc * bc[..., None]
    ar = jnp.arange(c)
    tril = ar[:, None] >= ar[None, :]
    strict = ar[:, None] > ar[None, :]
    diff = gc[..., :, None] - gc[..., None, :]
    decay = jnp.where(tril, jnp.exp(jnp.where(tril, diff, 0.0)), 0.0)
    lmat = jnp.where(strict, jnp.einsum('nbhid,nbhjd->nbhij', kb, kc) * decay, 0.0)
    eye = jnp.eye(c, dtype=F32)
    tinv = lax.linalg.triangular_solve(eye + lmat, jnp.broadcast_to(eye, lmat.shape),
                                       left_side=True, lower=True)
    u = tinv @ vb
    w = tinv @ (kb * jnp.exp(gc)[..., None])
    a_intra = jnp.where(tril, jnp.einsum('nbhid,nbhjd->nbhij', qc, kc) * decay, 0.0)
    q_dec = qc * jnp.exp(gc)[..., None]
    k_dec = kc * jnp.exp(gc[..., -1:] - gc)[..., None]
    g_last = jnp.exp(gc[..., -1])

    def step(s, xs):
        qd, kd, ui, wi, ai, gl = xs
        v_new = ui - wi @ s
        o = qd @ s + ai @ v_new
        s = s * gl[..., None, None] + jnp.einsum('bhck,bhcv->bhkv', kd, v_new)
        return s, o

    s_fin, o = lax.scan(step, s0, (q_dec, k_dec, u, w, a_intra, g_last))
    o = o.transpose(1, 0, 3, 2, 4).reshape(b, tp, h, dv)[:, :t]
    return o, s_fin

def _gdn_mixer(h, conv_hist, s0, w_in, w_conv, a_log, dt_bias, norm_w, w_out):
    b, t, _ = h.shape
    z = h @ w_in
    qkv = z[..., :GDN_CONV_CH]
    gate = z[..., GDN_CONV_CH:GDN_CONV_CH + GDN_VW]
    b_raw = z[..., GDN_CONV_CH + GDN_VW:GDN_CONV_CH + GDN_VW + GDN_HEADS]
    a_raw = z[..., GDN_CONV_CH + GDN_VW + GDN_HEADS:]
    qkv, new_conv = _short_conv(qkv, conv_hist, w_conv)
    qkv = qkv.astype(F32)
    q = _l2norm(qkv[..., :GDN_QK].reshape(b, t, GDN_HEADS, GDN_DK)) * (GDN_DK ** -0.5)
    k = _l2norm(qkv[..., GDN_QK:2 * GDN_QK].reshape(b, t, GDN_HEADS, GDN_DK))
    v = qkv[..., 2 * GDN_QK:].reshape(b, t, GDN_HEADS, GDN_DV)
    beta = jax.nn.sigmoid(b_raw.astype(F32))
    g = -jnp.exp(a_log.astype(F32)) * jax.nn.softplus(a_raw.astype(F32) + dt_bias.astype(F32))
    o, s_new = _gated_delta_chunked(q, k, v, g, beta, s0.astype(F32))
    o = o * lax.rsqrt(jnp.mean(o * o, axis=-1, keepdims=True) + RMS_EPS) * norm_w.astype(F32)
    o = o.reshape(b, t, GDN_VW) * jax.nn.silu(gate.astype(F32))
    y = o.astype(h.dtype) @ w_out
    return y, new_conv, s_new.astype(s0.dtype)

def setup_inputs(seed: int = 0) -> dict:
    key = jax.random.key(seed)
    ks = jax.random.split(key, 24)

    def nrm(k, shape, scale):
        return jax.random.normal(k, shape, F32) * scale

    n_hist_a = min(A_MAX_WINDOW, PAST_LEN)
    dt = jnp.exp(jax.random.uniform(ks[18], (N_ODD, GDN_HEADS), F32, math.log(1e-3), math.log(1e-1)))
    return {
        'x_prompt': nrm(ks[0], (BATCH, SEQ, D_MODEL), 1.0),
        'x_sample': nrm(ks[1], (DEC_BATCH, DEC_SEQ, D_MODEL), 1.0),
        'state_a_k': nrm(ks[2], (N_EVEN, DEC_BATCH, n_hist_a, A_HEADS, HEAD_DIM), 1.0),
        'state_a_v': nrm(ks[3], (N_EVEN, DEC_BATCH, n_hist_a, A_HEADS, HEAD_DIM), 1.0),
        'state_pool': nrm(ks[4], (N_EVEN, DEC_BATCH, POOL_HIST, POOL_WIDTH), 1.0),
        'state_conv': nrm(ks[5], (N_ODD, DEC_BATCH, CONV_WIDTH - 1, GDN_CONV_CH), 1.0),
        'state_gdn': nrm(ks[6], (N_ODD, DEC_BATCH, GDN_HEADS, GDN_DK, GDN_DV), 0.05),
        'norm_mix': 1.0 + nrm(ks[7], (DEPTH, D_MODEL), 0.02),
        'norm_ffn': 1.0 + nrm(ks[8], (DEPTH, D_MODEL), 0.02),
        'w_in_a': nrm(ks[9], (N_EVEN, D_MODEL, EVEN_IN), D_MODEL ** -0.5),
        'w_out_a': nrm(ks[10], (N_EVEN, EVEN_MIX, D_MODEL), EVEN_MIX ** -0.5),
        'w_pool': nrm(ks[11], (N_EVEN, POOL_GROUPS, POOL_GROUP_DIM, POOL_GROUP_DIM), POOL_GROUP_DIM ** -0.5),
        'pool_scale': 1.0 + nrm(ks[12], (N_EVEN, POOL_WIDTH), 0.02),
        'w_in_c': nrm(ks[13], (N_ODD, D_MODEL, ODD_IN), D_MODEL ** -0.5),
        'w_conv_c': nrm(ks[14], (N_ODD, CONV_WIDTH, GDN_CONV_CH), CONV_WIDTH ** -0.5),
        'a_log_c': jnp.log(jax.random.uniform(ks[15], (N_ODD, GDN_HEADS), F32, 1.0, 16.0)),
        'dt_bias_c': dt + jnp.log(-jnp.expm1(-dt)),
        'norm_out_c': 1.0 + nrm(ks[16], (N_ODD, GDN_DV), 0.02),
        'w_out_c': nrm(ks[17], (N_ODD, GDN_VW, D_MODEL), GDN_VW ** -0.5),
        'w_ffn_gate': nrm(ks[19], (DEPTH, D_MODEL, FFN_HIDDEN), D_MODEL ** -0.5),
        'w_ffn_up': nrm(ks[20], (DEPTH, D_MODEL, FFN_HIDDEN), D_MODEL ** -0.5),
        'w_ffn_down': nrm(ks[21], (DEPTH, FFN_HIDDEN, D_MODEL), FFN_HIDDEN ** -0.5),
        'norm_final': 1.0 + nrm(ks[22], (D_MODEL,), 0.02),
    }

def reference(x_prompt, x_sample, state_a_k, state_a_v, state_pool, state_conv, state_gdn,
              norm_mix, norm_ffn, w_in_a, w_out_a, w_pool, pool_scale,
              w_in_c, w_conv_c, a_log_c, dt_bias_c, norm_out_c, w_out_c,
              w_ffn_gate, w_ffn_up, w_ffn_down, norm_final):
    slopes = _alibi_slopes(A_HEADS)
    xp, xs = x_prompt, x_sample
    bp, bs = xp.shape[0], xs.shape[0]
    ak_p, av_p, pl_p, cv_p, gd_p = [], [], [], [], []
    ak_s, av_s, pl_s, cv_s, gd_s = [], [], [], [], []
    for layer in range(DEPTH):
        i = layer // 2
        hp = _rmsnorm(xp, norm_mix[layer])
        hs = _rmsnorm(xs, norm_mix[layer])
        if layer % 2 == 0:
            yp, kp, vp, pp = _even_mixer(hp, None, None, jnp.zeros((bp, POOL_HIST, POOL_WIDTH), hp.dtype), 0,
                                         w_in_a[i], w_out_a[i], w_pool[i], pool_scale[i], slopes)
            ys, ks_, vs, ps = _even_mixer(hs, state_a_k[i], state_a_v[i], state_pool[i], PAST_LEN,
                                          w_in_a[i], w_out_a[i], w_pool[i], pool_scale[i], slopes)
            ak_p.append(kp); av_p.append(vp); pl_p.append(pp)
            ak_s.append(ks_); av_s.append(vs); pl_s.append(ps)
        else:
            yp, cp, sp = _gdn_mixer(hp, jnp.zeros((bp, CONV_WIDTH - 1, GDN_CONV_CH), hp.dtype),
                                    jnp.zeros((bp, GDN_HEADS, GDN_DK, GDN_DV), state_gdn.dtype),
                                    w_in_c[i], w_conv_c[i], a_log_c[i], dt_bias_c[i], norm_out_c[i], w_out_c[i])
            ys, cs_, ss = _gdn_mixer(hs, state_conv[i], state_gdn[i],
                                     w_in_c[i], w_conv_c[i], a_log_c[i], dt_bias_c[i], norm_out_c[i], w_out_c[i])
            cv_p.append(cp); gd_p.append(sp)
            cv_s.append(cs_); gd_s.append(ss)
        xp = xp + yp
        xs = xs + ys
        xp = xp + _swiglu(_rmsnorm(xp, norm_ffn[layer]), w_ffn_gate[layer], w_ffn_up[layer], w_ffn_down[layer])
        xs = xs + _swiglu(_rmsnorm(xs, norm_ffn[layer]), w_ffn_gate[layer], w_ffn_up[layer], w_ffn_down[layer])
    y_prompt = _rmsnorm(xp, norm_final)
    y_sample = _rmsnorm(xs, norm_final)
    a_k_prompt, a_v_prompt = jnp.stack(ak_p), jnp.stack(av_p)
    pool_prompt, conv_prompt, gdn_prompt = jnp.stack(pl_p), jnp.stack(cv_p), jnp.stack(gd_p)
    a_k_sample, a_v_sample = jnp.stack(ak_s), jnp.stack(av_s)
    pool_sample, conv_sample, gdn_sample = jnp.stack(pl_s), jnp.stack(cv_s), jnp.stack(gd_s)
    return (y_prompt, y_sample, a_k_prompt, a_v_prompt, pool_prompt, conv_prompt, gdn_prompt,
            a_k_sample, a_v_sample, pool_sample, conv_sample, gdn_sample)


_drawn_inputs = setup_inputs


def setup_inputs(seed=0):
    import zlib

    import numpy as np

    out = dict(_drawn_inputs(seed))
    spreads = {}
    factors = {'norm_ffn': 2.834, 'pool_scale': 3.327, 'norm_out_c': 26.659, 'norm_final': 7.954}
    for name, (base, spread) in spreads.items():
        noise = np.random.default_rng([zlib.crc32(name.encode()), seed]).standard_normal(out[name].shape)
        drawn = base * np.exp(spread * noise) if base else spread * noise
        out[name] = __import__('jax').numpy.asarray(drawn.astype(out[name].dtype))
    for name, factor in factors.items():
        out[name] = (out[name] * factor).astype(out[name].dtype)
    return out
```

```python
import math
from contextlib import ExitStack

import concourse.bass as bass
import numpy as np
from concourse import mybir

F32 = mybir.dt.float32
F32R = mybir.dt.float32r
ALU = mybir.AluOpType
ACT = mybir.ActivationFunctionType
AX = mybir.AxisListType

P = 128
D_MODEL = 1024
SEQ = 512
NS = 8
T = SEQ + NS
TH = T // 2
KD = D_MODEL // P
HEADS = 8
HD = 64
A_W = HEADS * HD
PAST = 512
POOL_HIST = 15
POOL_WINDOWS = (2, 4, 8, 16)
QB = SEQ // P
FFN = 2816
FT = FFN // P
PARTS = (8, 8, 6)
GH = 8
CONV = 4
QK = GH * P
SLOT = 2048
LEVELS = (1, 2, 4, 8, 16, 32, 64)
EPS = 1e-6
NEG = -1e30
KEYS_A = 128
KEYS_B = 96
KEYS = KEYS_A + KEYS_B + 1

N_IN_A = 0
N_OUT_A = N_IN_A + 16
N_FFN0 = N_OUT_A + KD
N_FFN = 2 * FT + KD * len(PARTS)
N_IN_C = N_FFN0 + N_FFN
N_OUT_C = N_IN_C + 4 * GH
N_FFN1 = N_OUT_C + KD
N_ALL = N_FFN1 + N_FFN
BLOCK = KD * P
IN_A_TILES = [t + 4 * r for t in range(4) for r in range(3)] + [12, 13, 14, 15]

C_ID = 0
C_ONE = C_ID + P
C_COL = C_ONE + P
C_END = C_COL + 3
G_LEVEL = 0
G_TRI = G_LEVEL + len(LEVELS) * P
G_HALF = G_TRI + P
G_KEEP = G_HALF + 2 * P
G_SEL = G_KEEP + T
G_END = G_SEL + GH


def multiplicity(d):
    return int(0 <= d <= 128) + int(d >= 0 and d % 4 == 0 and d // 4 <= 128) + int(d >= 0 and d % 16 == 0 and d // 16 <= 128)


def slope(h):
    return 2.0 ** (-8.0 * (h + 1) / HEADS)


def log_count(d):
    c = multiplicity(d)
    return math.log(c) if c else NEG


def constant_table():
    t = np.ones((P, C_END), np.float32)
    t[:, C_ID:C_ID + P] = np.eye(P)
    t[:, C_COL] = EPS
    t[:, C_COL + 1] = -0.5 * math.log(P)
    return t


def delta_table():
    t = np.zeros((P, G_END), np.float32)
    j = np.arange(P)[:, None]
    i = np.arange(P)[None, :]
    for n, s in enumerate(LEVELS):
        t[:, G_LEVEL + n * P:G_LEVEL + (n + 1) * P] = (j // (2 * s) == i // (2 * s)) & (j % (2 * s) < s) & (i % (2 * s) >= s)
    t[:, G_TRI:G_TRI + P] = np.where(i >= j, 0.0, NEG)
    t[0:32, G_HALF:G_HALF + P] = 1.0
    t[32:64, G_HALF + P:G_HALF + 2 * P] = 1.0
    t[:, G_KEEP:G_KEEP + SEQ] = (np.arange(SEQ) % P != 0)[None, :]
    for h in range(GH):
        t[h, G_SEL + h] = t[32 + h, G_SEL + h] = 1.0
    return t


def attention_table():
    d = np.arange(P)[:, None] + 3 * P - np.arange(SEQ)[None, :]
    count = np.vectorize(log_count)(np.arange(-P, SEQ + P + 1))
    lc = count[d + P]
    return np.concatenate([d, np.where(lc < NEG / 2, NEG, 8.0 * lc)], 1).astype(np.float32)


def decode_table():
    dist = [PAST - t for t in range(PAST - KEYS_A, PAST)] + [PAST - 4 * r for r in range(KEYS_B)] + [0]
    rows = [[8.0 * (log_count(d) - slope(h) * d) for d in dist] for _ in range(NS) for h in range(HEADS)]
    return np.asarray(rows, np.float32)


def pool_table():
    rows = [[1.0 / min(t + 1, w) for t in range(SEQ)] + [1.0 / w] * NS for w in POOL_WINDOWS]
    return np.broadcast_to(np.asarray(rows, np.float32).reshape(1, -1), (P, len(rows) * T)).copy()


def select_table():
    return np.repeat(np.eye(NS, dtype=np.float32), P, 1)


NORM_ROWS = (0, 2, 1, 3, 4)


class Steps:

    def __init__(self, sem, names):
        self.sem, self.names, self.n = sem, {x: n for n, x in enumerate(names)}, 0
        assert len(self.names) == len(names)

    def at(self, name, turn=0):
        return turn * len(self.names) + self.names[name] + 1

    def all(self, turn=1):
        return turn * len(self.names)

    def done(self, name, instruction):
        assert self.names[name] == self.n % len(self.names), (name, self.n)
        self.n += 1
        instruction.then_inc(self.sem, 1)


def build(nc, a, o):
    ctx = ExitStack()
    with ctx:
        def sem(name):
            return ctx.enter_context(nc.semaphore(name))

        def sb(name, cols, dt=F32, stack=ctx):
            shape = [P, *cols] if isinstance(cols, (list, tuple)) else [P, cols]
            return stack.enter_context(nc.sbuf_tensor(name, shape, dt))

        xT = sb("xT", [KD, T])
        const = sb("const", C_END)
        par = sb("par", 48)
        wconv = sb("wconv", [CONV, 3 * GH])
        rstd = sb("rstd", T)
        ssum = sb("ssum", T)
        sq = sb("sq", [2, T])
        w_raw = sb("w_raw", [2, BLOCK])
        w_hi = sb("w_hi", [2, BLOCK], F32R)
        w_lo = sb("w_lo", [2, BLOCK], F32R)
        g_hi = sb("g_hi", [KD, T], F32R)
        g_lo = sb("g_lo", [KD, T], F32R)

        with ExitStack() as s:
            ck = sb("ck", [4, 2, A_W], F32, s)
            cv = sb("cv", [4, 2, A_W], F32, s)
        h_hi = sb("h_hi", [KD, T], F32R)
        h_lo = sb("h_lo", [KD, T], F32R)

        with ExitStack() as s:
            x_tok = sb("x_tok", [QB, D_MODEL], F32, s)
            xs_tok = sb("xs_tok", D_MODEL, F32, s)
            par_rows = sb("par_rows", [2, P], F32, s)
        with ExitStack() as s:
            zT = sb("zT", [16, T], F32, s)
            v_tok = sb("v_tok", [QB, A_W], F32, s)
            k_stage = sb("k_stage", [2, QB, P], F32, s)
            z_tok = sb("z_tok", [3, A_W], F32, s)
            u_tok = sb("u_tok", A_W, F32, s)
            hist_rows = sb("hist_rows", A_W, F32, s)
            sel8 = sb("sel8", [NS, P], F32, s)
            prod = sb("prod", [2, A_W], F32, s)
            dec_s = sb("dec_s", [2, NS * HEADS], F32, s)
            dec_tab = sb("dec_tab", KEYS, F32, s)
            dec_p = sb("dec_p", KEYS, F32, s)
            dec_pT = sb("dec_pT", [2, NS * HEADS], F32, s)
            dec_col = sb("dec_col", 4, F32, s)
            with ExitStack() as s1:
                att_tab = sb("att_tab", [2, SEQ], F32, s1)
                bias = sb("bias", SEQ, F32, s1)
                prob = sb("prob", [2, 10 * P], F32, s1)
                probT = sb("probT", [2, SEQ], F32, s1)
                o_tok = sb("o_tok", [QB, P], F32, s1)
                att_col = sb("att_col", [2, 4, QB], F32, s1)
            with ExitStack() as s1:
                histT = sb("histT", [4, NS, POOL_HIST], F32, s1)
                cnt = sb("cnt", [4, T], F32, s1)
                wpool = sb("wpool", [4, P], F32, s1)
                run = sb("run", [2, T], F32, s1)
                tail = sb("tail", NS, F32, s1)
                pooled = sb("pooled", [2, T], F32, s1)
        with ExitStack() as s:
            gate_n = sb("gate_n", T, F32, s)
            gate_s = sb("gate_s", T, F32, s)
            up_n = sb("up_n", T, F32, s)
            gu = sb("gu", T, F32, s)
        with ExitStack() as s:
            zc = sb("zc", [2, CONV - 1 + T], F32, s)
            y = sb("y", [4, T], F32, s)
            delta = sb("delta", G_END, F32, s)
            wab_hi = sb("wab_hi", [KD, 64], F32R, s)
            wab_lo = sb("wab_lo", [KD, 64], F32R, s)
            chist = sb("chist", [3 * GH, NS, CONV - 1], F32, s)
            cprod = sb("cprod", [3 * GH, NS], F32, s)
            rows = sb("rows", T, F32, s)
            acol = sb("acol", 4, F32, s)
            tokcols = sb("tokcols", [QB, 64], F32, s)
            with ExitStack() as s1:
                crow = sb("crow", 3 * GH * P, F32, s1)
                ctmp = sb("ctmp", [3 * GH, NS], F32, s1)
                wab_raw = sb("wab_raw", [KD, 2 * GH], F32, s1)
                wab_pad = sb("wab_pad", [KD, 64], F32, s1)
                ab = sb("ab", T, F32, s1)
                abt = sb("abt", [3, T], F32, s1)
            with ExitStack() as s1:
                rowsel = sb("rowsel", T, F32, s1)
                sqg = sb("sqg", [2, T], F32, s1)
                rqk = sb("rqk", [2, T], F32, s1)
                gcb = sb("gcb", T, F32, s1)
                egb = sb("egb", T, F32, s1)
                betab = sb("betab", T, F32, s1)
                qg = sb("qg", T, F32, s1)
                kbg = sb("kbg", T, F32, s1)
                decay = sb("decay", [QB, P], F32, s1)
                attT = sb("attT", [QB, P], F32, s1)
                lowT = sb("lowT", [QB, P], F32, s1)
                lev = sb("lev", [2, QB, P], F32, s1)
                ip = sb("ip", [QB, P], F32, s1)
                tinv = sb("tinv", [QB, P], F32, s1)
                tinvT = sb("tinvT", [QB, P], F32, s1)
                vb = sb("vb", [QB, P], F32, s1)
                kdec = sb("kdec", [QB, P], F32, s1)
                edk = sb("edk", QB, F32, s1)
                state = sb("state", P, F32, s1)
                resid = sb("resid", P, F32, s1)
                vnew = sb("vnew", P, F32, s1)
                z_rows = sb("z_rows", [3, P], F32, s1)
                s_in = sb("s_in", [NS, P], F32, s1)
                kq = sb("kq", [NS, 2], F32, s1)
                sm = sb("sm", [4, NS], F32, s1)
                kv_rows = sb("kv_rows", [2, P], F32, s1)
        with ExitStack() as s:
            y_fin = sb("y_fin", [KD, T], F32, s)
            y_tok = sb("y_tok", [QB + 1, D_MODEL], F32, s)

        acc = ctx.enter_context(nc.psum_tensor("acc", [P, 4, 512], F32))
        aux = ctx.enter_context(nc.psum_tensor("aux", [P, 4, 512], F32))

        def halves(x):
            return x.rearrange("p (b t) -> p b t", b=2)

        def apart(engine):
            engine.nop()

        def blocks(x):
            return x.rearrange("p (c m) -> p c m", m=P)

        def accv(slot):
            return acc[:, 2 * slot:2 * slot + 2, 0:TH]

        def auxv(pair):
            return aux[:, 2 * pair:2 * pair + 2, 0:TH]

        def column(tensor, n):
            return tensor[:, n:n + 1] if isinstance(n, int) else tensor[:, bass.ds(n, 1)]

        ident = const[:, C_ID:C_ID + P]
        ones = const[:, C_ONE:C_ONE + P]
        eps_col = const[:, C_COL:C_COL + 1]
        lnq_col = const[:, C_COL + 1:C_COL + 2]
        one_col = const[:, C_COL + 2:C_COL + 3]

        const_in, par_in, xs_in, tab_in, sel_in, hist_in, pool_in = (
            sem(n) for n in ("const_in", "par_in", "xs_in", "tab_in", "sel_in", "hist_in", "pool_in"))
        x_in = [sem(f"x_in{b}") for b in range(QB)]
        w_loaded = [sem("w_loaded0"), sem("w_loaded1")]
        w_hi_made, w_lo_made = sem("w_hi_made"), sem("w_lo_made")
        acc_full = sem("acc_full")
        acc_read = sem("acc_read")
        h_hi_made, h_lo_made, sq_made, ss_added = (sem(n) for n in ("h_hi_made", "h_lo_made", "sq_made", "ss_added"))
        ss_clear, ss_full, ln_made, rstd_made = (sem(n) for n in ("ss_clear", "ss_full", "ln_made", "rstd_made"))
        silu_made, gu_made, g_hi_made, g_lo_made = (sem(n) for n in ("silu_made", "gu_made", "g_hi_made", "g_lo_made"))
        ck_in, cv_in, ck2_in, cv2_in, self_in, self2_in = (
            sem(n) for n in ("ck_in", "cv_in", "ck2_in", "cv2_in", "self_in", "self2_in"))
        k_stored = [sem("k_stored0"), sem("k_stored1")]
        delta_in, crow_in, wab_in, acol_in, s_read, s_stored, st_stored, zr_stored = (
            sem(n) for n in ("delta_in", "crow_in", "wab_in", "acol_in", "s_read", "s_stored", "st_stored", "zr_stored"))
        stored = sem("stored")
        copied = sem("copied")
        y_stored = sem("y_stored")

        up = {e: Steps(sem(f"up_{e}"), n) for e, n in {
            "pe": ["par", "xs"] + [f"x{m}" for m in range(KD)],
            "dve": ["par", "wconv", "xs"] + [f"x{m}" for m in range(KD)],
        }.items()}
        heads_a = [f"{h}{b}" for h in range(HEADS) for b in range(QB)]
        order = [("sc", h, b) for h in range(HEADS) for b in range(QB)]
        pe_att = []
        for t in range(4):
            pe_att += [f"v_turned{t}", f"k_turned{t}"]
        pe_att += ["u_turned", "z_turned"]
        for h in range(HEADS + 1):
            for b in range(QB):
                if h < HEADS:
                    pe_att.append(f"scores{h}{b}")
                if h:
                    pe_att += [f"pv{h - 1}{b - 1}"] if b else []
                    pe_att.append(f"p_turned{h - 1}{b}")
            if h:
                pe_att.append(f"pv{h - 1}{QB - 1}")
                if h % 2 == 0:
                    pe_att.append(f"o_turned{h // 2 - 1}")
        pe_att += ["hist_turned"] + [f"pooled{g}" for g in range(4)]
        pe_att += [f"q_spread{b}" for b in range(NS)] + ["s_turned", "dp_turned", "dec_out"]
        dve_att = [f"v_kept{t}" for t in range(4)] + ["u_kept", "z_kept"]
        for h in range(HEADS + 1):
            if h < HEADS:
                dve_att.append(f"bias{h}")
            for b in range(QB):
                if h < HEADS:
                    dve_att += [f"max{h}{b}", f"neg{h}{b}"]
                if h and b % 2:
                    dve_att.append(f"pT{h - 1}{b}")
            if h:
                dve_att += [f"inv{h - 1}", f"o{h - 1}"]
                if h % 2 == 0:
                    dve_att.append(f"g_lo{h // 2 - 1}")
        dve_att += ["histT"] + [x for g in range(4) for x in (f"tail{g}", f"tail_sum{g}", f"tail_p{g}")]
        dve_att += [f"pool_lo{g}" for g in range(4)]
        dve_att += [f"{x}{b}" for b in range(NS) for x in ("prod_a", "prod_b", "sum_a", "sum_b")]
        dve_att += ["dec_max", "dec_neg", "dec_inv", "dec_norm", "dec_pT", "dec_lo0", "dec_lo1"]
        act_att = [f"k_kept{t}" for t in range(4)]
        for h in range(HEADS + 1):
            for b in range(QB):
                if h < HEADS:
                    act_att.append(f"exp{h}{b}")
                if h and b % 2 == 0:
                    act_att.append(f"pT{h - 1}{b}")
            if h and h % 2 == 0:
                act_att.append(f"g_hi{h // 2 - 1}")
        act_att += [f"pool_hi{g}" for g in range(4)] + ["dec_exp", "dec_hi0", "dec_hi1"]
        pool_att = []
        for g in range(4):
            pool_att += [f"run{g}{n}{x}" for n in range(g + 1) for x in "ab"] + [f"mean{g}", f"pool{g}"]
        at = {e: Steps(sem(f"mix_{e}"), n) for e, n in
              {"pe": pe_att, "dve": dve_att, "act": act_att, "pool": pool_att}.items()}

        pre = {e: Steps(sem(f"pre_{e}"), n) for e, n in {
            "pe": ["chist0", "chist1", "ab", "rows_turned"],
            "act": ["wab_hi", "exp_b", "exp_sp", "ln_sp", "exp_a"],
            "dve": ["wab_lo", "chist0", "chist1", "prod0", "prod1", "sum1", "prod2", "sum2", "ab",
                    "beta1", "beta", "dt", "abs", "sp", "nega", "g", "cum", "tokcols"],
            "pool": ["zc", "wab_zero", "wab_pad_b", "wab_pad_a", "rows_zero"],
        }.items()}
        pe_h = ["tail_q", "tail_k", "tail_v", "gc", "beta", "ss_q", "ss_k", "turn_v", "turn_k", "kk", "qk", "t_turned"]
        act_h = ["tap_q", "silu_q", "tap_k", "silu_k", "tap_v", "silu_v", "silu_g", "gcb", "egb",
                 "sq_q", "sq_k", "ln_q", "rs_q", "ln_k", "rs_k", "decay", "edk", "tinv"]
        dve_h = [f"tap_{r}{i}" for r in "qkv" for i in "0123"]
        dve_h += ["z_rows", "betab", "qn", "kn", "qg", "kb", "kbg", "diff", "edk", "vb", "kdec", "attT", "lowT", "low", "one"]
        pool_h = ["rowsel", "mask"] + [f"lev{n}" for n in range(len(LEVELS))]
        for n in range(1, len(LEVELS)):
            last = n == len(LEVELS) - 1
            pe_h += [f"p{n}"] + ([] if last else [f"t{n}"]) + [f"u{n}"]
            act_h += [] if last else [f"t{n}"]
            dve_h += [f"ip{n}", f"u{n}"]
        for c in range(QB):
            pe_h += ([f"ks{c}"] if c else []) + [f"v{c}", f"o{c}", f"s{c}"]
            act_h += [f"v{c}"]
            dve_h += ([f"r{c}"] if c else []) + [f"s{c}"]
        pe_h += ["dx", "dqk", "dk_turned", "dv_turned", "outer", "osum"]
        act_h += ["kq_k", "kq_q", "oT", "o_sq", "o_ln", "o_rs", "g_hi"]
        dve_h += ["dkq", "dvb", "dv", "dqk", "do", "d_rows", "dvexp", "s_new", "on", "og", "g_lo"]
        pool_h += ["s_decayed"]
        gh = {e: Steps(sem(f"head_{e}"), n) for e, n in {"pe": pe_h, "act": act_h, "dve": dve_h, "pool": pool_h}.items()}
        fin = {e: Steps(sem(f"fin_{e}"), n) for e, n in {
            "pe": [f"y{b}" for b in range(QB + 1)], "dve": [f"y{m}" for m in range(KD)] + [f"y_tok{b}" for b in range(QB + 1)]}.items()}

        w_in_a, w_out_a = a["w_in_a"][0], a["w_out_a"][0]
        w_in_c, w_out_c = a["w_in_c"][0], a["w_out_c"][0]

        def column_blocks(w, k0=0, kt=KD, cols=None):
            w = w[k0 * P:(k0 + kt) * P, 0:cols or w.shape[1]]
            return w.rearrange("(k p) (c m) -> c p k m", p=P, m=P)

        block = ctx.enter_context(nc.Block())

        @block.sync
        def _(sp):
            def load(n, slot, src, kt=KD):
                if not isinstance(n, int) or n >= 2:
                    sp.wait_ge(w_lo_made, n - 1)
                sp.dma_start(w_raw[:, slot, 0:kt * P].rearrange("p (k m) -> p k m", m=P), src).then_inc(w_loaded[slot], 16)

            for b in range(QB):
                sp.dma_start(x_tok[:, b], a["x_prompt"][0, b * P:(b + 1) * P, :]).then_inc(x_in[b], 16)
            in_a = column_blocks(w_in_a)
            for n in range(16):
                load(N_IN_A + n, n % 2, in_a[IN_A_TILES[n]])
            out_a = column_blocks(w_out_a)
            load(N_OUT_A, 0, out_a[0])
            load(N_OUT_A + 1, 1, out_a[1])
            sp.wait_ge(acc_full, N_OUT_A)

            sp.dma_start(o["pool_sample"][0, :, 0:POOL_HIST - 1, :], a["state_pool"][0, :, 1:POOL_HIST, :]).then_inc(copied, 16)
            sp.dma_start(o["conv_sample"][0, :, 0:CONV - 2, :], a["state_conv"][0, :, 1:CONV - 1, :]).then_inc(copied, 16)

            def cached(dst, src, b0, signal):
                cache = src[0, b0:b0 + 4].rearrange("b t h d -> t b (h d)")
                sp.dma_start(dst[:, :, 0, :], cache[PAST - KEYS_A:PAST]).then_inc(signal, 16)
                sp.dma_start(dst[0:KEYS_B, :, 1, :], cache[0:PAST - KEYS_A:4]).then_inc(signal, 16)

            def own_row(dst, r, b0, signal):
                for b in range(4):
                    sp.dma_start(dst[KEYS_B:KEYS_B + 1, b, 1, :], z_tok[b0 + b:b0 + b + 1, r, :]).then_inc(signal, 16)

            sp.wait_ge(at["dve"].sem, at["dve"].at("z_kept"))
            cached(ck, a["state_a_k"], 0, ck_in)
            own_row(ck, 1, 0, self_in)
            cached(cv, a["state_a_v"], 0, cv_in)
            own_row(cv, 2, 0, cv_in)
            sp.wait_ge(at["dve"].sem, at["dve"].at("sum_b3"))
            cached(ck, a["state_a_k"], 4, ck2_in)
            own_row(ck, 1, 4, self2_in)
            sp.wait_ge(at["dve"].sem, at["dve"].at(f"sum_b{NS - 1}"))
            cached(ck, a["state_a_v"], 4, cv2_in)
            own_row(ck, 2, 4, cv2_in)
            for n in range(2, KD, 1):
                load(N_OUT_A + n, n % 2, out_a[n])

            def ffn(layer, base):
                gate, upw = column_blocks(a["w_ffn_gate"][layer]), column_blocks(a["w_ffn_up"][layer])
                k0 = 0
                for part, kt in enumerate(PARTS):
                    with sp.Fori(0, kt) as i:
                        load(base + 2 * i, 0, gate[i + k0])
                        load(base + 2 * i + 1, 1, upw[i + k0])
                        if layer == 0 and part < 2:
                            old, new = (("state_a_k", "a_k_sample"), ("state_a_v", "a_v_sample"))[part]
                            sp.dma_start(o[new][0].rearrange("b t h d -> b t (h d)")[:, 0:PAST][i],
                                         a[old][0].rearrange("b t h d -> b t (h d)")[i]).then_inc(copied, 16)
                    base += 2 * kt
                    down = column_blocks(a["w_ffn_down"][layer], k0, kt)
                    with sp.Fori(0, KD // 2) as i:
                        for s in range(2):
                            load(base + 2 * i + s, s, down[2 * i + s], kt)
                    base += KD
                    k0 += kt

            ffn(0, N_FFN0)
            in_c = column_blocks(w_in_c, cols=4 * QK)
            out_c = column_blocks(w_out_c)
            dh = gh["dve"]

            def head(h, ahead):
                for r in range(2, 4):
                    load(N_IN_C + 4 * h + r, r % 2, in_c[GH * r + h])
                for s in range(2):
                    load(N_IN_C + 4 * h + 4 + s, s, ahead[s])
                if not isinstance(h, int) or h:
                    sp.wait_ge(s_stored, 16 * h)
                sp.dma_start(s_in[:], a["state_gdn"][0].rearrange("b h k v -> h k b v")[h]).then_inc(s_read, 16)
                sp.wait_ge(dh.sem, dh.at("z_rows", h))
                sp.dma_start(o["conv_prompt"][0, 0].rearrange("i (r h m) -> h i r m", r=3, m=P)[h], z_rows[0:3]).then_inc(zr_stored, 16)
                sp.dma_start(o["conv_sample"][0, :, CONV - 2].rearrange("b (r h m) -> h b r m", r=3, m=P)[h], z_rows[3:11]).then_inc(zr_stored, 16)
                sp.wait_ge(dh.sem, dh.at(f"s{QB - 1}", h))
                sp.dma_start(o["gdn_prompt"][0, 0].rearrange("h k v -> h k v")[h], state[:]).then_inc(st_stored, 16)
                sp.wait_ge(dh.sem, dh.at("s_new", h))
                sp.dma_start(o["gdn_sample"][0].rearrange("b h k v -> h k b v")[h], s_in[:]).then_inc(s_stored, 16)

            for r in range(2):
                load(N_IN_C + r, r, in_c[GH * r])
            with sp.Fori(0, GH - 1) as h:
                head(h, [in_c[GH * r + h + 1] for r in range(2)])
            head(GH - 1, [out_c[0], out_c[1]])
            with sp.Fori(1, KD // 2) as i:
                for s in range(2):
                    load(N_OUT_C + 2 * i + s, s, out_c[2 * i + s])
            ffn(1, N_FFN1)
            for b in range(QB + 1):
                sp.wait_ge(fin["dve"].sem, fin["dve"].at(f"y_tok{b}"))
                if b < QB:
                    sp.dma_start(o["y_prompt"][0, b * P:(b + 1) * P, :], y_tok[:, b]).then_inc(y_stored, 16)
                else:
                    sp.dma_start(o["y_sample"].rearrange("b t d -> (b t) d"), y_tok[0:NS, b]).then_inc(y_stored, 16)
            sp.wait_ge(y_stored, 16 * (QB + 1))
            sp.wait_ge(stored, 16 * 5)
            for q in range(2):
                sp.wait_ge(k_stored[q], 32)
            sp.wait_ge(copied, 16 * (2 * NS + 2))
            sp.wait_ge(s_stored, 16 * GH)
            sp.wait_ge(st_stored, 16 * GH)
            sp.wait_ge(zr_stored, 32 * GH)

        @block.tensor
        def _(pe):
            def product(n, slot, kt, xh, xl, hi_at=None, lo_at=None):
                if not isinstance(n, int) or n >= 2:
                    pe.wait_ge(acc_read, n - 1)
                pe.wait_ge(w_hi_made, n + 1)
                for part, (w, x, ready) in enumerate(((w_hi, xh, hi_at), (w_hi, xl, lo_at), (w_lo, xh, None))):
                    if part == 2:
                        pe.wait_ge(w_lo_made, n + 1)
                    for k in range(kt):
                        if ready:
                            pe.wait_ge(*ready(k))
                        for b in range(2):
                            last = nc.tensor.matmul(acc[:, 2 * slot + b, 0:TH], w[:, slot, k * P:(k + 1) * P],
                                                    x[:, k, b * TH:(b + 1) * TH], start=part == 0 and k == 0,
                                                    stop=part == 2 and k == kt - 1)
                last.then_inc(acc_full, 1)

            def norm_sum(k):
                pe.wait_ge(ss_added, KD * (k + 1))
                for b in range(2):
                    mm = nc.tensor.matmul(aux[:, b, 0:TH], ones, ssum[:, b * TH:(b + 1) * TH], start=True, stop=True)
                mm.then_inc(ss_full, 1)

            def normed(k):
                return {"hi_at": lambda kt: (h_hi_made, KD * k + kt + 1), "lo_at": lambda kt: (h_lo_made, KD * k + kt + 1)}

            def ffn(k, base, g_base):
                norm_sum(k)
                for kt in PARTS:
                    with pe.Fori(0, kt) as i:
                        product(base + 2 * i, 0, KD, h_hi, h_lo, **normed(k))
                        product(base + 2 * i + 1, 1, KD, h_hi, h_lo)
                    base += 2 * kt
                    with pe.Fori(0, KD // 2) as i:
                        product(base + 2 * i, 0, kt, g_hi, g_lo, lambda j: (g_hi_made, g_base + j + 1), lambda j: (g_lo_made, g_base + j + 1))
                        product(base + 2 * i + 1, 1, kt, g_hi, g_lo)
                    base += KD
                    g_base += kt

            U = up["pe"]
            pe.wait_ge(const_in, 16)
            pe.wait_ge(par_in, 32)
            nc.tensor.transpose(aux[:, 3, 0:45], par_rows[0:45, 0], ident[0:45, 0:45])
            U.done("par", nc.tensor.transpose(aux[:, 3, 64:64 + 96], par_rows[0:96, 1], ident[0:96, 0:96]))
            pe.wait_ge(xs_in, 16)
            for m in range(KD):
                tr = nc.tensor.transpose(aux[:, 2, m * NS:(m + 1) * NS], xs_tok[0:NS, m * P:(m + 1) * P], ident[0:NS, 0:NS])
            U.done("xs", tr)
            for m in range(KD):
                if m >= 2:
                    pe.wait_ge(up["dve"].sem, up["dve"].at(f"x{m - 2}"))
                for b in range(QB):
                    if m == 0:
                        pe.wait_ge(x_in[b], 16)
                    tr = nc.tensor.transpose(aux[:, m % 2, b * P:(b + 1) * P], x_tok[:, b, m * P:(m + 1) * P], ident)
                U.done(f"x{m}", tr)
            pe.wait_ge(up["dve"].sem, up["dve"].at(f"x{KD - 1}"))
            norm_sum(0)
            for n in range(16):
                product(N_IN_A + n, n % 2, KD, h_hi, h_lo, **(normed(0) if n == 0 else {}))

            A, dve_at, act_at = at["pe"], at["dve"], at["act"]
            pe.wait_ge(acc_read, 16)
            pe.wait_ge(rstd_made, 1)
            for t in range(4):
                if t >= 2:
                    pe.wait_ge(dve_at.sem, dve_at.at(f"v_kept{t - 2}"))
                for b in range(QB):
                    tr = nc.tensor.transpose(aux[:, t % 2, b * P:(b + 1) * P], zT[:, 8 + t, b * P:(b + 1) * P], ident)
                A.done(f"v_turned{t}", tr)
                if t >= 2:
                    pe.wait_ge(act_at.sem, act_at.at(f"k_kept{t - 2}"))
                for b in range(QB):
                    tr = nc.tensor.transpose(aux[:, 2 + t % 2, b * P:(b + 1) * P], zT[:, 4 + t, b * P:(b + 1) * P], ident)
                A.done(f"k_turned{t}", tr)
            pe.wait_ge(dve_at.sem, dve_at.at("v_kept3"))
            for t in range(4):
                tr = nc.tensor.transpose(aux[0:POOL_HIST + NS, 0, t * P:(t + 1) * P], zT[:, 12 + t, SEQ - POOL_HIST:T], ident)
            A.done("u_turned", tr)
            pe.wait_ge(act_at.sem, act_at.at("k_kept3"))
            for r in range(3):
                for t in range(4):
                    tr = nc.tensor.transpose(aux[0:NS, 1 + r, t * P:(t + 1) * P], zT[:, 4 * r + t, SEQ:T], ident)
            A.done("z_turned", tr)
            pe.wait_ge(dve_at.sem, dve_at.at("z_kept"))

            def scores(h, b):
                rows_h = slice(HD * (h % 2), HD * (h % 2) + HD)
                if h or b >= 2:
                    hh, bb = (h, b - 2) if b >= 2 else (h - 1, b + 2)
                    pe.wait_ge(dve_at.sem, dve_at.at(f"max{hh}{bb}"))
                A.done(f"scores{h}{b}", nc.tensor.matmul(
                    aux[:, b % 2, 0:(b + 1) * P], zT[rows_h, h // 2, b * P:(b + 1) * P],
                    zT[rows_h, 4 + h // 2, 0:(b + 1) * P], start=True, stop=True))

            def turn_probs(h, b):
                pe.wait_ge(act_at.sem, act_at.at(f"exp{h}{b}"))
                if b:
                    last_at = act_at if b % 2 else dve_at
                    pe.wait_ge(last_at.sem, last_at.at(f"pT{h}{b - 1}"))
                elif h:
                    pe.wait_ge(dve_at.sem, dve_at.at(f"pT{h - 1}3"))
                    if h % 2 == 0:
                        pe.wait_ge(dve_at.sem, dve_at.at(f"g_lo{h // 2 - 1}"))
                off = P * b * (b + 1) // 2
                for k in range(b + 1):
                    tr = nc.tensor.transpose(aux[:, 2, k * P:(k + 1) * P], prob[:, h % 2, off + k * P:off + (k + 1) * P], ident)
                A.done(f"p_turned{h}{b}", tr)

            def weigh(h, b):
                made = dve_at if b % 2 else act_at
                pe.wait_ge(made.sem, made.at(f"pT{h}{b}"))
                if h and b == 0:
                    pe.wait_ge(dve_at.sem, dve_at.at(f"o{h - 1}"))
                for k in range(b + 1):
                    mm = nc.tensor.matmul(aux[:, 3, b * HD:(b + 1) * HD], probT[:, b % 2, k * P:(k + 1) * P],
                                          v_tok[:, k, h * HD:(h + 1) * HD], start=k == 0, stop=k == b)
                A.done(f"pv{h}{b}", mm)

            for h in range(HEADS + 1):
                for b in range(QB):
                    if h < HEADS:
                        scores(h, b)
                    if h:
                        if b:
                            weigh(h - 1, b - 1)
                        turn_probs(h - 1, b)
                if h:
                    weigh(h - 1, QB - 1)
                    if h % 2 == 0:
                        t = h // 2 - 1
                        pe.wait_ge(dve_at.sem, dve_at.at(f"o{h - 1}"))
                        for b in range(QB):
                            tr = nc.tensor.transpose(aux[:, 2, b * P:(b + 1) * P], o_tok[:, b], ident)
                        A.done(f"o_turned{t}", tr)
            pe.wait_ge(hist_in, 16)
            for g in range(4):
                tr = nc.tensor.transpose(aux[:, 3, g * 120:(g + 1) * 120], hist_rows[0:120, g * P:(g + 1) * P], ident[0:120, 0:120])
            A.done("hist_turned", tr)
            for g in range(4):
                pe.wait_ge(at["pool"].sem, at["pool"].at(f"pool{g}"))
                pe.wait_ge(dve_at.sem, dve_at.at(f"tail_p{g}"))
                if g == 0:
                    pe.wait_ge(dve_at.sem, dve_at.at("g_lo3"))
                    pe.wait_ge(pool_in, 32)
                if g >= 2:
                    pe.wait_ge(dve_at.sem, dve_at.at(f"pool_lo{g - 2}"))
                for b in range(2):
                    mm = nc.tensor.matmul(auxv(g % 2)[:, b], wpool[:, g], pooled[:, g % 2, b * TH:(b + 1) * TH], start=True, stop=True)
                A.done(f"pooled{g}", mm)
            pe.wait_ge(sel_in, 32)
            pe.wait_ge(dve_at.sem, dve_at.at("pool_lo3"))
            for b in range(NS):
                if b >= 2:
                    pe.wait_ge(dve_at.sem, dve_at.at(f"prod_b{b - 2}"))
                A.done(f"q_spread{b}", nc.tensor.matmul(aux[:, b % 2, 0:A_W], sel8[0:NS, b], z_tok[0:NS, 0], start=True, stop=True))
            pe.wait_ge(dve_at.sem, dve_at.at(f"sum_b{NS - 1}"))
            nc.tensor.transpose(aux[0:64, 2, 0:KEYS_A], dec_s[:, 0], ident)
            A.done("s_turned", nc.tensor.transpose(aux[0:64, 2, KEYS_A:KEYS], dec_s[0:KEYS_B + 1, 1], ident[0:KEYS_B + 1, 0:KEYS_B + 1]))
            pe.wait_ge(dve_at.sem, dve_at.at("dec_norm"))
            nc.tensor.transpose(aux[:, 3, 0:64], dec_p[0:64, 0:KEYS_A], ident[0:64, 0:64])
            A.done("dp_turned", nc.tensor.transpose(aux[0:KEYS_B + 1, 3, 64:128], dec_p[0:64, KEYS_A:KEYS], ident[0:64, 0:64]))
            pe.wait_ge(dve_at.sem, dve_at.at("dec_pT"))
            pe.wait_ge(cv_in, 96)
            for b in range(NS):
                if b == 4:
                    pe.wait_ge(cv2_in, 96)
                vals = cv if b < 4 else ck
                for t in range(4):
                    c = (t * NS + b) * 2
                    nc.tensor.matmul(aux[:, 0, c:c + 2], vals[:, b % 4, 0, t * P:(t + 1) * P],
                                     dec_pT[:, 0, b * HEADS + 2 * t:b * HEADS + 2 * t + 2], start=True, stop=False)
                    mm = nc.tensor.matmul(aux[:, 0, c:c + 2], vals[0:KEYS_B + 1, b % 4, 1, t * P:(t + 1) * P],
                                          dec_pT[0:KEYS_B + 1, 1, b * HEADS + 2 * t:b * HEADS + 2 * t + 2], start=False, stop=True)
            A.done("dec_out", mm)
            pe.wait_ge(act_at.sem, act_at.all())
            pe.wait_ge(dve_at.sem, dve_at.all())
            for n in range(KD):
                product(N_OUT_A + n, n % 2, KD, g_hi, g_lo)
            ffn(1, N_FFN0, 0)

            R = pre["pe"]
            norm_sum(2)
            pe.wait_ge(rstd_made, 3)
            pe.wait_ge(crow_in, 16)
            for half in range(2):
                for t in range(12):
                    tile = 12 * half + t
                    tr = nc.tensor.transpose(aux[:, half, t * 24:(t + 1) * 24], crow[0:24, tile * P:(tile + 1) * P], ident[0:24, 0:24])
                R.done(f"chist{half}", tr)
            pe.wait_ge(pre["dve"].sem, pre["dve"].at("wab_lo"))
            for w, x, part in ((wab_hi, h_hi, 0), (wab_hi, h_lo, 1), (wab_lo, h_hi, 2)):
                pe.wait_ge(h_hi_made, KD * 3)
                pe.wait_ge(h_lo_made, KD * 3)
                for k in range(KD):
                    for b in range(2):
                        mm = nc.tensor.matmul(aux[0:64, 2 + b, 0:TH], w[:, k], x[:, k, b * TH:(b + 1) * TH],
                                              start=part == 0 and k == 0, stop=part == 2 and k == KD - 1)
            R.done("ab", mm)
            pe.wait_ge(pre["dve"].sem, pre["dve"].at("cum"))
            for c in range(QB):
                tr = nc.tensor.transpose(aux[:, 0, c * 64:(c + 1) * 64], rows[0:64, c * P:(c + 1) * P], ident[0:64, 0:64])
            R.done("rows_turned", tr)
            pe.wait_ge(pre["dve"].sem, pre["dve"].at("tokcols"))

            H, dh, ah, ph = gh["pe"], gh["dve"], gh["act"], gh["pool"]
            with pe.Fori(0, GH) as h:
                def wait(steps, name):
                    pe.wait_ge(steps.sem, steps.at(name, h))

                def tail_rows(r, slot):
                    pe.wait_ge(acc_read, N_IN_C + 4 * h + r + 1)
                    H.done(f"tail_{'qkv'[r]}", nc.tensor.transpose(aux[0:11, 3, r * P:(r + 1) * P], zc[:, slot, SEQ:CONV - 1 + T], ident))

                pe.wait_ge(dh.sem, dh.all(h))
                for r in range(4):
                    product(N_IN_C + 4 * h + r, r % 2, KD, h_hi, h_lo)
                    if r:
                        tail_rows(r - 1, (r - 1) % 2)
                wait(ph, "rowsel")
                for b in range(2):
                    mm = nc.tensor.matmul(auxv(0)[:, b], delta[0:64, G_HALF + P:G_HALF + 2 * P], rowsel[0:64, b * TH:(b + 1) * TH], start=True, stop=True)
                H.done("gc", mm)
                wait(dh, "z_rows")
                for b in range(2):
                    mm = nc.tensor.matmul(auxv(1)[:, b], delta[0:64, G_HALF:G_HALF + P], rowsel[0:64, b * TH:(b + 1) * TH], start=True, stop=True)
                H.done("beta", mm)
                wait(ah, "sq_q")
                for b in range(2):
                    mm = nc.tensor.matmul(auxv(0)[:, b], ones, sqg[:, 0, b * TH:(b + 1) * TH], start=True, stop=True)
                H.done("ss_q", mm)
                wait(ah, "sq_k")
                wait(dh, "betab")
                for b in range(2):
                    mm = nc.tensor.matmul(auxv(1)[:, b], ones, sqg[:, 1, b * TH:(b + 1) * TH], start=True, stop=True)
                H.done("ss_k", mm)
                wait(ah, "rs_k")
                for c in range(QB):
                    tr = nc.tensor.transpose(aux[:, 0, c * P:(c + 1) * P], y[:, 2, c * P:(c + 1) * P], ident)
                H.done("turn_v", tr)
                wait(dh, "kn")
                for c in range(QB):
                    tr = nc.tensor.transpose(aux[:, 1, c * P:(c + 1) * P], y[:, 1, c * P:(c + 1) * P], ident)
                H.done("turn_k", tr)
                for name, r, bank in (("kk", 1, 2), ("qk", 0, 3)):
                    for c in range(QB):
                        mm = nc.tensor.matmul(aux[:, bank, c * P:(c + 1) * P], y[:, 1, c * P:(c + 1) * P], y[:, r, c * P:(c + 1) * P], start=True, stop=True)
                    H.done(name, mm)
                wait(dh, "one")
                for c in range(QB):
                    tr = nc.tensor.transpose(aux[:, 0, c * P:(c + 1) * P], tinvT[:, c], ident)
                H.done("t_turned", tr)
                for n in range(1, len(LEVELS)):
                    last_level = n == len(LEVELS) - 1
                    wait(ah, "tinv" if n == 1 else f"t{n - 1}")
                    wait(ph, f"lev{n}")
                    for c in range(QB):
                        mm = nc.tensor.matmul(aux[:, 1, c * P:(c + 1) * P], lev[:, n % 2, c], tinv[:, c], start=True, stop=True)
                    H.done(f"p{n}", mm)
                    wait(dh, f"ip{n}")
                    if n > 1:
                        wait(dh, f"u{n - 1}")
                    if not last_level:
                        for c in range(QB):
                            mm = nc.tensor.matmul(aux[:, 2, c * P:(c + 1) * P], tinvT[:, c], ip[:, c], start=True, stop=True)
                        H.done(f"t{n}", mm)
                    for c in range(QB):
                        mm = nc.tensor.matmul(aux[:, 3, c * P:(c + 1) * P], ip[:, c], tinvT[:, c], start=True, stop=True)
                    H.done(f"u{n}", mm)
                wait(dh, f"u{len(LEVELS) - 1}")
                for c in range(QB):
                    if c:
                        wait(dh, f"s{c - 1}")
                        H.done(f"ks{c}", nc.tensor.matmul(aux[:, 0, 0:P], kbg[:, c * P:(c + 1) * P], state[:], start=True, stop=True))
                        wait(dh, f"r{c}")
                        src = resid[:]
                    else:
                        src = vb[:, 0]
                    H.done(f"v{c}", nc.tensor.matmul(aux[:, 1, 0:P], tinvT[:, c], src, start=True, stop=True))
                    wait(ah, f"v{c}")
                    if c:
                        nc.tensor.matmul(aux[:, 3, c * P:(c + 1) * P], state[:], qg[:, c * P:(c + 1) * P], start=True, stop=False)
                    H.done(f"o{c}", nc.tensor.matmul(aux[:, 3, c * P:(c + 1) * P], vnew[:], attT[:, c], start=c == 0, stop=True))
                    H.done(f"s{c}", nc.tensor.matmul(aux[:, 2, 0:P], kdec[:, c], vnew[:], start=True, stop=True))
                pe.wait_ge(s_read, 16 * h + 16)
                wait(ah, "kq_q")
                for b in range(NS):
                    mm = nc.tensor.matmul(aux[:, 0, 2 * b:2 * b + 2], s_in[:, b], kq[:, b], start=True, stop=True)
                H.done("dx", mm)
                wait(dh, "dkq")
                H.done("dqk", nc.tensor.matmul(aux[:, 1, 0:NS], ones, sm[:, 0], start=True, stop=True))
                H.done("dk_turned", nc.tensor.transpose(aux[0:NS, 2, 0:P], y[:, 1, SEQ:T], ident))
                wait(dh, "dv")
                H.done("dv_turned", nc.tensor.transpose(aux[0:NS, 2, P:2 * P], sm[:, 2], ident))
                wait(dh, "dvexp")
                for b in range(2):
                    mm = nc.tensor.matmul(aux[:, b], kv_rows[0:NS, 0], lev[0:NS, b], start=True, stop=True)
                H.done("outer", mm)
                wait(ah, "o_sq")
                wait(dh, "s_new")
                for b in range(2):
                    mm = nc.tensor.matmul(auxv(0)[:, b], ones, sqg[:, 0, b * TH:(b + 1) * TH], start=True, stop=True)
                H.done("osum", mm)
            pe.wait_ge(dh.sem, dh.all(GH))
            pe.wait_ge(ah.sem, ah.all(GH))
            with pe.Fori(0, KD // 2) as i:
                for s in range(2):
                    product(N_OUT_C + 2 * i + s, s, KD, g_hi, g_lo)
            ffn(3, N_FFN1, FT)
            norm_sum(4)
            Z, fd = fin["pe"], fin["dve"]
            for b in range(QB + 1):
                rows_b = P if b < QB else NS
                pe.wait_ge(fd.sem, fd.at(f"y{KD - 1}") if b < 2 else fd.at(f"y_tok{b - 2}"))
                for m in range(KD):
                    tr = nc.tensor.transpose(acc[0:rows_b, m // 4 + 2 * (b % 2), (m % 4) * P:(m % 4 + 1) * P], y_fin[:, m, b * P:b * P + rows_b], ident)
                Z.done(f"y{b}", tr)

        @block.scalar
        def _(act):
            def convert(n, slot, turn):
                act.wait_ge(w_loaded[slot], 16 * turn + 16)
                if not isinstance(n, int) or n >= 2:
                    act.wait_ge(acc_full, n - 1)
                nc.scalar.activation(w_hi[:, slot], w_raw[:, slot], ACT.Copy).then_inc(w_hi_made, 1)

            def gamma(k, m):
                return column(par, KD * NORM_ROWS[k] + m)

            def norm_tile(k, m, slot, x_sem, x_at):
                if k or not isinstance(m, int) or m >= 2:
                    act.wait_ge(ss_added, KD * k + m - 1)
                act.wait_ge(x_sem, x_at)
                apart(act)
                if k < 4:
                    nc.scalar.activation(h_hi[:, m], xT[:, m], ACT.Copy, scale=gamma(k, m)).then_inc(h_hi_made, 1)
                nc.scalar.activation(sq[:, slot], xT[:, m], ACT.Square).then_inc(sq_made, 1)

            def norm_factor(k):
                nc.scalar.preload_act_table_set("natural_log_exp_and_others")
                act.wait_ge(ss_full, k + 1)
                nc.scalar.activation(halves(rstd), auxv(0), ACT.Ln, bias=eps_col, scale=1.0 / D_MODEL).then_inc(ln_made, 1)
                act.wait_ge(ln_made, k + 1)
                nc.scalar.activation(rstd[:], rstd[:], ACT.Exp, scale=-0.5).then_inc(rstd_made, 1)

            def ffn(k, base, g_base):
                norm_factor(k)
                nc.scalar.preload_act_table_set("silu_and_others")
                for part, kt in enumerate(PARTS):
                    with act.Fori(0, kt) as i:
                        n = base + 2 * i
                        convert(n + 1, 1, base // 2 + i)
                        act.wait_ge(acc_read, n + 1)
                        nc.scalar.activation(gate_s[:], gate_n[:], ACT.Silu).then_inc(silu_made, 1)
                        convert(n + 2, 0, base // 2 + i + 1)
                        act.wait_ge(gu_made, g_base + i + 1)
                        apart(act)
                        nc.scalar.activation(g_hi[:, i], gu[:], ACT.Copy).then_inc(g_hi_made, 1)
                    base += 2 * kt
                    g_base += kt

                    def down(i, last):
                        for s in range(2):
                            n = base + 2 * i + s
                            if not last:
                                convert(n + 1, 1 - s, base // 2 + i + s)
                            if part == 2:
                                norm_tile(k + 1, 2 * i + s, s, acc_read, n + 1)

                    with act.Fori(0, KD // 2 - 1) as i:
                        down(i, False)
                    i = KD // 2 - 1
                    if base + KD < N_ALL:
                        down(i, False)
                    else:
                        convert(base + KD - 1, 1, base // 2 + i)
                        for s in range(2):
                            norm_tile(k + 1, 2 * i + s, s, acc_read, base + 2 * i + s + 1)
                    base += KD

            act.dma_start(const[:], a["const_table"]).then_inc(const_in, 16)
            act.dma_start(par_rows[0:45, 0], a["par_rows"]).then_inc(par_in, 16)
            act.dma_start(par_rows[0:96, 1], a["w_conv_c"][0].rearrange("i (t p) -> (i t) p", p=P)).then_inc(par_in, 16)
            act.dma_start(xs_tok[0:NS, :], a["x_sample"].rearrange("b t d -> (b t) d")).then_inc(xs_in, 16)
            nc.scalar.preload_act_table_set("natural_log_exp_and_others")
            convert(0, 0, 0)
            act.wait_ge(up["dve"].sem, up["dve"].at("par"))
            for m in range(KD):
                norm_tile(0, m, m % 2, up["dve"].sem, up["dve"].at(f"x{m}"))
            norm_factor(0)
            for n in range(16):
                convert(N_IN_A + n + 1, (n + 1) % 2, (n + 1) // 2)

            A, pe_at, dve_at = at["act"], at["pe"], at["dve"]
            for t in range(4):
                act.wait_ge(pe_at.sem, pe_at.at(f"k_turned{t}"))
                if t >= 2:
                    act.wait_ge(k_stored[t % 2], 16)
                A.done(f"k_kept{t}", nc.scalar.activation(k_stage[:, t % 2].rearrange("p b m -> p (b m)"), aux[:, 2 + t % 2], ACT.Copy))
            for h in range(HEADS + 1):
                for b in range(QB):
                    off = P * b * (b + 1) // 2
                    if h < HEADS:
                        act.wait_ge(dve_at.sem, dve_at.at(f"neg{h}{b}"))
                        pr = prob[:, h % 2, off:off + (b + 1) * P]
                        A.done(f"exp{h}{b}", nc.scalar.activation(pr, pr, ACT.Exp, bias=att_col[:, h % 2, 1, b:b + 1],
                                                                 accum_out=att_col[:, h % 2, 2, b:b + 1]))
                    if h and b % 2 == 0:
                        act.wait_ge(pe_at.sem, pe_at.at(f"p_turned{h - 1}{b}"))
                        if b or h > 1:
                            act.wait_ge(pe_at.sem, pe_at.at(f"pv{h - 1}{b - 2}" if b else f"pv{h - 2}2"))
                        A.done(f"pT{h - 1}{b}", nc.scalar.activation(probT[:, 0, 0:(b + 1) * P], aux[:, 2, 0:(b + 1) * P], ACT.Copy))
                if h and h % 2 == 0:
                    t = h // 2 - 1
                    act.wait_ge(pe_at.sem, pe_at.at(f"o_turned{t}"))
                    A.done(f"g_hi{t}", nc.scalar.activation(g_hi[:, t, 0:SEQ], aux[:, 2], ACT.Copy))
            for g in range(4):
                act.wait_ge(pe_at.sem, pe_at.at(f"pooled{g}"))
                A.done(f"pool_hi{g}", nc.scalar.activation(halves(g_hi[:, 4 + g]), auxv(g % 2), ACT.Copy, scale=par[:, 40 + g:41 + g]))
            act.wait_ge(dve_at.sem, dve_at.at("dec_neg"))
            A.done("dec_exp", nc.scalar.activation(dec_p[0:64], dec_p[0:64], ACT.Exp, bias=dec_col[0:64, 1:2], accum_out=dec_col[0:64, 2:3]))
            act.wait_ge(pe_at.sem, pe_at.at("dec_out"))
            for r in range(2):
                rows_r = slice(HD * r, HD * r + HD)
                out = aux[rows_r, 0, 0:64].rearrange("p (t b r) -> p t b r", t=4, r=2)[:, :, :, r]
                A.done(f"dec_hi{r}", nc.scalar.activation(g_hi[rows_r, 0:4, SEQ:T], out, ACT.Copy))
            for n in range(KD):
                convert(N_OUT_A + n + 1, (n + 1) % 2, (N_OUT_A + n + 1) // 2)
                norm_tile(1, n, n % 2, acc_read, N_OUT_A + n + 1)
            ffn(1, N_FFN0, 0)

            R = pre["act"]
            norm_factor(2)
            pre_dve = pre["dve"]
            act.wait_ge(pre["pool"].sem, pre["pool"].at("wab_pad_a"))
            R.done("wab_hi", nc.scalar.activation(wab_hi[:], wab_pad[:], ACT.Copy))
            act.wait_ge(pre_dve.sem, pre_dve.at("ab"))
            R.done("exp_b", nc.scalar.activation(abt[0:8, 0], ab[0:8], ACT.Exp, scale=-1.0))
            act.wait_ge(pre_dve.sem, pre_dve.at("abs"))
            R.done("exp_sp", nc.scalar.activation(abt[32:40, 1], abt[32:40, 1], ACT.Exp))
            act.wait_ge(R.sem, R.at("exp_sp"))
            R.done("ln_sp", nc.scalar.activation(abt[32:40, 1], abt[32:40, 1], ACT.Ln, bias=one_col[32:40]))
            R.done("exp_a", nc.scalar.activation(acol[32:40, 2:3], acol[32:40, 0:1], ACT.Exp))

            H, dh, hp = gh["act"], gh["dve"], gh["pe"]
            with act.Fori(0, GH) as h:
                def wait(steps, name):
                    act.wait_ge(steps.sem, steps.at(name, h))

                nc.scalar.preload_act_table_set("silu_and_others")
                for r in range(4):
                    n = N_IN_C + 4 * h + r
                    convert(n + 1, (r + 1) % 2, N_IN_C // 2 + 2 * h + (r + 1) // 2)
                    act.wait_ge(acc_read, n + 1)
                    if r < 3:
                        name = "qkv"[r]
                        apart(act)
                        H.done(f"tap_{name}", nc.scalar.activation(y[:, r], zc[:, r % 2, CONV - 1:], ACT.Copy,
                                                                  scale=column(wconv[:, CONV - 1], r * GH + h)))
                        wait(dh, f"tap_{name}3")
                        H.done(f"silu_{name}", nc.scalar.activation(y[:, r], y[:, r], ACT.Silu))
                    else:
                        H.done("silu_g", nc.scalar.activation(y[:, 3], y[:, 3], ACT.Silu))
                nc.scalar.preload_act_table_set("natural_log_exp_and_others")
                wait(hp, "gc")
                H.done("gcb", nc.scalar.activation(halves(gcb), auxv(0), ACT.Copy))
                H.done("egb", nc.scalar.activation(halves(egb), auxv(0), ACT.Exp))
                wait(H, "silu_k")
                H.done("sq_q", nc.scalar.activation(sqg[:, 0], y[:, 0], ACT.Square))
                H.done("sq_k", nc.scalar.activation(sqg[:, 1], y[:, 1], ACT.Square))
                for r, name in enumerate("qk"):
                    wait(hp, f"ss_{name}")
                    H.done(f"ln_{name}", nc.scalar.activation(halves(rqk[:, r]), auxv(r), ACT.Ln, bias=eps_col))
                    wait(H, f"ln_{name}")
                    H.done(f"rs_{name}", nc.scalar.activation(rqk[:, r], rqk[:, r], ACT.Exp, scale=-0.5, **({"bias": lnq_col} if r == 0 else {})))
                wait(gh["pool"], "mask")
                H.done("decay", nc.scalar.activation(decay[:], decay[:], ACT.Exp))
                wait(dh, "edk")
                H.done("edk", nc.scalar.activation(edk[:], edk[:], ACT.Exp))
                wait(hp, "t_turned")
                H.done("tinv", nc.scalar.activation(tinv[:].rearrange("p c m -> p (c m)"), aux[:, 0], ACT.Copy))
                for n in range(1, len(LEVELS) - 1):
                    wait(hp, f"t{n}")
                    H.done(f"t{n}", nc.scalar.activation(tinv[:].rearrange("p c m -> p (c m)"), aux[:, 2], ACT.Copy))
                for c in range(QB):
                    wait(hp, f"v{c}")
                    if c:
                        wait(hp, f"s{c - 1}")
                    H.done(f"v{c}", nc.scalar.activation(vnew[:], aux[:, 1, 0:P], ACT.Copy))
                wait(dh, "kbg")
                H.done("kq_k", nc.scalar.activation(kq[:, :, 0], kbg[:, SEQ:T], ACT.Copy))
                H.done("kq_q", nc.scalar.activation(kq[:, :, 1], qg[:, SEQ:T], ACT.Copy))
                wait(hp, f"o{QB - 1}")
                H.done("oT", nc.scalar.activation(y[:, 0, 0:SEQ], aux[:, 3], ACT.Copy))
                wait(H, "oT")
                wait(dh, "do")
                H.done("o_sq", nc.scalar.activation(sqg[:, 0], y[:, 0], ACT.Square))
                wait(hp, "osum")
                H.done("o_ln", nc.scalar.activation(halves(rqk[:, 0]), auxv(0), ACT.Ln, bias=eps_col, scale=1.0 / P))
                wait(H, "o_ln")
                H.done("o_rs", nc.scalar.activation(rqk[:, 0], rqk[:, 0], ACT.Exp, scale=-0.5))
                wait(dh, "og")
                apart(act)
                H.done("g_hi", nc.scalar.activation(g_hi[:, h], y[:, 0], ACT.Copy))
            with act.Fori(0, KD // 2) as i:
                for s in range(2):
                    n = N_OUT_C + 2 * i + s
                    convert(n + 1, 1 - s, N_OUT_C // 2 + i + s)
                    norm_tile(3, 2 * i + s, s, acc_read, n + 1)
            ffn(3, N_FFN1, FT)
            norm_factor(4)

        @block.vector
        def _(dve):
            def convert(n, slot):
                dve.wait_ge(w_hi_made, n + 1)
                nc.vector.tensor_tensor(w_lo[:, slot], w_raw[:, slot], w_hi[:, slot].bitcast(F32), ALU.subtract).then_inc(w_lo_made, 1)

            def norm_tile(k, m, x_sem=None, x_at=None):
                if k == 4:
                    return
                dve.wait_ge(h_hi_made, KD * k + m + 1)
                nc.vector.scalar_tensor_tensor(h_lo[:, m], xT[:, m], column(par, KD * NORM_ROWS[k] + m), h_hi[:, m].bitcast(F32),
                                               ALU.mult, ALU.subtract).then_inc(h_lo_made, 1)

            def add_to_stream(n, m, slot):
                dve.wait_ge(acc_full, n + 1)
                nc.vector.tensor_tensor(halves(xT[:, m]), accv(slot), halves(xT[:, m]), ALU.add).then_inc(acc_read, 1)

            def scaled(out, n, slot):
                dve.wait_ge(acc_full, n + 1)
                nc.vector.tensor_tensor(halves(out), accv(slot), halves(rstd), ALU.mult).then_inc(acc_read, 1)

            def ffn(k, base, g_base):
                dve.wait_ge(rstd_made, k + 1)
                for part, kt in enumerate(PARTS):
                    with dve.Fori(0, kt) as i:
                        n, g = base + 2 * i, g_base + i
                        convert(n + 1, 1)
                        scaled(gate_n, n, 0)
                        convert(n + 2, 0)
                        scaled(up_n, n + 1, 1)
                        dve.wait_ge(silu_made, g + 1)
                        dve.wait_ge(acc_read, n + 2)
                        nc.vector.tensor_tensor(gu[:], up_n[:], gate_s[:], ALU.mult).then_inc(gu_made, 1)
                        dve.wait_ge(g_hi_made, g + 1)
                        nc.vector.tensor_tensor(g_lo[:, i], gu[:], g_hi[:, i].bitcast(F32), ALU.subtract).then_inc(g_lo_made, 1)
                    base += 2 * kt
                    g_base += kt
                    with dve.Fori(0, KD // 2 - 1) as i:
                        for s in range(2):
                            convert(base + 2 * i + s + 1, 1 - s)
                            add_to_stream(base + 2 * i + s, 2 * i + s, s)
                            if part == 2:
                                norm_tile(k + 1, 2 * i + s)
                    i = KD // 2 - 1
                    for s in range(2):
                        if base + 2 * i + s + 1 < N_ALL:
                            convert(base + 2 * i + s + 1, 1 - s)
                        add_to_stream(base + 2 * i + s, 2 * i + s, s)
                        if part == 2:
                            norm_tile(k + 1, 2 * i + s)
                    base += KD

            U, upe = up["dve"], up["pe"]
            dve.wait_ge(upe.sem, upe.at("par"))
            U.done("par", nc.vector.tensor_copy(par[:, 0:45], aux[:, 3, 0:45]))
            U.done("wconv", nc.vector.tensor_copy(wconv[:].rearrange("p i t -> p (i t)"), aux[:, 3, 64:160]))
            dve.wait_ge(upe.sem, upe.at("xs"))
            U.done("xs", nc.vector.tensor_copy(xT[:, :, SEQ:T], aux[:, 2, 0:64].rearrange("p (m t) -> p m t", t=NS)))
            for m in range(KD):
                dve.wait_ge(upe.sem, upe.at(f"x{m}"))
                U.done(f"x{m}", nc.vector.tensor_copy(xT[:, m, 0:SEQ], aux[:, m % 2]))
            dve.wait_ge(U.sem, U.all())
            convert(0, 0)
            for m in range(KD):
                norm_tile(0, m)
            dve.wait_ge(rstd_made, 1)
            for n in range(16):
                convert(N_IN_A + n + 1, (n + 1) % 2)
                scaled(zT[:, IN_A_TILES[n]], N_IN_A + n, n % 2)

            A, pe_at, act_at, pool_at = at["dve"], at["pe"], at["act"], at["pool"]
            for t in range(4):
                dve.wait_ge(pe_at.sem, pe_at.at(f"v_turned{t}"))
                A.done(f"v_kept{t}", nc.vector.tensor_copy(v_tok[:, :, t * P:(t + 1) * P], blocks(aux[:, t % 2])))
            dve.wait_ge(pe_at.sem, pe_at.at("u_turned"))
            A.done("u_kept", nc.vector.tensor_copy(u_tok[0:23], aux[0:23, 0]))
            dve.wait_ge(pe_at.sem, pe_at.at("z_turned"))
            A.done("z_kept", nc.vector.tensor_copy(z_tok[0:NS], aux[0:NS, 1:4]))
            dve.wait_ge(tab_in, 16)
            for h in range(HEADS + 1):
                if h < HEADS:
                    if h:
                        dve.wait_ge(A.sem, A.at(f"max{h - 1}3"))
                    A.done(f"bias{h}", nc.vector.scalar_tensor_tensor(bias[:], att_tab[:, 0], -8.0 * slope(h), att_tab[:, 1], ALU.mult, ALU.add))
                    dve.wait_ge(A.sem, A.at(f"bias{h}"))
                for b in range(QB):
                    off = P * b * (b + 1) // 2
                    if h < HEADS:
                        dve.wait_ge(pe_at.sem, pe_at.at(f"scores{h}{b}"))
                        if h >= 2:
                            dve.wait_ge(pe_at.sem, pe_at.at(f"p_turned{h - 2}{b}"))
                        A.done(f"max{h}{b}", nc.vector.tensor_tensor_reduce(
                            out=prob[:, h % 2, off:off + (b + 1) * P], in0=aux[:, b % 2, 0:(b + 1) * P],
                            in1=bias[:, (3 - b) * P:SEQ], scale=0.125, scalar=NEG, op0=ALU.add, op1=ALU.max,
                            accum_out=att_col[:, h % 2, 0, b:b + 1]))
                        dve.wait_ge(A.sem, A.at(f"max{h}{b}"))
                        A.done(f"neg{h}{b}", nc.vector.tensor_scalar(att_col[:, h % 2, 1, b:b + 1], att_col[:, h % 2, 0, b:b + 1], -1.0, None, ALU.mult))
                    if h and b % 2:
                        dve.wait_ge(pe_at.sem, pe_at.at(f"p_turned{h - 1}{b}"))
                        if b == 3 or h > 1:
                            dve.wait_ge(pe_at.sem, pe_at.at(f"pv{h - 1}1" if b == 3 else f"pv{h - 2}3"))
                        A.done(f"pT{h - 1}{b}", nc.vector.tensor_copy(probT[:, 1, 0:(b + 1) * P], aux[:, 2, 0:(b + 1) * P]))
                if h:
                    hp, par_h = h - 1, (h - 1) % 2
                    dve.wait_ge(act_at.sem, act_at.at(f"exp{hp}3"))
                    A.done(f"inv{hp}", nc.vector.reciprocal(att_col[:, par_h, 3], att_col[:, par_h, 2]))
                    dve.wait_ge(A.sem, A.at(f"inv{hp}"))
                    dve.wait_ge(pe_at.sem, pe_at.at(f"pv{hp}3"))
                    if hp % 2 == 0 and hp:
                        dve.wait_ge(pe_at.sem, pe_at.at(f"o_turned{hp // 2 - 1}"))
                    A.done(f"o{hp}", nc.vector.tensor_tensor(
                        o_tok[:, :, HD * par_h:HD * par_h + HD], aux[:, 3, 0:QB * HD].rearrange("p (b d) -> p b d", d=HD),
                        att_col[:, par_h, 3].unsqueeze(2).to_broadcast([P, QB, HD]), ALU.mult))
                    if h % 2 == 0:
                        t = h // 2 - 1
                        dve.wait_ge(act_at.sem, act_at.at(f"g_hi{t}"))
                        A.done(f"g_lo{t}", nc.vector.tensor_tensor(g_lo[:, t, 0:SEQ], aux[:, 2], g_hi[:, t, 0:SEQ].bitcast(F32), ALU.subtract))
            dve.wait_ge(pe_at.sem, pe_at.at("hist_turned"))
            A.done("histT", nc.vector.tensor_copy(histT[:].rearrange("p g b j -> p (g b j)"), aux[:, 3, 0:480]))
            dve.wait_ge(A.sem, A.at("histT"))
            for g, w in enumerate(POOL_WINDOWS):
                A.done(f"tail{g}", nc.vector.tensor_reduce(tail[:], histT[:, g, :, POOL_HIST - (w - 1):POOL_HIST], AX.X, ALU.add))
                dve.wait_ge(A.sem, A.at(f"tail{g}"))
                A.done(f"tail_sum{g}", nc.vector.tensor_tensor(tail[:], tail[:], zT[:, 12 + g, SEQ:T], ALU.add))
                dve.wait_ge(A.sem, A.at(f"tail_sum{g}"))
                if g >= 2:
                    dve.wait_ge(pe_at.sem, pe_at.at(f"pooled{g - 2}"))
                A.done(f"tail_p{g}", nc.vector.scalar_tensor_tensor(pooled[:, g % 2, SEQ:T], tail[:], 1.0 / w, zT[:, 12 + g, SEQ:T], ALU.mult, ALU.subtract))
                dve.wait_ge(A.sem, A.at(f"tail_p{g}"))
            for g in range(4):
                dve.wait_ge(act_at.sem, act_at.at(f"pool_hi{g}"))
                A.done(f"pool_lo{g}", nc.vector.scalar_tensor_tensor(halves(g_lo[:, 4 + g]), auxv(g % 2), par[:, 40 + g:41 + g],
                                                                    halves(g_hi[:, 4 + g].bitcast(F32)), ALU.mult, ALU.subtract))
            for b in range(NS):
                dve.wait_ge(pe_at.sem, pe_at.at(f"q_spread{b}"))
                if b == 0:
                    dve.wait_ge(ck_in, 32)
                    dve.wait_ge(self_in, 64)
                if b == 4:
                    dve.wait_ge(ck2_in, 32)
                    dve.wait_ge(self2_in, 64)
                ext = (P, KEYS_B + 1)
                for x in range(2):
                    if b:
                        dve.wait_ge(A.sem, A.at(f"sum_{'ab'[x]}{b - 1}"))
                    A.done(f"prod_{'ab'[x]}{b}", nc.vector.tensor_tensor(prod[0:ext[x], x], aux[0:ext[x], b % 2], ck[0:ext[x], b % 4, x], ALU.mult))
                for x in range(2):
                    dve.wait_ge(A.sem, A.at(f"prod_{'ab'[x]}{b}"))
                    A.done(f"sum_{'ab'[x]}{b}", nc.vector.tensor_reduce(
                        dec_s[0:ext[x], x, b * HEADS:(b + 1) * HEADS], prod[0:ext[x], x].rearrange("p (h d) -> p h d", d=HD), AX.X, ALU.add))
            dve.wait_ge(pe_at.sem, pe_at.at("s_turned"))
            dve.wait_ge(sel_in, 32)
            A.done("dec_max", nc.vector.tensor_tensor_reduce(out=dec_p[0:64], in0=aux[0:64, 2, 0:KEYS], in1=dec_tab[0:64], scale=0.125, scalar=NEG,
                                                             op0=ALU.add, op1=ALU.max, accum_out=dec_col[0:64, 0:1]))
            dve.wait_ge(A.sem, A.at("dec_max"))
            A.done("dec_neg", nc.vector.tensor_scalar(dec_col[0:64, 1:2], dec_col[0:64, 0:1], -1.0, None, ALU.mult))
            dve.wait_ge(act_at.sem, act_at.at("dec_exp"))
            A.done("dec_inv", nc.vector.reciprocal(dec_col[0:64, 3:4], dec_col[0:64, 2:3]))
            dve.wait_ge(A.sem, A.at("dec_inv"))
            A.done("dec_norm", nc.vector.tensor_scalar(dec_p[0:64], dec_p[0:64], dec_col[0:64, 3:4], None, ALU.mult))
            dve.wait_ge(pe_at.sem, pe_at.at("dp_turned"))
            nc.vector.tensor_copy(dec_pT[:, 0], aux[:, 3, 0:64])
            A.done("dec_pT", nc.vector.tensor_copy(dec_pT[0:KEYS_B + 1, 1], aux[0:KEYS_B + 1, 3, 64:128]))
            for r in range(2):
                rows_r = slice(HD * r, HD * r + HD)
                out = aux[rows_r, 0, 0:64].rearrange("p (t b r) -> p t b r", t=4, r=2)[:, :, :, r]
                dve.wait_ge(act_at.sem, act_at.at(f"dec_hi{r}"))
                A.done(f"dec_lo{r}", nc.vector.tensor_tensor(g_lo[rows_r, 0:4, SEQ:T], out, g_hi[rows_r, 0:4, SEQ:T].bitcast(F32), ALU.subtract))
            for n in range(KD):
                convert(N_OUT_A + n + 1, (n + 1) % 2)
                add_to_stream(N_OUT_A + n, n, n % 2)
                norm_tile(1, n)
            ffn(1, N_FFN0, 0)

            R, ppe, pact, ppool = pre["dve"], pre["pe"], pre["act"], pre["pool"]

            def own(steps, name, turn=0):
                dve.wait_ge(steps.sem, steps.at(name, turn))

            dve.wait_ge(rstd_made, 3)
            own(pact, "wab_hi")
            R.done("wab_lo", nc.vector.tensor_tensor(wab_lo[:], wab_pad[:], wab_hi[:].bitcast(F32), ALU.subtract))
            for half in range(2):
                own(ppe, f"chist{half}")
                R.done(f"chist{half}", nc.vector.tensor_copy(chist[:, 12 * half:12 * half + 12].rearrange("p t b i -> p (t b i)"), aux[:, half, 0:288]))
            own(R, "chist1")
            for i in range(CONV - 1):
                dst = cprod if i == 0 else ctmp
                if i == 2:
                    own(R, "sum1")
                R.done(f"prod{i}", nc.vector.tensor_tensor(dst[:], chist[:, :, :, i], wconv[:, i].unsqueeze(2).to_broadcast([P, 3 * GH, NS]), ALU.mult))
                if i:
                    own(R, f"prod{i}")
                    R.done(f"sum{i}", nc.vector.tensor_tensor(cprod[:], cprod[:], ctmp[:], ALU.add))
            own(ppe, "ab")
            R.done("ab", nc.vector.tensor_tensor(halves(ab[0:64]), aux[0:64, 2:4, 0:TH], halves(rstd[0:64]), ALU.mult))
            own(pact, "exp_b")
            R.done("beta1", nc.vector.tensor_scalar(abt[0:8, 0], abt[0:8, 0], 1.0, None, ALU.add))
            own(R, "beta1")
            own(ppool, "rows_zero")
            R.done("beta", nc.vector.reciprocal(rows[0:8], abt[0:8, 0]))
            dve.wait_ge(acol_in, 32)
            R.done("dt", nc.vector.tensor_scalar(abt[32:40, 0], ab[32:40], acol[32:40, 1:2], None, ALU.add))
            own(R, "dt")
            R.done("abs", nc.vector.scalar_tensor_tensor(abt[32:40, 1], abt[32:40, 0], -1.0, abt[32:40, 0], ALU.mult, ALU.min))
            own(pact, "ln_sp")
            R.done("sp", nc.vector.scalar_tensor_tensor(abt[32:40, 2], abt[32:40, 0], 0.0, abt[32:40, 1], ALU.max, ALU.add))
            own(pact, "exp_a")
            R.done("nega", nc.vector.tensor_scalar(acol[32:40, 3:4], acol[32:40, 2:3], -1.0, None, ALU.mult))
            own(R, "nega")
            R.done("g", nc.vector.tensor_scalar(abt[32:40, 0], abt[32:40, 2], acol[32:40, 3:4], None, ALU.mult))
            own(R, "g")
            R.done("cum", nc.vector.tensor_tensor_scan(rows[32:40], delta[32:40, G_KEEP:G_KEEP + T], abt[32:40, 0], 0.0, ALU.mult, ALU.add))
            own(ppe, "rows_turned")
            R.done("tokcols", nc.vector.tensor_copy(tokcols[:].rearrange("p c m -> p (c m)"), aux[:, 0, 0:256]))

            H, hp, ah, ph = gh["dve"], gh["pe"], gh["act"], gh["pool"]
            with dve.Fori(0, GH) as h:
                def wait(steps, name):
                    dve.wait_ge(steps.sem, steps.at(name, h))

                def chunk_col(row):
                    return tokcols[:, :, bass.ds(row + h, 1)].to_broadcast([P, QB, P])

                def chunks(x):
                    return x[:, 0:SEQ].rearrange("p (c m) -> p c m", m=P)

                for r in range(4):
                    n, name = N_IN_C + 4 * h + r, "qkvg"[r]
                    convert(n + 1, (r + 1) % 2)
                    if r == 2:
                        wait(hp, "tail_q")
                        wait(ah, "tap_q")
                    scaled(zc[:, r % 2, CONV - 1:] if r < 3 else y[:, 3], n, r % 2)
                    if r < 3:
                        wait(ah, f"tap_{name}")
                        for i in range(CONV - 1):
                            H.done(f"tap_{name}{i}", nc.vector.scalar_tensor_tensor(
                                y[:, r, 0:SEQ], zc[:, r % 2, i:i + SEQ], column(wconv[:, i], r * GH + h), y[:, r, 0:SEQ], ALU.mult, ALU.add))
                            wait(H, f"tap_{name}{i}")
                        H.done(f"tap_{name}3", nc.vector.tensor_tensor(y[:, r, SEQ:T], y[:, r, SEQ:T], cprod[:, r * GH + h], ALU.add))
                wait(hp, "tail_v")
                dve.wait_ge(zr_stored, 32 * h)
                H.done("z_rows", nc.vector.tensor_copy(z_rows[0:11].rearrange("p r m -> p (r m)"), aux[0:11, 3, 0:3 * P]))
                wait(hp, "beta")
                H.done("betab", nc.vector.tensor_copy(halves(betab), auxv(1)))
                wait(ah, "rs_q")
                H.done("qn", nc.vector.tensor_tensor(y[:, 0], y[:, 0], rqk[:, 0], ALU.mult))
                wait(ah, "rs_k")
                H.done("kn", nc.vector.tensor_tensor(y[:, 1], y[:, 1], rqk[:, 1], ALU.mult))
                wait(H, "kn")
                H.done("qg", nc.vector.tensor_tensor(qg[:], y[:, 0], egb[:], ALU.mult))
                H.done("kb", nc.vector.tensor_tensor(kbg[:], y[:, 1], betab[:], ALU.mult))
                wait(H, "kb")
                H.done("kbg", nc.vector.tensor_tensor(kbg[:], kbg[:], egb[:], ALU.mult))
                H.done("diff", nc.vector.tensor_tensor(decay[:], chunks(gcb), chunk_col(32), ALU.subtract))
                H.done("edk", nc.vector.tensor_tensor(edk[:], chunks(gcb)[:, :, P - 1], tokcols[:, :, bass.ds(32 + h, 1)].rearrange("p c m -> p (c m)"), ALU.subtract))
                wait(hp, "turn_v")
                H.done("vb", nc.vector.tensor_tensor(vb[:], blocks(aux[:, 0]), chunk_col(0), ALU.mult))
                wait(hp, "turn_k")
                wait(ah, "edk")
                H.done("kdec", nc.vector.tensor_tensor(kdec[:], blocks(aux[:, 1]), edk[:].unsqueeze(2).to_broadcast([P, QB, P]), ALU.mult))
                wait(ah, "decay")
                wait(hp, "qk")
                H.done("attT", nc.vector.tensor_tensor(attT[:], blocks(aux[:, 3]), decay[:], ALU.mult))
                H.done("lowT", nc.vector.tensor_tensor(lowT[:], blocks(aux[:, 2]), decay[:], ALU.mult))
                wait(H, "lowT")
                H.done("low", nc.vector.scalar_tensor_tensor(lowT[:].rearrange("p c m -> p (c m)"), betab[:, 0:SEQ], -1.0,
                                                             lowT[:].rearrange("p c m -> p (c m)"), ALU.mult, ALU.mult))
                wait(ph, "lev0")
                identity = ident.unsqueeze(1).to_broadcast([P, QB, P])
                H.done("one", nc.vector.tensor_tensor(tinvT[:], lev[:, 0], identity, ALU.add))
                for n in range(1, len(LEVELS)):
                    wait(hp, f"p{n}")
                    if n > 1:
                        wait(hp, f"u{n - 1}")
                    H.done(f"ip{n}", nc.vector.tensor_tensor(ip[:], blocks(aux[:, 1]), identity, ALU.add))
                    wait(hp, f"u{n}")
                    H.done(f"u{n}", nc.vector.tensor_copy(tinvT[:].rearrange("p c m -> p (c m)"), aux[:, 3]))
                for c in range(QB):
                    if c:
                        wait(hp, f"ks{c}")
                        H.done(f"r{c}", nc.vector.tensor_tensor(resid[:], vb[:, c], aux[:, 0, 0:P], ALU.subtract))
                    wait(hp, f"s{c}")
                    if c == 0:
                        dve.wait_ge(st_stored, 16 * h)
                        H.done("s0", nc.vector.tensor_copy(state[:], aux[:, 2, 0:P]))
                    else:
                        wait(H, f"s{c - 1}")
                        H.done(f"s{c}", nc.vector.scalar_tensor_tensor(state[:], state[:], egb[:, (c + 1) * P - 1:(c + 1) * P], aux[:, 2, 0:P], ALU.mult, ALU.add))
                H.done("dkq", nc.vector.tensor_tensor(sm[:, 0], y[:, 0, SEQ:T], y[:, 1, SEQ:T], ALU.mult))
                H.done("dvb", nc.vector.tensor_tensor(sm[:, 1], y[:, 2, SEQ:T], betab[:, SEQ:T], ALU.mult))
                wait(H, "dvb")
                wait(hp, "dx")
                sx = aux[:, 0, 0:2 * NS].rearrange("p (b r) -> p b r", r=2)
                H.done("dv", nc.vector.tensor_tensor(sm[:, 2], sm[:, 1], sx[:, :, 0], ALU.subtract))
                wait(H, "dv")
                wait(hp, "dqk")
                H.done("dqk", nc.vector.tensor_tensor(sm[:, 3], sm[:, 2], aux[:, 1, 0:NS], ALU.mult))
                wait(H, "dqk")
                H.done("do", nc.vector.tensor_tensor(y[:, 0, SEQ:T], sm[:, 3], sx[:, :, 1], ALU.add))
                wait(hp, "dv_turned")
                H.done("d_rows", nc.vector.tensor_copy(kv_rows[0:NS].rearrange("p r m -> p (r m)"), aux[0:NS, 2, 0:2 * P]))
                wait(H, "d_rows")
                H.done("dvexp", nc.vector.tensor_tensor(lev[0:NS].rearrange("p a c m -> p (a c) m"), kv_rows[0:NS, 1].unsqueeze(1).to_broadcast([NS, NS, P]),
                                                        ident[0:NS, 0:NS].unsqueeze(2).to_broadcast([NS, NS, P]), ALU.mult))
                wait(hp, "outer")
                wait(ph, "s_decayed")
                H.done("s_new", nc.vector.tensor_tensor(s_in[:].rearrange("p b m -> p (b m)"), s_in[:].rearrange("p b m -> p (b m)"),
                                                        aux[:, 0:2].rearrange("p a t -> p (a t)"), ALU.add))
                wait(ah, "o_rs")
                H.done("on", nc.vector.scalar_tensor_tensor(y[:, 0], y[:, 0], par[:, 44:45], rqk[:, 0], ALU.mult, ALU.mult))
                wait(H, "on")
                H.done("og", nc.vector.tensor_tensor(y[:, 0], y[:, 0], y[:, 3], ALU.mult))
                wait(ah, "g_hi")
                H.done("g_lo", nc.vector.tensor_tensor(g_lo[:, h], y[:, 0], g_hi[:, h].bitcast(F32), ALU.subtract))
            with dve.Fori(0, KD // 2) as i:
                for s in range(2):
                    convert(N_OUT_C + 2 * i + s + 1, 1 - s)
                    add_to_stream(N_OUT_C + 2 * i + s, 2 * i + s, s)
                    norm_tile(3, 2 * i + s)
            ffn(3, N_FFN1, FT)

            Z, pf = fin["dve"], fin["pe"]
            dve.wait_ge(rstd_made, 5)
            dve.wait_ge(acc_read, N_ALL)
            for m in range(KD):
                Z.done(f"y{m}", nc.vector.scalar_tensor_tensor(y_fin[:, m], xT[:, m], par[:, 4 * KD + m:4 * KD + m + 1], rstd[:], ALU.mult, ALU.mult))
            for b in range(QB + 1):
                rows_b = P if b < QB else NS
                dve.wait_ge(pf.sem, pf.at(f"y{b}"))
                Z.done(f"y_tok{b}", nc.vector.tensor_copy(y_tok[0:rows_b, b], acc[0:rows_b, 2 * (b % 2):2 * (b % 2) + 2].rearrange("p a t -> p (a t)")))

        @block.gpsimd
        def _(pool):
            def add_squares(k):
                if k:
                    pool.wait_ge(ss_full, k)
                nc.gpsimd.memset(ssum[:], 0.0).then_inc(ss_clear, 1)
                pool.wait_ge(ss_clear, k + 1)
                with pool.Fori(0, KD // 2) as i:
                    for s in range(2):
                        at_least = KD * k + 2 * i + s
                        pool.wait_ge(sq_made, at_least + 1)
                        pool.wait_ge(ss_added, at_least)
                        nc.gpsimd.tensor_tensor(ssum[:], ssum[:], sq[:, s], ALU.add).then_inc(ss_added, 1)

            add_squares(0)
            A, up_dve, pe_at, dve_at, act_at = at["pool"], up["dve"], at["pe"], at["dve"], at["act"]
            pool.wait_ge(up_dve.sem, up_dve.all())
            pool.wait_ge(up["pe"].sem, up["pe"].all())
            pool.dma_start(att_tab[:], a["attention_table"].rearrange("p (r c) -> p r c", r=2)).then_inc(tab_in, 16)
            pool.dma_start(hist_rows[0:120], a["state_pool"][0].rearrange("b j c -> (b j) c")).then_inc(hist_in, 16)
            pool.dma_start(sel8[0:NS], a["select_table"].rearrange("b (c m) -> b c m", m=P)).then_inc(sel_in, 16)
            pool.dma_start(dec_tab[0:64], a["decode_table"]).then_inc(sel_in, 16)
            for t in range(4):
                pool.wait_ge(act_at.sem, act_at.at(f"k_kept{t}"))
                pool.dma_start(o["a_k_prompt"][0, 0].rearrange("(b p) h d -> p b (h d)", p=P)[:, :, t * P:(t + 1) * P],
                               k_stage[:, t % 2]).then_inc(k_stored[t % 2], 16)
            pool.wait_ge(dve_at.sem, dve_at.at("v_kept3"))
            pool.dma_start(o["a_v_prompt"][0, 0].rearrange("(b p) h d -> p b (h d)", p=P), v_tok[:]).then_inc(stored, 16)
            pool.wait_ge(dve_at.sem, dve_at.at("z_kept"))
            pool.dma_start(o["pool_prompt"][0, 0], u_tok[0:POOL_HIST]).then_inc(stored, 16)
            pool.dma_start(o["pool_sample"][0, :, POOL_HIST - 1, :], u_tok[POOL_HIST:POOL_HIST + NS]).then_inc(stored, 16)
            pool.dma_start(o["a_k_sample"][0].rearrange("b t h d -> b t (h d)")[:, PAST], z_tok[0:NS, 1]).then_inc(stored, 16)
            pool.dma_start(o["a_v_sample"][0].rearrange("b t h d -> b t (h d)")[:, PAST], z_tok[0:NS, 2]).then_inc(stored, 16)
            pool.wait_ge(dve_at.sem, dve_at.at("g_lo3"))
            pool.dma_start(cnt[:], a["pool_table"].rearrange("p (g t) -> p g t", g=4)).then_inc(pool_in, 16)
            pool.dma_start(wpool[:], a["w_pool"][0].rearrange("g c d -> c g d")).then_inc(pool_in, 16)
            pool.wait_ge(pool_in, 32)
            for g in range(4):
                src = zT[:, 12 + g]
                for n in range(g + 1):
                    dst, s = run[:, n % 2], 1 << n
                    A.done(f"run{g}{n}a", nc.gpsimd.tensor_tensor(dst[:, s:SEQ], src[:, s:SEQ], src[:, 0:SEQ - s], ALU.add))
                    A.done(f"run{g}{n}b", nc.gpsimd.tensor_copy(dst[:, 0:s], src[:, 0:s]))
                    pool.wait_ge(A.sem, A.at(f"run{g}{n}b"))
                    src = dst
                mean = run[:, (g + 1) % 2]
                A.done(f"mean{g}", nc.gpsimd.tensor_tensor(mean[:, 0:SEQ], src[:, 0:SEQ], cnt[:, g, 0:SEQ], ALU.mult))
                pool.wait_ge(A.sem, A.at(f"mean{g}"))
                if g >= 2:
                    pool.wait_ge(pe_at.sem, pe_at.at(f"pooled{g - 2}"))
                A.done(f"pool{g}", nc.gpsimd.tensor_tensor(pooled[:, g % 2, 0:SEQ], mean[:, 0:SEQ], zT[:, 12 + g, 0:SEQ], ALU.subtract))
                pool.wait_ge(A.sem, A.at(f"pool{g}"))
            add_squares(1)
            R = pre["pool"]
            pool.wait_ge(acc_full, N_OUT_A + 1)
            for q in range(2):
                pool.wait_ge(k_stored[q], 32)
            pool.wait_ge(stored, 16 * 5)
            pool.dma_start(delta[:], a["delta_table"]).then_inc(delta_in, 16)
            pool.dma_start(crow[0:3 * NS], a["state_conv"][0].rearrange("b i c -> (b i) c")).then_inc(crow_in, 16)
            pool.dma_start(wab_raw[:], w_in_c[:, 4 * QK:].rearrange("(k p) m -> p k m", p=P)).then_inc(wab_in, 16)
            pool.dma_start(acol[32:40, 0:1], a["a_log_c"].rearrange("o h -> h o")).then_inc(acol_in, 16)
            pool.dma_start(acol[32:40, 1:2], a["dt_bias_c"].rearrange("o h -> h o")).then_inc(acol_in, 16)
            add_squares(2)
            pool.wait_ge(acc_read, N_IN_C)
            pool.wait_ge(g_lo_made, FT)
            R.done("zc", nc.gpsimd.memset(zc[:, :, 0:CONV - 1], 0.0))
            R.done("wab_zero", nc.gpsimd.memset(wab_pad[:], 0.0))
            pool.wait_ge(wab_in, 16)
            pool.wait_ge(R.sem, R.at("wab_zero"))
            R.done("wab_pad_b", nc.gpsimd.tensor_copy(wab_pad[:, :, 0:GH], wab_raw[:, :, 0:GH]))
            R.done("wab_pad_a", nc.gpsimd.tensor_copy(wab_pad[:, :, 32:32 + GH], wab_raw[:, :, GH:2 * GH]))
            R.done("rows_zero", nc.gpsimd.memset(rows[:], 0.0))
            pool.wait_ge(pre["dve"].sem, pre["dve"].all())

            H, dh, hp = gh["pool"], gh["dve"], gh["pe"]
            with pool.Fori(0, GH) as h:
                def wait(steps, name):
                    pool.wait_ge(steps.sem, steps.at(name, h))

                pool.wait_ge(dh.sem, dh.all(h))
                H.done("rowsel", nc.gpsimd.tensor_tensor(rowsel[0:64], rows[0:64], delta[0:64, bass.ds(G_SEL + h, 1)].to_broadcast([64, T]), ALU.mult))
                wait(dh, "diff")
                tri = delta[:, G_TRI:G_TRI + P].unsqueeze(1).to_broadcast([P, QB, P])
                H.done("mask", nc.gpsimd.tensor_tensor(decay[:], decay[:], tri, ALU.add))
                wait(dh, "low")
                for n in range(len(LEVELS)):
                    if n == 2:
                        wait(dh, "one")
                    elif n > 2:
                        wait(hp, f"p{n - 2}")
                    level = delta[:, G_LEVEL + n * P:G_LEVEL + (n + 1) * P].unsqueeze(1).to_broadcast([P, QB, P])
                    H.done(f"lev{n}", nc.gpsimd.tensor_tensor(lev[:, n % 2], lowT[:], level, ALU.mult))
                wait(hp, "dx")
                pool.wait_ge(s_read, 16 * h + 16)
                H.done("s_decayed", nc.gpsimd.tensor_tensor(s_in[:], s_in[:], egb[:, SEQ:T].unsqueeze(2).to_broadcast([P, NS, P]), ALU.mult))
            add_squares(3)
            add_squares(4)


_OUTS = {
    "y_prompt": (1, 512, 1024), "y_sample": (8, 1, 1024),
    "a_k_prompt": (1, 1, 512, 8, 64), "a_v_prompt": (1, 1, 512, 8, 64),
    "pool_prompt": (1, 1, 15, 512), "conv_prompt": (1, 1, 3, 3072), "gdn_prompt": (1, 1, 8, 128, 128),
    "a_k_sample": (1, 8, 513, 8, 64), "a_v_sample": (1, 8, 513, 8, 64),
    "pool_sample": (1, 8, 15, 512), "conv_sample": (1, 8, 3, 3072), "gdn_sample": (1, 8, 8, 128, 128),
}


def kernel(**inputs):
    import numpy as _np
    import concourse.bacc as _bacc
    from concourse import mybir as _mybir
    from concourse.bass_utils import run_bass_kernel_spmd as _run

    arrays = {name: _np.ascontiguousarray(x) for name, x in inputs.items()}
    arrays["par_rows"] = _np.concatenate([arrays[n].reshape(-1, P) for n in (
        "norm_mix", "norm_ffn", "norm_final", "pool_scale", "norm_out_c")], 0)
    arrays["const_table"], arrays["delta_table"] = constant_table(), delta_table()
    arrays["attention_table"], arrays["decode_table"] = attention_table(), decode_table()
    arrays["pool_table"], arrays["select_table"] = pool_table(), select_table()
    used = [n for n in arrays if n not in ("norm_mix", "norm_ffn", "norm_final", "pool_scale", "norm_out_c")]
    nc = _bacc.Bacc("TRN2", target_bir_lowering=False, num_devices=1)
    a = {n: nc.dram_tensor(f"in_{n}", arrays[n].shape, _mybir.dt.from_np(arrays[n].dtype), kind="ExternalInput").ap() for n in used}
    o = {n: nc.dram_tensor(f"out_{n}", shape, F32, kind="ExternalOutput").ap() for n, shape in _OUTS.items()}
    build(nc, a, o)
    r = _run(nc, [{f"in_{n}": arrays[n] for n in used}], core_ids=[0])
    return tuple(r.results[0][f"out_{n}"] for n in _OUTS)
```

```python
import math
from contextlib import ExitStack

import concourse.bass as bass
import numpy as np
from concourse import mybir

F32 = mybir.dt.float32
F32R = mybir.dt.float32r
ALU = mybir.AluOpType
ACT = mybir.ActivationFunctionType
AX = mybir.AxisListType

P = 128
D_MODEL = 1024
SEQ = 512
NS = 8
T = SEQ + NS
TH = T // 2
KD = D_MODEL // P
HEADS = 8
HD = 64
A_W = HEADS * HD
PAST = 512
POOL_HIST = 15
POOL_WINDOWS = (2, 4, 8, 16)
QB = SEQ // P
FFN = 2816
FT = FFN // P
PARTS = (8, 8, 6)
GH = 8
CONV = 4
QK = GH * P
SLOT = 2048
LEVELS = (1, 2, 4, 8, 16, 32, 64)
EPS = 1e-6
NEG = -1e30
KEYS_A = 128
KEYS_B = 96
KEYS = KEYS_A + KEYS_B + 1

N_IN_A = 0
N_OUT_A = N_IN_A + 16
N_FFN0 = N_OUT_A + KD
N_FFN = 2 * FT + KD * len(PARTS)
N_IN_C = N_FFN0 + N_FFN
N_OUT_C = N_IN_C + 4 * GH
N_FFN1 = N_OUT_C + KD
N_ALL = N_FFN1 + N_FFN
BLOCK = KD * P
IN_A_TILES = [t + 4 * r for t in range(4) for r in range(3)] + [12, 13, 14, 15]

C_ID = 0
C_ONE = C_ID + P
C_COL = C_ONE + P
C_END = C_COL + 3
G_LEVEL = 0
G_TRI = G_LEVEL + len(LEVELS) * P
G_HALF = G_TRI + P
G_KEEP = G_HALF + 2 * P
G_SEL = G_KEEP + T
G_END = G_SEL + GH


def multiplicity(d):
    return int(0 <= d <= 128) + int(d >= 0 and d % 4 == 0 and d // 4 <= 128) + int(d >= 0 and d % 16 == 0 and d // 16 <= 128)


def slope(h):
    return 2.0 ** (-8.0 * (h + 1) / HEADS)


def log_count(d):
    c = multiplicity(d)
    return math.log(c) if c else NEG


def constant_table():
    t = np.ones((P, C_END), np.float32)
    t[:, C_ID:C_ID + P] = np.eye(P)
    t[:, C_COL] = EPS
    t[:, C_COL + 1] = -0.5 * math.log(P)
    return t


def delta_table():
    t = np.zeros((P, G_END), np.float32)
    j = np.arange(P)[:, None]
    i = np.arange(P)[None, :]
    for n, s in enumerate(LEVELS):
        t[:, G_LEVEL + n * P:G_LEVEL + (n + 1) * P] = (j // (2 * s) == i // (2 * s)) & (j % (2 * s) < s) & (i % (2 * s) >= s)
    t[:, G_TRI:G_TRI + P] = np.where(i >= j, 0.0, NEG)
    t[0:32, G_HALF:G_HALF + P] = 1.0
    t[32:64, G_HALF + P:G_HALF + 2 * P] = 1.0
    t[:, G_KEEP:G_KEEP + SEQ] = (np.arange(SEQ) % P != 0)[None, :]
    for h in range(GH):
        t[h, G_SEL + h] = t[32 + h, G_SEL + h] = 1.0
    return t


def attention_table():
    d = np.arange(P)[:, None] + 3 * P - np.arange(SEQ)[None, :]
    count = np.vectorize(log_count)(np.arange(-P, SEQ + P + 1))
    lc = count[d + P]
    return np.concatenate([d, np.where(lc < NEG / 2, NEG, 8.0 * lc)], 1).astype(np.float32)


def decode_table():
    dist = [PAST - t for t in range(PAST - KEYS_A, PAST)] + [PAST - 4 * r for r in range(KEYS_B)] + [0]
    rows = [[8.0 * (log_count(d) - slope(h) * d) for d in dist] for _ in range(NS) for h in range(HEADS)]
    return np.asarray(rows, np.float32)


def pool_table():
    rows = [[1.0 / min(t + 1, w) for t in range(SEQ)] + [1.0 / w] * NS for w in POOL_WINDOWS]
    return np.broadcast_to(np.asarray(rows, np.float32).reshape(1, -1), (P, len(rows) * T)).copy()


def select_table():
    return np.repeat(np.eye(NS, dtype=np.float32), P, 1)


IN_C_PART = (0, 1, 3, 2)
NORM_ROWS = (0, 2, 1, 3, 4)


class Steps:

    def __init__(self, sem, names):
        self.sem, self.names, self.n = sem, {x: n for n, x in enumerate(names)}, 0
        assert len(self.names) == len(names)

    def at(self, name, turn=0):
        return turn * len(self.names) + self.names[name] + 1

    def all(self, turn=1):
        return turn * len(self.names)

    def done(self, name, instruction):
        assert self.names[name] == self.n % len(self.names), (name, self.n)
        self.n += 1
        instruction.then_inc(self.sem, 1)


def build(nc, a, o):
    ctx = ExitStack()
    with ctx:
        def sem(name):
            return ctx.enter_context(nc.semaphore(name))

        def sb(name, cols, dt=F32, stack=ctx):
            shape = [P, *cols] if isinstance(cols, (list, tuple)) else [P, cols]
            return stack.enter_context(nc.sbuf_tensor(name, shape, dt))

        xT = sb("xT", [KD, T])
        const = sb("const", C_END)
        par = sb("par", 48)
        wconv = sb("wconv", [CONV, 3 * GH])
        rstd = sb("rstd", T)
        ssum = sb("ssum", T)
        sq = sb("sq", [2, T])
        w_raw = sb("w_raw", [2, BLOCK])
        w_hi = sb("w_hi", [2, BLOCK], F32R)
        w_lo = sb("w_lo", [2, BLOCK], F32R)
        with ExitStack() as s:
            gateT = sb("gateT", [KD, T], F32, s)
        g_hi = sb("g_hi", [KD, T], F32R)
        g_lo = sb("g_lo", [KD, T], F32R)

        with ExitStack() as s:
            ck = sb("ck", [4, 2, A_W], F32, s)
            cv = sb("cv", [4, 2, A_W], F32, s)
        h_hi = sb("h_hi", [KD, T], F32R)
        h_lo = sb("h_lo", [KD, T], F32R)

        with ExitStack() as s:
            x_tok = sb("x_tok", [QB, D_MODEL], F32, s)
            xs_tok = sb("xs_tok", D_MODEL, F32, s)
            par_rows = sb("par_rows", [2, P], F32, s)
        with ExitStack() as s:
            zT = sb("zT", [16, T], F32, s)
            v_tok = sb("v_tok", [QB, A_W], F32, s)
            k_stage = sb("k_stage", [2, QB, P], F32, s)
            z_tok = sb("z_tok", [3, A_W], F32, s)
            u_tok = sb("u_tok", A_W, F32, s)
            hist_rows = sb("hist_rows", A_W, F32, s)
            sel8 = sb("sel8", [NS, P], F32, s)
            prod = sb("prod", [2, A_W], F32, s)
            dec_s = sb("dec_s", [2, NS * HEADS], F32, s)
            dec_tab = sb("dec_tab", KEYS, F32, s)
            dec_p = sb("dec_p", KEYS, F32, s)
            dec_pT = sb("dec_pT", [2, NS * HEADS], F32, s)
            dec_col = sb("dec_col", 4, F32, s)
            with ExitStack() as s1:
                att_tab = sb("att_tab", [2, SEQ], F32, s1)
                bias = sb("bias", SEQ, F32, s1)
                prob = sb("prob", [2, 10 * P], F32, s1)
                probT = sb("probT", [2, SEQ], F32, s1)
                o_tok = sb("o_tok", [QB, P], F32, s1)
                att_col = sb("att_col", [2, 4, QB], F32, s1)
            with ExitStack() as s1:
                histT = sb("histT", [4, NS, POOL_HIST], F32, s1)
                cnt = sb("cnt", [4, T], F32, s1)
                wpool = sb("wpool", [4, P], F32, s1)
                run = sb("run", [2, T], F32, s1)
                tail = sb("tail", NS, F32, s1)
                pooled = sb("pooled", [2, T], F32, s1)
        with ExitStack() as s:
            gate_n = sb("gate_n", T, F32, s)
            gate_s = sb("gate_s", T, F32, s)
            up_n = sb("up_n", T, F32, s)
            gu = sb("gu", T, F32, s)
        with ExitStack() as s:
            zc = sb("zc", [2, CONV - 1 + T], F32, s)
            y = sb("y", [3, T], F32, s)
            delta = sb("delta", G_END, F32, s)
            chist = sb("chist", [3 * GH, NS, CONV - 1], F32, s)
            cprod = sb("cprod", [3 * GH, NS], F32, s)
            rows = sb("rows", T, F32, s)
            acol = sb("acol", 4, F32, s)
            tokcols = sb("tokcols", [QB, 64], F32, s)
            z_rows = sb("z_rows", [3, P], F32, s)
            with ExitStack() as s1:
                wab_hi = sb("wab_hi", [KD, 64], F32R, s1)
                wab_lo = sb("wab_lo", [KD, 64], F32R, s1)
                crow = sb("crow", 3 * GH * P, F32, s1)
                ctmp = sb("ctmp", [3 * GH, NS], F32, s1)
                wab_raw = sb("wab_raw", [KD, 2 * GH], F32, s1)
                wab_pad = sb("wab_pad", [KD, 64], F32, s1)
                ab = sb("ab", T, F32, s1)
                abt = sb("abt", [3, T], F32, s1)
            with ExitStack() as s1:
                qn = sb("qn", T, F32, s1)
                kn = sb("kn", T, F32, s1)
                rowsel = sb("rowsel", T, F32, s1)
                gcb = sb("gcb", T, F32, s1)
                egb = sb("egb", T, F32, s1)
                betab = sb("betab", T, F32, s1)
                decay = sb("decay", [QB, P], F32, s1)
                bdecay = sb("bdecay", [QB, P], F32, s1)
                lowT = sb("lowT", [QB, P], F32, s1)
                ip = sb("ip", [QB, P], F32, s1)
                edk = sb("edk", QB, F32, s1)
                with ExitStack() as s2:
                    sqg = sb("sqg", [2, T], F32, s2)
                    rqk = sb("rqk", [2, T], F32, s2)
                with ExitStack() as s2:
                    lev = sb("lev", [2, QB, P], F32, s2)
                    sb("unused", 2 * (T - SEQ), F32, s2)
                    tinv = sb("tinv", [QB, P], F32, s2)
                    tinvT = sb("tinvT", [QB, P], F32, s2)
                    sb("unused2", 2 * (T - SEQ), F32, s2)
                    qg = sb("qg", T, F32, s2)
                    kbg = sb("kbg", T, F32, s2)
                    attT = sb("attT", [QB, P], F32, s2)
                    vb = sb("vb", [QB, P], F32, s2)
                    kdec = sb("kdec", [QB, P], F32, s2)
                    t_all = sb("t_all", [QB, P], F32, s2)
                    kq = sb("kq", [NS, 2], F32, s2)
                    sm = sb("sm", [7, NS], F32, s2)
                    state = sb("state", P, F32, s2)
                    resid = sb("resid", P, F32, s2)
                    vnew = sb("vnew", P, F32, s2)
                    yo = sb("yo", T, F32, s2)
                    osq = sb("osq", T, F32, s2)
                    ors = sb("ors", T, F32, s2)
                    s_in = sb("s_in", [NS, P], F32, s2)
                    dvexp = sb("dvexp", [2, SEQ], F32, s2)
                    kv_rows = sb("kv_rows", [2, P], F32, s2)
        with ExitStack() as s:
            y_fin = sb("y_fin", [KD, T], F32, s)
            y_tok = sb("y_tok", [QB + 1, D_MODEL], F32, s)

        acc = ctx.enter_context(nc.psum_tensor("acc", [P, 4, 512], F32))
        aux = ctx.enter_context(nc.psum_tensor("aux", [P, 4, 512], F32))

        def halves(x):
            return x.rearrange("p (b t) -> p b t", b=2)

        def apart(engine):
            engine.nop()

        def blocks(x):
            return x.rearrange("p (c m) -> p c m", m=P)

        def accv(slot):
            return acc[:, 2 * slot:2 * slot + 2, 0:TH]

        def auxv(pair):
            return aux[:, 2 * pair:2 * pair + 2, 0:TH]

        def column(tensor, n):
            return tensor[:, n:n + 1] if isinstance(n, int) else tensor[:, bass.ds(n, 1)]

        ident = const[:, C_ID:C_ID + P]
        ones = const[:, C_ONE:C_ONE + P]
        eps_col = const[:, C_COL:C_COL + 1]
        lnq_col = const[:, C_COL + 1:C_COL + 2]
        one_col = const[:, C_COL + 2:C_COL + 3]

        const_in, par_in, xs_in, tab_in, sel_in, hist_in, pool_in = (
            sem(n) for n in ("const_in", "par_in", "xs_in", "tab_in", "sel_in", "hist_in", "pool_in"))
        x_in = [sem(f"x_in{b}") for b in range(QB)]
        w_loaded = [sem("w_loaded0"), sem("w_loaded1")]
        w_hi_made, w_lo_made = sem("w_hi_made"), sem("w_lo_made")
        acc_full = sem("acc_full")
        acc_read = sem("acc_read")
        h_hi_made, h_lo_made, sq_made, ss_added = (sem(n) for n in ("h_hi_made", "h_lo_made", "sq_made", "ss_added"))
        ss_clear, ss_full, ln_made, rstd_made = (sem(n) for n in ("ss_clear", "ss_full", "ln_made", "rstd_made"))
        silu_made, gu_made, g_hi_made, g_lo_made = (sem(n) for n in ("silu_made", "gu_made", "g_hi_made", "g_lo_made"))
        ck_in, cv_in, ck2_in, cv2_in, self_in, self2_in = (
            sem(n) for n in ("ck_in", "cv_in", "ck2_in", "cv2_in", "self_in", "self2_in"))
        k_stored = [sem("k_stored0"), sem("k_stored1")]
        delta_in, crow_in, wab_in, acol_in, s_read, s_stored, st_stored, zr_stored = (
            sem(n) for n in ("delta_in", "crow_in", "wab_in", "acol_in", "s_read", "s_stored", "st_stored", "zr_stored"))
        stored = sem("stored")
        copied = sem("copied")
        y_stored = sem("y_stored")

        up = {e: Steps(sem(f"up_{e}"), n) for e, n in {
            "pe": ["par", "xs"] + [f"x{m}" for m in range(KD)],
            "dve": ["par", "wconv", "xs"] + [f"x{m}" for m in range(KD)],
        }.items()}
        heads_a = [f"{h}{b}" for h in range(HEADS) for b in range(QB)]
        order = [("sc", h, b) for h in range(HEADS) for b in range(QB)]
        pe_att = []
        for t in range(4):
            pe_att += [f"v_turned{t}", f"k_turned{t}"]
        pe_att += ["u_turned", "z_turned"]
        for h in range(HEADS + 1):
            for b in range(QB):
                if h < HEADS:
                    pe_att.append(f"scores{h}{b}")
                if h:
                    pe_att += [f"pv{h - 1}{b - 1}"] if b else []
                    pe_att.append(f"p_turned{h - 1}{b}")
            if h:
                pe_att.append(f"pv{h - 1}{QB - 1}")
                if h % 2 == 0:
                    pe_att.append(f"o_turned{h // 2 - 1}")
        pe_att += ["hist_turned"] + [f"pooled{g}" for g in range(4)]
        pe_att += [f"q_spread{b}" for b in range(NS)] + ["s_turned", "dp_turned", "dec_out"]
        dve_att = [f"v_kept{t}" for t in range(4)] + ["u_kept", "z_kept"]
        for h in range(HEADS + 1):
            if h < HEADS:
                dve_att.append(f"bias{h}")
            for b in range(QB):
                if h < HEADS:
                    dve_att += [f"max{h}{b}", f"neg{h}{b}"]
                if h and b % 2:
                    dve_att.append(f"pT{h - 1}{b}")
            if h:
                dve_att += [f"inv{h - 1}", f"o{h - 1}"]
                if h % 2 == 0:
                    dve_att.append(f"g_lo{h // 2 - 1}")
        dve_att += ["histT"] + [x for g in range(4) for x in (f"tail{g}", f"tail_sum{g}", f"tail_p{g}")]
        dve_att += [f"pool_lo{g}" for g in range(4)]
        dve_att += [f"{x}{b}" for b in range(NS) for x in ("prod_a", "prod_b", "sum_a", "sum_b")]
        dve_att += ["dec_max", "dec_neg", "dec_inv", "dec_norm", "dec_pT", "dec_lo0", "dec_lo1"]
        act_att = [f"k_kept{t}" for t in range(4)]
        for h in range(HEADS + 1):
            for b in range(QB):
                if h < HEADS:
                    act_att.append(f"exp{h}{b}")
                if h and b % 2 == 0:
                    act_att.append(f"pT{h - 1}{b}")
            if h and h % 2 == 0:
                act_att.append(f"g_hi{h // 2 - 1}")
        act_att += [f"pool_hi{g}" for g in range(4)] + ["dec_exp", "dec_hi0", "dec_hi1"]
        pool_att = []
        for g in range(4):
            pool_att += [f"run{g}{n}{x}" for n in range(g + 1) for x in "ab"] + [f"mean{g}", f"pool{g}"]
        at = {e: Steps(sem(f"mix_{e}"), n) for e, n in
              {"pe": pe_att, "dve": dve_att, "act": act_att, "pool": pool_att}.items()}

        pre = {e: Steps(sem(f"pre_{e}"), n) for e, n in {
            "pe": ["chist0", "chist1", "ab", "rows_turned"],
            "act": ["wab_hi", "exp_b", "exp_sp", "ln_sp", "exp_a"],
            "dve": ["wab_lo", "chist0", "chist1", "prod0", "prod1", "sum1", "prod2", "sum2", "ab",
                    "beta1", "beta", "dt", "abs", "sp", "nega", "g", "cum", "tokcols"],
            "pool": ["zc", "wab_zero", "wab_pad_b", "wab_pad_a", "rows_zero"],
        }.items()}
        NL = len(LEVELS)
        taps = lambda r: [f"tap_{r}{i}" for i in range(4)]
        gg = {e: Steps(sem(f"heads_g_{e}"), n) for e, n in {
            "pe": ["tail_q", "tail_k"],
            "act": ["tap_q", "tap_k", "silu_q", "silu_k", "silu_g"],
            "dve": ["z_q"] + taps("q") + ["z_k"] + taps("k"),
        }.items()}
        ga = {e: Steps(sem(f"heads_a_{e}"), n) for e, n in {
            "pe": ["tail_v", "gc", "beta", "ss_q", "ss_k", "kk", "t_turned", "p1", "t1", "u1", "p2", "t2", "u2", "p3", "t3", "u3",
                   "p4", "t4", "u4", "p5", "t5", "u5", "turn_k", "p6", "turn_v", "u6", "qk"],
            "act": ["tap_v", "gcb", "egb", "sq_q", "sq_k", "ln_q", "rs_q", "ln_k", "rs_k", "decay", "edk", "tinv",
                    "t1", "t2", "t3", "t4", "kq_k", "kq_q", "silu_v", "t5"],
            "dve": taps("v") + ["betab", "z_v", "diff", "edk", "qn", "kn", "bdecay", "low", "one", "ip1", "u1", "ip2", "u2",
                                "qg", "kb", "kbg", "ip3", "u3", "ip4", "u4", "ip5", "u5", "kdec", "dkq", "dvb", "keep_k", "keep_e", "keep_c",
                                "ip6", "vb", "u6", "attT"],
            "pool": ["rowsel", "mask"] + [f"lev{n}" for n in range(NL)],
        }.items()}
        gb = {e: Steps(sem(f"heads_b_{e}"), n) for e, n in {
            "pe": ["v0", "o0", "s0"] + [f"{x}{c}" for c in range(1, QB) for x in ("ks", "v", "o", "s")] + ["dx", "dqk", "dk_turned", "dv_turned", "osum", "outer"],
            "act": [f"v{c}" for c in range(QB)] + ["oT", "o_sq", "o_ln", "o_rs", "g_hi"],
            "dve": ["s0", "r1", "s1", "r2", "s2", "r3", "s3", "dv", "dqk", "do", "d_rows", "dvexp", "s_new", "on", "og", "g_lo"],
            "pool": ["s_decayed"],
        }.items()}
        fin = {e: Steps(sem(f"fin_{e}"), n) for e, n in {
            "pe": [f"y{b}" for b in range(QB + 1)], "dve": [f"y{m}" for m in range(KD)] + [f"y_tok{b}" for b in range(QB + 1)]}.items()}

        w_in_a, w_out_a = a["w_in_a"][0], a["w_out_a"][0]
        w_in_c, w_out_c = a["w_in_c"][0], a["w_out_c"][0]

        def column_blocks(w, k0=0, kt=KD, cols=None):
            w = w[k0 * P:(k0 + kt) * P, 0:cols or w.shape[1]]
            return w.rearrange("(k p) (c m) -> c p k m", p=P, m=P)

        block = ctx.enter_context(nc.Block())

        @block.sync
        def _(sp):
            def load(n, slot, src, kt=KD):
                if not isinstance(n, int) or n >= 2:
                    sp.wait_ge(w_lo_made, n - 1)
                sp.dma_start(w_raw[:, slot, 0:kt * P].rearrange("p (k m) -> p k m", m=P), src).then_inc(w_loaded[slot], 16)

            for b in range(QB):
                sp.dma_start(x_tok[:, b], a["x_prompt"][0, b * P:(b + 1) * P, :]).then_inc(x_in[b], 16)
            in_a = column_blocks(w_in_a)
            for n in range(16):
                load(N_IN_A + n, n % 2, in_a[IN_A_TILES[n]])
            out_a = column_blocks(w_out_a)
            load(N_OUT_A, 0, out_a[0])
            load(N_OUT_A + 1, 1, out_a[1])
            sp.wait_ge(acc_full, N_OUT_A)

            sp.dma_start(o["pool_sample"][0, :, 0:POOL_HIST - 1, :], a["state_pool"][0, :, 1:POOL_HIST, :]).then_inc(copied, 16)
            sp.dma_start(o["conv_sample"][0, :, 0:CONV - 2, :], a["state_conv"][0, :, 1:CONV - 1, :]).then_inc(copied, 16)

            def cached(dst, src, b0, signal):
                cache = src[0, b0:b0 + 4].rearrange("b t h d -> t b (h d)")
                sp.dma_start(dst[:, :, 0, :], cache[PAST - KEYS_A:PAST]).then_inc(signal, 16)
                sp.dma_start(dst[0:KEYS_B, :, 1, :], cache[0:PAST - KEYS_A:4]).then_inc(signal, 16)

            def own_row(dst, r, b0, signal):
                for b in range(4):
                    sp.dma_start(dst[KEYS_B:KEYS_B + 1, b, 1, :], z_tok[b0 + b:b0 + b + 1, r, :]).then_inc(signal, 16)

            sp.wait_ge(at["dve"].sem, at["dve"].at("z_kept"))
            cached(ck, a["state_a_k"], 0, ck_in)
            own_row(ck, 1, 0, self_in)
            cached(cv, a["state_a_v"], 0, cv_in)
            own_row(cv, 2, 0, cv_in)
            sp.wait_ge(at["dve"].sem, at["dve"].at("sum_b3"))
            cached(ck, a["state_a_k"], 4, ck2_in)
            own_row(ck, 1, 4, self2_in)
            sp.wait_ge(at["dve"].sem, at["dve"].at(f"sum_b{NS - 1}"))
            cached(ck, a["state_a_v"], 4, cv2_in)
            own_row(ck, 2, 4, cv2_in)
            for n in range(2, KD, 1):
                load(N_OUT_A + n, n % 2, out_a[n])

            def ffn(layer, base):
                gate, upw = column_blocks(a["w_ffn_gate"][layer]), column_blocks(a["w_ffn_up"][layer])
                k0 = 0
                for part, kt in enumerate(PARTS):
                    with sp.Fori(0, kt) as i:
                        load(base + 2 * i, 0, gate[i + k0])
                        load(base + 2 * i + 1, 1, upw[i + k0])
                        if layer == 0 and part < 2:
                            old, new = (("state_a_k", "a_k_sample"), ("state_a_v", "a_v_sample"))[part]
                            sp.dma_start(o[new][0].rearrange("b t h d -> b t (h d)")[:, 0:PAST][i],
                                         a[old][0].rearrange("b t h d -> b t (h d)")[i]).then_inc(copied, 16)
                    base += 2 * kt
                    down = column_blocks(a["w_ffn_down"][layer], k0, kt)
                    with sp.Fori(0, KD // 2) as i:
                        for s in range(2):
                            load(base + 2 * i + s, s, down[2 * i + s], kt)
                    base += KD
                    k0 += kt

            ffn(0, N_FFN0)
            in_c = column_blocks(w_in_c, cols=4 * QK)
            out_c = column_blocks(w_out_c)
            a_dve, b_dve = ga["dve"], gb["dve"]

            def turn(it, ahead=None, a_on=True, b_on=True):
                if a_on:
                    conv_prompt = o["conv_prompt"][0, 0].rearrange("i (r h m) -> h i r m", r=3, m=P)[it - 1]
                    conv_sample = o["conv_sample"][0, :, CONV - 2].rearrange("b (r h m) -> h b r m", r=3, m=P)[it - 1]
                if b_on:
                    gdn_prompt = o["gdn_prompt"][0, 0].rearrange("h k v -> h k v")[it - 2]
                    gdn_sample = o["gdn_sample"][0].rearrange("b h k v -> h k b v")[it - 2]
                    if not isinstance(it, int) or it > 2:
                        sp.wait_ge(s_stored, 16 * (it - 2))
                    sp.dma_start(s_in[:], a["state_gdn"][0].rearrange("b h k v -> h k b v")[it - 2]).then_inc(s_read, 16)
                if ahead:
                    load(N_IN_C + 4 * it + 2, 0, in_c[GH * IN_C_PART[2] + it])
                if a_on:
                    sp.wait_ge(a_dve.sem, a_dve.at("z_v", it - 1))
                    sp.dma_start(conv_prompt, z_rows[0:3]).then_inc(zr_stored, 16)
                    sp.dma_start(conv_sample, z_rows[3:11]).then_inc(zr_stored, 16)
                if ahead:
                    load(N_IN_C + 4 * it + 3, 1, in_c[GH * IN_C_PART[3] + it])
                    load(N_IN_C + 4 * it + 4, 0, ahead[0])
                if b_on:
                    sp.wait_ge(b_dve.sem, b_dve.at(f"s{QB - 1}", it - 2))
                    sp.dma_start(gdn_prompt, state[:]).then_inc(st_stored, 16)
                if ahead:
                    load(N_IN_C + 4 * it + 5, 1, ahead[1])
                if b_on:
                    sp.wait_ge(b_dve.sem, b_dve.at("s_new", it - 2))
                    sp.dma_start(gdn_sample, s_in[:]).then_inc(s_stored, 16)

            for r in range(2):
                load(N_IN_C + r, r, in_c[GH * r])
            turn(0, [in_c[GH * r + 1] for r in range(2)], False, False)
            turn(1, [in_c[GH * r + 2] for r in range(2)], True, False)
            turn(2, [in_c[GH * r + 3] for r in range(2)])
            with sp.Fori(3, GH - 1) as it:
                turn(it, [in_c[GH * r + it + 1] for r in range(2)])
            turn(GH - 1, [out_c[0], out_c[1]])
            turn(GH)
            turn(GH + 1, None, False)
            with sp.Fori(1, KD // 2) as i:
                for s in range(2):
                    load(N_OUT_C + 2 * i + s, s, out_c[2 * i + s])
            ffn(1, N_FFN1)
            for b in range(QB + 1):
                sp.wait_ge(fin["dve"].sem, fin["dve"].at(f"y_tok{b}"))
                if b < QB:
                    sp.dma_start(o["y_prompt"][0, b * P:(b + 1) * P, :], y_tok[:, b]).then_inc(y_stored, 16)
                else:
                    sp.dma_start(o["y_sample"].rearrange("b t d -> (b t) d"), y_tok[0:NS, b]).then_inc(y_stored, 16)
            sp.wait_ge(y_stored, 16 * (QB + 1))
            sp.wait_ge(stored, 16 * 5)
            for q in range(2):
                sp.wait_ge(k_stored[q], 32)
            sp.wait_ge(copied, 16 * (2 * NS + 2))
            sp.wait_ge(s_stored, 16 * GH)
            sp.wait_ge(st_stored, 16 * GH)
            sp.wait_ge(zr_stored, 32 * GH)

        @block.tensor
        def _(pe):
            def product(n, slot, kt, xh, xl, hi_at=None, lo_at=None):
                if not isinstance(n, int) or n >= 2:
                    pe.wait_ge(acc_read, n - 1)
                pe.wait_ge(w_hi_made, n + 1)
                for part, (w, x, ready) in enumerate(((w_hi, xh, hi_at), (w_hi, xl, lo_at), (w_lo, xh, None))):
                    if part == 2:
                        pe.wait_ge(w_lo_made, n + 1)
                    for k in range(kt):
                        if ready:
                            pe.wait_ge(*ready(k))
                        for b in range(2):
                            last = nc.tensor.matmul(acc[:, 2 * slot + b, 0:TH], w[:, slot, k * P:(k + 1) * P],
                                                    x[:, k, b * TH:(b + 1) * TH], start=part == 0 and k == 0,
                                                    stop=part == 2 and k == kt - 1)
                last.then_inc(acc_full, 1)

            def norm_sum(k):
                pe.wait_ge(ss_added, KD * (k + 1))
                for b in range(2):
                    mm = nc.tensor.matmul(aux[:, b, 0:TH], ones, ssum[:, b * TH:(b + 1) * TH], start=True, stop=True)
                mm.then_inc(ss_full, 1)

            def normed(k):
                return {"hi_at": lambda kt: (h_hi_made, KD * k + kt + 1), "lo_at": lambda kt: (h_lo_made, KD * k + kt + 1)}

            def ffn(k, base, g_base):
                norm_sum(k)
                for kt in PARTS:
                    with pe.Fori(0, kt) as i:
                        product(base + 2 * i, 0, KD, h_hi, h_lo, **normed(k))
                        product(base + 2 * i + 1, 1, KD, h_hi, h_lo)
                    base += 2 * kt
                    with pe.Fori(0, KD // 2) as i:
                        product(base + 2 * i, 0, kt, g_hi, g_lo, lambda j: (g_hi_made, g_base + j + 1), lambda j: (g_lo_made, g_base + j + 1))
                        product(base + 2 * i + 1, 1, kt, g_hi, g_lo)
                    base += KD
                    g_base += kt

            U = up["pe"]
            pe.wait_ge(const_in, 16)
            pe.wait_ge(par_in, 32)
            nc.tensor.transpose(aux[:, 3, 0:45], par_rows[0:45, 0], ident[0:45, 0:45])
            U.done("par", nc.tensor.transpose(aux[:, 3, 64:64 + 96], par_rows[0:96, 1], ident[0:96, 0:96]))
            pe.wait_ge(xs_in, 16)
            for m in range(KD):
                tr = nc.tensor.transpose(aux[:, 2, m * NS:(m + 1) * NS], xs_tok[0:NS, m * P:(m + 1) * P], ident[0:NS, 0:NS])
            U.done("xs", tr)
            for m in range(KD):
                if m >= 2:
                    pe.wait_ge(up["dve"].sem, up["dve"].at(f"x{m - 2}"))
                for b in range(QB):
                    if m == 0:
                        pe.wait_ge(x_in[b], 16)
                    tr = nc.tensor.transpose(aux[:, m % 2, b * P:(b + 1) * P], x_tok[:, b, m * P:(m + 1) * P], ident)
                U.done(f"x{m}", tr)
            pe.wait_ge(up["dve"].sem, up["dve"].at(f"x{KD - 1}"))
            norm_sum(0)
            for n in range(16):
                product(N_IN_A + n, n % 2, KD, h_hi, h_lo, **(normed(0) if n == 0 else {}))

            A, dve_at, act_at = at["pe"], at["dve"], at["act"]
            pe.wait_ge(acc_read, 16)
            pe.wait_ge(rstd_made, 1)
            for t in range(4):
                if t >= 2:
                    pe.wait_ge(dve_at.sem, dve_at.at(f"v_kept{t - 2}"))
                for b in range(QB):
                    tr = nc.tensor.transpose(aux[:, t % 2, b * P:(b + 1) * P], zT[:, 8 + t, b * P:(b + 1) * P], ident)
                A.done(f"v_turned{t}", tr)
                if t >= 2:
                    pe.wait_ge(act_at.sem, act_at.at(f"k_kept{t - 2}"))
                for b in range(QB):
                    tr = nc.tensor.transpose(aux[:, 2 + t % 2, b * P:(b + 1) * P], zT[:, 4 + t, b * P:(b + 1) * P], ident)
                A.done(f"k_turned{t}", tr)
            pe.wait_ge(dve_at.sem, dve_at.at("v_kept3"))
            for t in range(4):
                tr = nc.tensor.transpose(aux[0:POOL_HIST + NS, 0, t * P:(t + 1) * P], zT[:, 12 + t, SEQ - POOL_HIST:T], ident)
            A.done("u_turned", tr)
            pe.wait_ge(act_at.sem, act_at.at("k_kept3"))
            for r in range(3):
                for t in range(4):
                    tr = nc.tensor.transpose(aux[0:NS, 1 + r, t * P:(t + 1) * P], zT[:, 4 * r + t, SEQ:T], ident)
            A.done("z_turned", tr)
            pe.wait_ge(dve_at.sem, dve_at.at("z_kept"))

            def scores(h, b):
                rows_h = slice(HD * (h % 2), HD * (h % 2) + HD)
                if h or b >= 2:
                    hh, bb = (h, b - 2) if b >= 2 else (h - 1, b + 2)
                    pe.wait_ge(dve_at.sem, dve_at.at(f"max{hh}{bb}"))
                A.done(f"scores{h}{b}", nc.tensor.matmul(
                    aux[:, b % 2, 0:(b + 1) * P], zT[rows_h, h // 2, b * P:(b + 1) * P],
                    zT[rows_h, 4 + h // 2, 0:(b + 1) * P], start=True, stop=True))

            def turn_probs(h, b):
                pe.wait_ge(act_at.sem, act_at.at(f"exp{h}{b}"))
                if b:
                    last_at = act_at if b % 2 else dve_at
                    pe.wait_ge(last_at.sem, last_at.at(f"pT{h}{b - 1}"))
                elif h:
                    pe.wait_ge(dve_at.sem, dve_at.at(f"pT{h - 1}3"))
                    if h % 2 == 0:
                        pe.wait_ge(dve_at.sem, dve_at.at(f"g_lo{h // 2 - 1}"))
                off = P * b * (b + 1) // 2
                for k in range(b + 1):
                    tr = nc.tensor.transpose(aux[:, 2, k * P:(k + 1) * P], prob[:, h % 2, off + k * P:off + (k + 1) * P], ident)
                A.done(f"p_turned{h}{b}", tr)

            def weigh(h, b):
                made = dve_at if b % 2 else act_at
                pe.wait_ge(made.sem, made.at(f"pT{h}{b}"))
                if h and b == 0:
                    pe.wait_ge(dve_at.sem, dve_at.at(f"o{h - 1}"))
                for k in range(b + 1):
                    mm = nc.tensor.matmul(aux[:, 3, b * HD:(b + 1) * HD], probT[:, b % 2, k * P:(k + 1) * P],
                                          v_tok[:, k, h * HD:(h + 1) * HD], start=k == 0, stop=k == b)
                A.done(f"pv{h}{b}", mm)

            for h in range(HEADS + 1):
                for b in range(QB):
                    if h < HEADS:
                        scores(h, b)
                    if h:
                        if b:
                            weigh(h - 1, b - 1)
                        turn_probs(h - 1, b)
                if h:
                    weigh(h - 1, QB - 1)
                    if h % 2 == 0:
                        t = h // 2 - 1
                        pe.wait_ge(dve_at.sem, dve_at.at(f"o{h - 1}"))
                        for b in range(QB):
                            tr = nc.tensor.transpose(aux[:, 2, b * P:(b + 1) * P], o_tok[:, b], ident)
                        A.done(f"o_turned{t}", tr)
            pe.wait_ge(hist_in, 16)
            for g in range(4):
                tr = nc.tensor.transpose(aux[:, 3, g * 120:(g + 1) * 120], hist_rows[0:120, g * P:(g + 1) * P], ident[0:120, 0:120])
            A.done("hist_turned", tr)
            for g in range(4):
                pe.wait_ge(at["pool"].sem, at["pool"].at(f"pool{g}"))
                pe.wait_ge(dve_at.sem, dve_at.at(f"tail_p{g}"))
                if g == 0:
                    pe.wait_ge(dve_at.sem, dve_at.at("g_lo3"))
                    pe.wait_ge(pool_in, 32)
                if g >= 2:
                    pe.wait_ge(dve_at.sem, dve_at.at(f"pool_lo{g - 2}"))
                for b in range(2):
                    mm = nc.tensor.matmul(auxv(g % 2)[:, b], wpool[:, g], pooled[:, g % 2, b * TH:(b + 1) * TH], start=True, stop=True)
                A.done(f"pooled{g}", mm)
            pe.wait_ge(sel_in, 32)
            pe.wait_ge(dve_at.sem, dve_at.at("pool_lo3"))
            for b in range(NS):
                if b >= 2:
                    pe.wait_ge(dve_at.sem, dve_at.at(f"prod_b{b - 2}"))
                A.done(f"q_spread{b}", nc.tensor.matmul(aux[:, b % 2, 0:A_W], sel8[0:NS, b], z_tok[0:NS, 0], start=True, stop=True))
            pe.wait_ge(dve_at.sem, dve_at.at(f"sum_b{NS - 1}"))
            nc.tensor.transpose(aux[0:64, 2, 0:KEYS_A], dec_s[:, 0], ident)
            A.done("s_turned", nc.tensor.transpose(aux[0:64, 2, KEYS_A:KEYS], dec_s[0:KEYS_B + 1, 1], ident[0:KEYS_B + 1, 0:KEYS_B + 1]))
            pe.wait_ge(dve_at.sem, dve_at.at("dec_norm"))
            nc.tensor.transpose(aux[:, 3, 0:64], dec_p[0:64, 0:KEYS_A], ident[0:64, 0:64])
            A.done("dp_turned", nc.tensor.transpose(aux[0:KEYS_B + 1, 3, 64:128], dec_p[0:64, KEYS_A:KEYS], ident[0:64, 0:64]))
            pe.wait_ge(dve_at.sem, dve_at.at("dec_pT"))
            pe.wait_ge(cv_in, 96)
            for b in range(NS):
                if b == 4:
                    pe.wait_ge(cv2_in, 96)
                vals = cv if b < 4 else ck
                for t in range(4):
                    c = (t * NS + b) * 2
                    nc.tensor.matmul(aux[:, 0, c:c + 2], vals[:, b % 4, 0, t * P:(t + 1) * P],
                                     dec_pT[:, 0, b * HEADS + 2 * t:b * HEADS + 2 * t + 2], start=True, stop=False)
                    mm = nc.tensor.matmul(aux[:, 0, c:c + 2], vals[0:KEYS_B + 1, b % 4, 1, t * P:(t + 1) * P],
                                          dec_pT[0:KEYS_B + 1, 1, b * HEADS + 2 * t:b * HEADS + 2 * t + 2], start=False, stop=True)
            A.done("dec_out", mm)
            pe.wait_ge(act_at.sem, act_at.all())
            pe.wait_ge(dve_at.sem, dve_at.all())
            for n in range(KD):
                product(N_OUT_A + n, n % 2, KD, g_hi, g_lo)
            ffn(1, N_FFN0, 0)

            R = pre["pe"]
            norm_sum(2)
            pe.wait_ge(rstd_made, 3)
            pe.wait_ge(crow_in, 16)
            for half in range(2):
                for t in range(12):
                    tile = 12 * half + t
                    tr = nc.tensor.transpose(aux[:, half, t * 24:(t + 1) * 24], crow[0:24, tile * P:(tile + 1) * P], ident[0:24, 0:24])
                R.done(f"chist{half}", tr)
            pe.wait_ge(pre["dve"].sem, pre["dve"].at("wab_lo"))
            for w, x, part in ((wab_hi, h_hi, 0), (wab_hi, h_lo, 1), (wab_lo, h_hi, 2)):
                pe.wait_ge(h_hi_made, KD * 3)
                pe.wait_ge(h_lo_made, KD * 3)
                for k in range(KD):
                    for b in range(2):
                        mm = nc.tensor.matmul(aux[0:64, 2 + b, 0:TH], w[:, k], x[:, k, b * TH:(b + 1) * TH],
                                              start=part == 0 and k == 0, stop=part == 2 and k == KD - 1)
            R.done("ab", mm)
            pe.wait_ge(pre["dve"].sem, pre["dve"].at("cum"))
            for c in range(QB):
                tr = nc.tensor.transpose(aux[:, 0, c * 64:(c + 1) * 64], rows[0:64, c * P:(c + 1) * P], ident[0:64, 0:64])
            R.done("rows_turned", tr)
            pe.wait_ge(pre["dve"].sem, pre["dve"].at("tokcols"))

            G, A, B = gg["pe"], ga["pe"], gb["pe"]

            def product_sixth(n, slot, j):
                if j == 0:
                    pe.wait_ge(acc_read, n - 1)
                    pe.wait_ge(w_hi_made, n + 1)
                if j == 4:
                    pe.wait_ge(w_lo_made, n + 1)
                w, x = ((w_hi, h_hi), (w_hi, h_lo), (w_lo, h_hi))[j // 2]
                for k in range(4 * (j % 2), 4 * (j % 2) + 4):
                    for b in range(2):
                        last = nc.tensor.matmul(acc[:, 2 * slot + b, 0:TH], w[:, slot, k * P:(k + 1) * P],
                                                x[:, k, b * TH:(b + 1) * TH], start=j == 0 and k == 0, stop=j == 5 and k == KD - 1)
                if j == 5:
                    last.then_inc(acc_full, 1)

            def turn(it, g_on, a_on, b_on):
                ha, hb = it - 1, it - 2

                def wait(steps, name, h):
                    pe.wait_ge(steps.sem, steps.at(name, h))

                def weights_product(j):
                    if g_on:
                        if j == 6 and a_on:
                            wait(ga["dve"], "z_v", ha)
                        if j in (12, 18):
                            wait(gg["dve"], "z_q" if j == 12 else "z_k", it)
                        product_sixth(N_IN_C + 4 * it + j // 6, j // 6 % 2, j % 6)

                def tail_rows(stage, h, name, n, zslot, slot):
                    pe.wait_ge(acc_read, n + 1)
                    stage.done(f"tail_{name}", nc.tensor.transpose(acc[0:11, 2 * slot, TH:TH + P], zc[:, zslot, SEQ:CONV - 1 + T], ident))

                def spread(name, lhs, rhs):
                    for b in range(2):
                        mm = nc.tensor.matmul(aux[:, b, 0:TH], lhs, rhs[:, b * TH:(b + 1) * TH], start=True, stop=True)
                    A.done(name, mm)

                def by_chunk(name, bank, lhs, rhs):
                    for c in range(QB):
                        mm = nc.tensor.matmul(aux[:, bank, c * P:(c + 1) * P], lhs(c), rhs(c), start=True, stop=True)
                    A.done(name, mm)

                def turned(name, bank, src):
                    for c in range(QB):
                        tr = nc.tensor.transpose(aux[:, bank, c * P:(c + 1) * P], src(c), ident)
                    A.done(name, tr)

                def cols(x):
                    return lambda c: x[:, c * P:(c + 1) * P]

                def level_p(n):
                    if not a_on:
                        return
                    wait(ga["act"], "tinv" if n == 1 else f"t{n - 1}", ha)
                    if n > 1:
                        wait(ga["dve"], f"u{n - 1}", ha)
                    wait(ga["pool"], f"lev{n}", ha)
                    by_chunk(f"p{n}", 0, lambda c: lev[:, n % 2, c], lambda c: tinv[:, c])

                def level_t(n):
                    if not a_on:
                        return
                    wait(ga["dve"], f"ip{n}", ha)
                    if n < NL - 1:
                        by_chunk(f"t{n}", 1, lambda c: tinvT[:, c], lambda c: ip[:, c])
                    by_chunk(f"u{n}", 0, lambda c: ip[:, c], lambda c: tinvT[:, c])

                def chunk_k(c):
                    if b_on:
                        wait(gb["dve"], f"s{c - 1}", hb)
                        B.done(f"ks{c}", nc.tensor.matmul(aux[:, 2, 0:P], kbg[:, c * P:(c + 1) * P], state[:], start=True, stop=True))

                def chunk_v(c):
                    if b_on:
                        if c:
                            wait(gb["dve"], f"r{c}", hb)
                        B.done(f"v{c}", nc.tensor.matmul(aux[:, 2, P:2 * P], t_all[:, c], resid[:] if c else vb[:, 0], start=True, stop=True))

                def chunk_o(c):
                    if b_on:
                        wait(gb["act"], f"v{c}", hb)
                        if c:
                            nc.tensor.matmul(aux[:, 3, c * P:(c + 1) * P], state[:], qg[:, c * P:(c + 1) * P], start=True, stop=False)
                        B.done(f"o{c}", nc.tensor.matmul(aux[:, 3, c * P:(c + 1) * P], vnew[:], attT[:, c], start=c == 0, stop=True))
                        B.done(f"s{c}", nc.tensor.matmul(aux[:, 2, 2 * P:3 * P], kdec[:, c], vnew[:], start=True, stop=True))

                weights_product(0)
                if a_on:
                    wait(gg["dve"], "z_k", ha)
                    tail_rows(A, ha, "v", N_IN_C + 4 * ha + 3, 0, 1)
                weights_product(1)
                if a_on:
                    wait(ga["pool"], "rowsel", ha)
                    if b_on:
                        wait(ga["dve"], "attT", hb)
                    spread("gc", delta[0:64, G_HALF + P:G_HALF + 2 * P], rowsel[0:64])
                if b_on:
                    pe.wait_ge(ga["dve"].sem, ga["dve"].all(it - 1))
                    pe.wait_ge(ga["act"].sem, ga["act"].all(it - 1))
                chunk_v(0)
                weights_product(2)
                if a_on:
                    wait(ga["act"], "egb", ha)
                    spread("beta", delta[0:64, G_HALF:G_HALF + P], rowsel[0:64])
                chunk_o(0)
                weights_product(3)
                if a_on:
                    wait(ga["act"], "sq_q", ha)
                    wait(ga["dve"], "betab", ha)
                    spread("ss_q", ones, sqg[:, 0])
                chunk_k(1)
                weights_product(4)
                if a_on:
                    wait(ga["act"], "ln_q", ha)
                    spread("ss_k", ones, sqg[:, 1])
                chunk_v(1)
                weights_product(5)
                chunk_o(1)
                weights_product(6)
                chunk_k(2)
                weights_product(7)
                if a_on:
                    wait(ga["dve"], "kn", ha)
                    by_chunk("kk", 0, cols(kn), cols(kn))
                if g_on:
                    tail_rows(G, it, "q", N_IN_C + 4 * it, 0, 0)
                chunk_v(2)
                weights_product(8)
                chunk_o(2)
                weights_product(9)
                if a_on:
                    wait(ga["dve"], "one", ha)
                    turned("t_turned", 1, lambda c: tinvT[:, c])
                chunk_k(3)
                weights_product(10)
                level_p(1)
                chunk_v(3)
                weights_product(11)
                level_t(1)
                chunk_o(3)
                weights_product(12)
                level_p(2)
                if b_on:
                    pe.wait_ge(s_read, 16 * hb + 16)
                    wait(gb["dve"], f"s{QB - 1}", hb)
                    for b in range(NS):
                        mm = nc.tensor.matmul(aux[:, 2, 2 * b:2 * b + 2], s_in[:, b], kq[:, b], start=True, stop=True)
                    B.done("dx", mm)
                    B.done("dqk", nc.tensor.matmul(aux[:, 2, 2 * NS:3 * NS], ones, sm[:, 0], start=True, stop=True))
                    B.done("dk_turned", nc.tensor.transpose(aux[0:NS, 2, P:2 * P], sm[:, 4], ident))
                weights_product(13)
                level_t(2)
                if g_on:
                    tail_rows(G, it, "k", N_IN_C + 4 * it + 1, 1, 1)
                weights_product(14)
                level_p(3)
                if b_on:
                    wait(gb["dve"], "do", hb)
                    B.done("dv_turned", nc.tensor.transpose(aux[0:NS, 2, 2 * P:3 * P], sm[:, 2], ident))
                weights_product(15)
                level_t(3)
                if b_on:
                    wait(gb["act"], "o_sq", hb)
                    wait(gb["dve"], "d_rows", hb)
                    for b in range(2):
                        mm = nc.tensor.matmul(auxv(1)[:, b], ones, osq[:, b * TH:(b + 1) * TH], start=True, stop=True)
                    B.done("osum", mm)
                weights_product(16)
                level_p(4)
                if b_on:
                    wait(gb["dve"], "dvexp", hb)
                    wait(gb["act"], "o_ln", hb)
                    for b in range(2):
                        mm = nc.tensor.matmul(aux[:, 2 + b], kv_rows[0:NS, 0], dvexp[0:NS, b], start=True, stop=True)
                    B.done("outer", mm)
                weights_product(17)
                level_t(4)
                weights_product(18)
                level_p(5)
                weights_product(19)
                level_t(5)
                if a_on:
                    if b_on:
                        wait(gb["dve"], "s_new", hb)
                    turned("turn_k", 3, cols(kn))
                weights_product(20)
                level_p(6)
                if a_on:
                    wait(ga["act"], "silu_v", ha)
                    turned("turn_v", 2, cols(y[:, 2]))
                weights_product(21)
                level_t(6)
                weights_product(22)
                if a_on:
                    by_chunk("qk", 1, cols(kn), cols(qn))
                weights_product(23)

            turn(0, True, False, False)
            turn(1, True, True, False)
            with pe.Fori(2, GH) as it:
                turn(it, True, True, True)
            turn(GH, False, True, True)
            turn(GH + 1, False, False, True)
            for e in ("dve", "act"):
                pe.wait_ge(gb[e].sem, gb[e].all(GH))
            with pe.Fori(0, KD // 2) as i:
                for s in range(2):
                    product(N_OUT_C + 2 * i + s, s, KD, g_hi, g_lo)
            ffn(3, N_FFN1, FT)
            norm_sum(4)
            Z, fd = fin["pe"], fin["dve"]
            for b in range(QB + 1):
                rows_b = P if b < QB else NS
                pe.wait_ge(fd.sem, fd.at(f"y{KD - 1}") if b < 2 else fd.at(f"y_tok{b - 2}"))
                for m in range(KD):
                    tr = nc.tensor.transpose(acc[0:rows_b, m // 4 + 2 * (b % 2), (m % 4) * P:(m % 4 + 1) * P], y_fin[:, m, b * P:b * P + rows_b], ident)
                Z.done(f"y{b}", tr)

        @block.scalar
        def _(act):
            def convert(n, slot, turn):
                act.wait_ge(w_loaded[slot], 16 * turn + 16)
                if not isinstance(n, int) or n >= 2:
                    act.wait_ge(acc_full, n - 1)
                nc.scalar.activation(w_hi[:, slot], w_raw[:, slot], ACT.Copy).then_inc(w_hi_made, 1)

            def gamma(k, m):
                return column(par, KD * NORM_ROWS[k] + m)

            def norm_tile(k, m, slot, x_sem, x_at):
                if k or not isinstance(m, int) or m >= 2:
                    act.wait_ge(ss_added, KD * k + m - 1)
                act.wait_ge(x_sem, x_at)
                apart(act)
                if k < 4:
                    nc.scalar.activation(h_hi[:, m], xT[:, m], ACT.Copy, scale=gamma(k, m)).then_inc(h_hi_made, 1)
                nc.scalar.activation(sq[:, slot], xT[:, m], ACT.Square).then_inc(sq_made, 1)

            def norm_factor(k):
                nc.scalar.preload_act_table_set("natural_log_exp_and_others")
                act.wait_ge(ss_full, k + 1)
                nc.scalar.activation(halves(rstd), auxv(0), ACT.Ln, bias=eps_col, scale=1.0 / D_MODEL).then_inc(ln_made, 1)
                act.wait_ge(ln_made, k + 1)
                nc.scalar.activation(rstd[:], rstd[:], ACT.Exp, scale=-0.5).then_inc(rstd_made, 1)

            def ffn(k, base, g_base):
                norm_factor(k)
                nc.scalar.preload_act_table_set("silu_and_others")
                for part, kt in enumerate(PARTS):
                    with act.Fori(0, kt) as i:
                        n = base + 2 * i
                        convert(n + 1, 1, base // 2 + i)
                        act.wait_ge(acc_read, n + 1)
                        nc.scalar.activation(gate_s[:], gate_n[:], ACT.Silu).then_inc(silu_made, 1)
                        convert(n + 2, 0, base // 2 + i + 1)
                        act.wait_ge(gu_made, g_base + i + 1)
                        apart(act)
                        nc.scalar.activation(g_hi[:, i], gu[:], ACT.Copy).then_inc(g_hi_made, 1)
                    base += 2 * kt
                    g_base += kt

                    def down(i, last):
                        for s in range(2):
                            n = base + 2 * i + s
                            if not last:
                                convert(n + 1, 1 - s, base // 2 + i + s)
                            if part == 2:
                                norm_tile(k + 1, 2 * i + s, s, acc_read, n + 1)

                    with act.Fori(0, KD // 2 - 1) as i:
                        down(i, False)
                    i = KD // 2 - 1
                    if base + KD < N_ALL:
                        down(i, False)
                    else:
                        convert(base + KD - 1, 1, base // 2 + i)
                        for s in range(2):
                            norm_tile(k + 1, 2 * i + s, s, acc_read, base + 2 * i + s + 1)
                    base += KD

            act.dma_start(const[:], a["const_table"]).then_inc(const_in, 16)
            act.dma_start(par_rows[0:45, 0], a["par_rows"]).then_inc(par_in, 16)
            act.dma_start(par_rows[0:96, 1], a["w_conv_c"][0].rearrange("i (t p) -> (i t) p", p=P)).then_inc(par_in, 16)
            act.dma_start(xs_tok[0:NS, :], a["x_sample"].rearrange("b t d -> (b t) d")).then_inc(xs_in, 16)
            nc.scalar.preload_act_table_set("natural_log_exp_and_others")
            convert(0, 0, 0)
            act.wait_ge(up["dve"].sem, up["dve"].at("par"))
            for m in range(KD):
                norm_tile(0, m, m % 2, up["dve"].sem, up["dve"].at(f"x{m}"))
            norm_factor(0)
            for n in range(16):
                convert(N_IN_A + n + 1, (n + 1) % 2, (n + 1) // 2)

            A, pe_at, dve_at = at["act"], at["pe"], at["dve"]
            for t in range(4):
                act.wait_ge(pe_at.sem, pe_at.at(f"k_turned{t}"))
                if t >= 2:
                    act.wait_ge(k_stored[t % 2], 16)
                A.done(f"k_kept{t}", nc.scalar.activation(k_stage[:, t % 2].rearrange("p b m -> p (b m)"), aux[:, 2 + t % 2], ACT.Copy))
            for h in range(HEADS + 1):
                for b in range(QB):
                    off = P * b * (b + 1) // 2
                    if h < HEADS:
                        act.wait_ge(dve_at.sem, dve_at.at(f"neg{h}{b}"))
                        pr = prob[:, h % 2, off:off + (b + 1) * P]
                        A.done(f"exp{h}{b}", nc.scalar.activation(pr, pr, ACT.Exp, bias=att_col[:, h % 2, 1, b:b + 1],
                                                                 accum_out=att_col[:, h % 2, 2, b:b + 1]))
                    if h and b % 2 == 0:
                        act.wait_ge(pe_at.sem, pe_at.at(f"p_turned{h - 1}{b}"))
                        if b or h > 1:
                            act.wait_ge(pe_at.sem, pe_at.at(f"pv{h - 1}{b - 2}" if b else f"pv{h - 2}2"))
                        A.done(f"pT{h - 1}{b}", nc.scalar.activation(probT[:, 0, 0:(b + 1) * P], aux[:, 2, 0:(b + 1) * P], ACT.Copy))
                if h and h % 2 == 0:
                    t = h // 2 - 1
                    act.wait_ge(pe_at.sem, pe_at.at(f"o_turned{t}"))
                    A.done(f"g_hi{t}", nc.scalar.activation(g_hi[:, t, 0:SEQ], aux[:, 2], ACT.Copy))
            for g in range(4):
                act.wait_ge(pe_at.sem, pe_at.at(f"pooled{g}"))
                A.done(f"pool_hi{g}", nc.scalar.activation(halves(g_hi[:, 4 + g]), auxv(g % 2), ACT.Copy, scale=par[:, 40 + g:41 + g]))
            act.wait_ge(dve_at.sem, dve_at.at("dec_neg"))
            A.done("dec_exp", nc.scalar.activation(dec_p[0:64], dec_p[0:64], ACT.Exp, bias=dec_col[0:64, 1:2], accum_out=dec_col[0:64, 2:3]))
            act.wait_ge(pe_at.sem, pe_at.at("dec_out"))
            for r in range(2):
                rows_r = slice(HD * r, HD * r + HD)
                out = aux[rows_r, 0, 0:64].rearrange("p (t b r) -> p t b r", t=4, r=2)[:, :, :, r]
                A.done(f"dec_hi{r}", nc.scalar.activation(g_hi[rows_r, 0:4, SEQ:T], out, ACT.Copy))
            for n in range(KD):
                convert(N_OUT_A + n + 1, (n + 1) % 2, (N_OUT_A + n + 1) // 2)
                norm_tile(1, n, n % 2, acc_read, N_OUT_A + n + 1)
            ffn(1, N_FFN0, 0)

            R = pre["act"]
            norm_factor(2)
            pre_dve = pre["dve"]
            act.wait_ge(pre["pool"].sem, pre["pool"].at("wab_pad_a"))
            R.done("wab_hi", nc.scalar.activation(wab_hi[:], wab_pad[:], ACT.Copy))
            act.wait_ge(pre_dve.sem, pre_dve.at("ab"))
            R.done("exp_b", nc.scalar.activation(abt[0:8, 0], ab[0:8], ACT.Exp, scale=-1.0))
            act.wait_ge(pre_dve.sem, pre_dve.at("abs"))
            R.done("exp_sp", nc.scalar.activation(abt[32:40, 1], abt[32:40, 1], ACT.Exp))
            act.wait_ge(R.sem, R.at("exp_sp"))
            R.done("ln_sp", nc.scalar.activation(abt[32:40, 1], abt[32:40, 1], ACT.Ln, bias=one_col[32:40]))
            R.done("exp_a", nc.scalar.activation(acol[32:40, 2:3], acol[32:40, 0:1], ACT.Exp))

            G, A, B = gg["act"], ga["act"], gb["act"]

            def turn(it, g_on, a_on, b_on):
                ha, hb = it - 1, it - 2
                n0 = N_IN_C + 4 * it

                def wait(steps, name, h):
                    act.wait_ge(steps.sem, steps.at(name, h))

                def to_t(n, dst="t"):
                    if a_on:
                        wait(ga["pe"], "t_turned" if n == 0 else f"t{n}", ha)
                        A.done("tinv" if n == 0 else f"t{n}", nc.scalar.activation(tinv[:].rearrange("p c m -> p (c m)"), aux[:, 1], ACT.Copy))

                def v_new(c):
                    if b_on:
                        wait(gb["pe"], f"v{c}", hb)
                        if c:
                            wait(gb["pe"], f"s{c - 1}", hb)
                        B.done(f"v{c}", nc.scalar.activation(vnew[:], aux[:, 2, P:2 * P], ACT.Copy))

                def last_tap(stage, name, r, h, zslot, n):
                    act.wait_ge(acc_read, n + 1)
                    apart(act)
                    stage.done(f"tap_{name}", nc.scalar.activation(y[:, r], zc[:, zslot, CONV - 1:], ACT.Copy,
                                                                   scale=column(wconv[:, CONV - 1], r * GH + h)))

                def silu(stage, name, h, out):
                    wait(ga["dve"] if name == "v" else gg["dve"], f"tap_{name}3", h)
                    stage.done(f"silu_{name}", nc.scalar.activation(out, out, ACT.Silu))

                nc.scalar.preload_act_table_set("natural_log_exp_and_others")
                if g_on:
                    convert(n0 + 1, 1, N_IN_C // 2 + 2 * it)
                if a_on:
                    if b_on:
                        wait(ga["pe"], "turn_v", hb)
                        wait(ga["dve"], "dvb", hb)
                    last_tap(A, "v", 2, ha, 0, n0 - 1)
                    wait(ga["pe"], "gc", ha)
                    A.done("gcb", nc.scalar.activation(halves(gcb), auxv(0), ACT.Copy))
                    A.done("egb", nc.scalar.activation(halves(egb), auxv(0), ACT.Exp))
                v_new(0)
                if a_on:
                    wait(gg["act"], "silu_k", ha)
                    A.done("sq_q", nc.scalar.activation(sqg[:, 0], y[:, 0], ACT.Square))
                    A.done("sq_k", nc.scalar.activation(sqg[:, 1], y[:, 1], ACT.Square))
                    for r, name in enumerate("qk"):
                        wait(ga["pe"], f"ss_{name}", ha)
                        A.done(f"ln_{name}", nc.scalar.activation(halves(rqk[:, r]), auxv(0), ACT.Ln, bias=eps_col))
                        wait(A, f"ln_{name}", ha)
                        A.done(f"rs_{name}", nc.scalar.activation(rqk[:, r], rqk[:, r], ACT.Exp, scale=-0.5, **({"bias": lnq_col} if r == 0 else {})))
                        if r == 0:
                            v_new(1)
                    wait(ga["pool"], "mask", ha)
                    A.done("decay", nc.scalar.activation(decay[:], decay[:], ACT.Exp))
                    wait(ga["dve"], "edk", ha)
                    A.done("edk", nc.scalar.activation(edk[:], edk[:], ACT.Exp))
                else:
                    v_new(1)
                v_new(2)
                if g_on:
                    convert(n0 + 2, 0, N_IN_C // 2 + 2 * it + 1)
                    if a_on:
                        wait(ga["dve"], "qn", ha)
                    last_tap(G, "q", 0, it, 0, n0)
                to_t(0)
                v_new(3)
                to_t(1)
                if b_on:
                    wait(gb["pe"], f"o{QB - 1}", hb)
                    B.done("oT", nc.scalar.activation(yo[:, 0:SEQ], aux[:, 3], ACT.Copy))
                if g_on:
                    convert(n0 + 3, 1, N_IN_C // 2 + 2 * it + 1)
                    if a_on:
                        wait(ga["dve"], "kn", ha)
                    last_tap(G, "k", 1, it, 1, n0 + 1)
                to_t(2)
                if b_on:
                    wait(B, "oT", hb)
                    wait(gb["dve"], "do", hb)
                    B.done("o_sq", nc.scalar.activation(osq[:], yo[:], ACT.Square))
                to_t(3)
                if b_on:
                    wait(gb["pe"], "osum", hb)
                    B.done("o_ln", nc.scalar.activation(halves(ors), auxv(1), ACT.Ln, bias=eps_col, scale=1.0 / P))
                    wait(B, "o_ln", hb)
                    B.done("o_rs", nc.scalar.activation(ors[:], ors[:], ACT.Exp, scale=-0.5))
                to_t(4)
                nc.scalar.preload_act_table_set("silu_and_others")
                if a_on:
                    wait(ga["dve"], "kbg", ha)
                    if b_on:
                        wait(gb["pe"], "dx", hb)
                    A.done("kq_k", nc.scalar.activation(kq[:, :, 0], kbg[:, SEQ:T], ACT.Copy))
                    A.done("kq_q", nc.scalar.activation(kq[:, :, 1], qg[:, SEQ:T], ACT.Copy))
                    silu(A, "v", ha, y[:, 2])
                if g_on:
                    silu(G, "q", it, y[:, 0])
                    silu(G, "k", it, y[:, 1])
                to_t(5)
                if g_on:
                    convert(n0 + 4, 0, N_IN_C // 2 + 2 * it + 2)
                if b_on:
                    wait(gb["dve"], "og", hb)
                    apart(act)
                    B.done("g_hi", nc.scalar.activation(g_hi[:, hb], yo[:], ACT.Copy))
                if g_on:
                    act.wait_ge(acc_read, n0 + 3)
                    apart(act)
                    G.done("silu_g", nc.scalar.activation(gateT[:, it], gateT[:, it], ACT.Silu))

            turn(0, True, False, False)
            turn(1, True, True, False)
            with act.Fori(2, GH) as it:
                turn(it, True, True, True)
            turn(GH, False, True, True)
            turn(GH + 1, False, False, True)
            with act.Fori(0, KD // 2) as i:
                for s in range(2):
                    n = N_OUT_C + 2 * i + s
                    convert(n + 1, 1 - s, N_OUT_C // 2 + i + s)
                    norm_tile(3, 2 * i + s, s, acc_read, n + 1)
            ffn(3, N_FFN1, FT)
            norm_factor(4)

        @block.vector
        def _(dve):
            def convert(n, slot):
                dve.wait_ge(w_hi_made, n + 1)
                nc.vector.tensor_tensor(w_lo[:, slot], w_raw[:, slot], w_hi[:, slot].bitcast(F32), ALU.subtract).then_inc(w_lo_made, 1)

            def norm_tile(k, m, x_sem=None, x_at=None):
                if k == 4:
                    return
                dve.wait_ge(h_hi_made, KD * k + m + 1)
                nc.vector.scalar_tensor_tensor(h_lo[:, m], xT[:, m], column(par, KD * NORM_ROWS[k] + m), h_hi[:, m].bitcast(F32),
                                               ALU.mult, ALU.subtract).then_inc(h_lo_made, 1)

            def add_to_stream(n, m, slot):
                dve.wait_ge(acc_full, n + 1)
                nc.vector.tensor_tensor(halves(xT[:, m]), accv(slot), halves(xT[:, m]), ALU.add).then_inc(acc_read, 1)

            def scaled(out, n, slot):
                dve.wait_ge(acc_full, n + 1)
                nc.vector.tensor_tensor(halves(out), accv(slot), halves(rstd), ALU.mult).then_inc(acc_read, 1)

            def ffn(k, base, g_base):
                dve.wait_ge(rstd_made, k + 1)
                for part, kt in enumerate(PARTS):
                    with dve.Fori(0, kt) as i:
                        n, g = base + 2 * i, g_base + i
                        convert(n + 1, 1)
                        scaled(gate_n, n, 0)
                        convert(n + 2, 0)
                        scaled(up_n, n + 1, 1)
                        dve.wait_ge(silu_made, g + 1)
                        dve.wait_ge(acc_read, n + 2)
                        nc.vector.tensor_tensor(gu[:], up_n[:], gate_s[:], ALU.mult).then_inc(gu_made, 1)
                        dve.wait_ge(g_hi_made, g + 1)
                        nc.vector.tensor_tensor(g_lo[:, i], gu[:], g_hi[:, i].bitcast(F32), ALU.subtract).then_inc(g_lo_made, 1)
                    base += 2 * kt
                    g_base += kt
                    with dve.Fori(0, KD // 2 - 1) as i:
                        for s in range(2):
                            convert(base + 2 * i + s + 1, 1 - s)
                            add_to_stream(base + 2 * i + s, 2 * i + s, s)
                            if part == 2:
                                norm_tile(k + 1, 2 * i + s)
                    i = KD // 2 - 1
                    for s in range(2):
                        if base + 2 * i + s + 1 < N_ALL:
                            convert(base + 2 * i + s + 1, 1 - s)
                        add_to_stream(base + 2 * i + s, 2 * i + s, s)
                        if part == 2:
                            norm_tile(k + 1, 2 * i + s)
                    base += KD

            U, upe = up["dve"], up["pe"]
            dve.wait_ge(upe.sem, upe.at("par"))
            U.done("par", nc.vector.tensor_copy(par[:, 0:45], aux[:, 3, 0:45]))
            U.done("wconv", nc.vector.tensor_copy(wconv[:].rearrange("p i t -> p (i t)"), aux[:, 3, 64:160]))
            dve.wait_ge(upe.sem, upe.at("xs"))
            U.done("xs", nc.vector.tensor_copy(xT[:, :, SEQ:T], aux[:, 2, 0:64].rearrange("p (m t) -> p m t", t=NS)))
            for m in range(KD):
                dve.wait_ge(upe.sem, upe.at(f"x{m}"))
                U.done(f"x{m}", nc.vector.tensor_copy(xT[:, m, 0:SEQ], aux[:, m % 2]))
            dve.wait_ge(U.sem, U.all())
            convert(0, 0)
            for m in range(KD):
                norm_tile(0, m)
            dve.wait_ge(rstd_made, 1)
            for n in range(16):
                convert(N_IN_A + n + 1, (n + 1) % 2)
                scaled(zT[:, IN_A_TILES[n]], N_IN_A + n, n % 2)

            A, pe_at, act_at, pool_at = at["dve"], at["pe"], at["act"], at["pool"]
            for t in range(4):
                dve.wait_ge(pe_at.sem, pe_at.at(f"v_turned{t}"))
                A.done(f"v_kept{t}", nc.vector.tensor_copy(v_tok[:, :, t * P:(t + 1) * P], blocks(aux[:, t % 2])))
            dve.wait_ge(pe_at.sem, pe_at.at("u_turned"))
            A.done("u_kept", nc.vector.tensor_copy(u_tok[0:23], aux[0:23, 0]))
            dve.wait_ge(pe_at.sem, pe_at.at("z_turned"))
            A.done("z_kept", nc.vector.tensor_copy(z_tok[0:NS], aux[0:NS, 1:4]))
            dve.wait_ge(tab_in, 16)
            for h in range(HEADS + 1):
                if h < HEADS:
                    if h:
                        dve.wait_ge(A.sem, A.at(f"max{h - 1}3"))
                    A.done(f"bias{h}", nc.vector.scalar_tensor_tensor(bias[:], att_tab[:, 0], -8.0 * slope(h), att_tab[:, 1], ALU.mult, ALU.add))
                    dve.wait_ge(A.sem, A.at(f"bias{h}"))
                for b in range(QB):
                    off = P * b * (b + 1) // 2
                    if h < HEADS:
                        dve.wait_ge(pe_at.sem, pe_at.at(f"scores{h}{b}"))
                        if h >= 2:
                            dve.wait_ge(pe_at.sem, pe_at.at(f"p_turned{h - 2}{b}"))
                        A.done(f"max{h}{b}", nc.vector.tensor_tensor_reduce(
                            out=prob[:, h % 2, off:off + (b + 1) * P], in0=aux[:, b % 2, 0:(b + 1) * P],
                            in1=bias[:, (3 - b) * P:SEQ], scale=0.125, scalar=NEG, op0=ALU.add, op1=ALU.max,
                            accum_out=att_col[:, h % 2, 0, b:b + 1]))
                        dve.wait_ge(A.sem, A.at(f"max{h}{b}"))
                        A.done(f"neg{h}{b}", nc.vector.tensor_scalar(att_col[:, h % 2, 1, b:b + 1], att_col[:, h % 2, 0, b:b + 1], -1.0, None, ALU.mult))
                    if h and b % 2:
                        dve.wait_ge(pe_at.sem, pe_at.at(f"p_turned{h - 1}{b}"))
                        if b == 3 or h > 1:
                            dve.wait_ge(pe_at.sem, pe_at.at(f"pv{h - 1}1" if b == 3 else f"pv{h - 2}3"))
                        A.done(f"pT{h - 1}{b}", nc.vector.tensor_copy(probT[:, 1, 0:(b + 1) * P], aux[:, 2, 0:(b + 1) * P]))
                if h:
                    hp, par_h = h - 1, (h - 1) % 2
                    dve.wait_ge(act_at.sem, act_at.at(f"exp{hp}3"))
                    A.done(f"inv{hp}", nc.vector.reciprocal(att_col[:, par_h, 3], att_col[:, par_h, 2]))
                    dve.wait_ge(A.sem, A.at(f"inv{hp}"))
                    dve.wait_ge(pe_at.sem, pe_at.at(f"pv{hp}3"))
                    if hp % 2 == 0 and hp:
                        dve.wait_ge(pe_at.sem, pe_at.at(f"o_turned{hp // 2 - 1}"))
                    A.done(f"o{hp}", nc.vector.tensor_tensor(
                        o_tok[:, :, HD * par_h:HD * par_h + HD], aux[:, 3, 0:QB * HD].rearrange("p (b d) -> p b d", d=HD),
                        att_col[:, par_h, 3].unsqueeze(2).to_broadcast([P, QB, HD]), ALU.mult))
                    if h % 2 == 0:
                        t = h // 2 - 1
                        dve.wait_ge(act_at.sem, act_at.at(f"g_hi{t}"))
                        A.done(f"g_lo{t}", nc.vector.tensor_tensor(g_lo[:, t, 0:SEQ], aux[:, 2], g_hi[:, t, 0:SEQ].bitcast(F32), ALU.subtract))
            dve.wait_ge(pe_at.sem, pe_at.at("hist_turned"))
            A.done("histT", nc.vector.tensor_copy(histT[:].rearrange("p g b j -> p (g b j)"), aux[:, 3, 0:480]))
            dve.wait_ge(A.sem, A.at("histT"))
            for g, w in enumerate(POOL_WINDOWS):
                A.done(f"tail{g}", nc.vector.tensor_reduce(tail[:], histT[:, g, :, POOL_HIST - (w - 1):POOL_HIST], AX.X, ALU.add))
                dve.wait_ge(A.sem, A.at(f"tail{g}"))
                A.done(f"tail_sum{g}", nc.vector.tensor_tensor(tail[:], tail[:], zT[:, 12 + g, SEQ:T], ALU.add))
                dve.wait_ge(A.sem, A.at(f"tail_sum{g}"))
                if g >= 2:
                    dve.wait_ge(pe_at.sem, pe_at.at(f"pooled{g - 2}"))
                A.done(f"tail_p{g}", nc.vector.scalar_tensor_tensor(pooled[:, g % 2, SEQ:T], tail[:], 1.0 / w, zT[:, 12 + g, SEQ:T], ALU.mult, ALU.subtract))
                dve.wait_ge(A.sem, A.at(f"tail_p{g}"))
            for g in range(4):
                dve.wait_ge(act_at.sem, act_at.at(f"pool_hi{g}"))
                A.done(f"pool_lo{g}", nc.vector.scalar_tensor_tensor(halves(g_lo[:, 4 + g]), auxv(g % 2), par[:, 40 + g:41 + g],
                                                                    halves(g_hi[:, 4 + g].bitcast(F32)), ALU.mult, ALU.subtract))
            for b in range(NS):
                dve.wait_ge(pe_at.sem, pe_at.at(f"q_spread{b}"))
                if b == 0:
                    dve.wait_ge(ck_in, 32)
                    dve.wait_ge(self_in, 64)
                if b == 4:
                    dve.wait_ge(ck2_in, 32)
                    dve.wait_ge(self2_in, 64)
                ext = (P, KEYS_B + 1)
                for x in range(2):
                    if b:
                        dve.wait_ge(A.sem, A.at(f"sum_{'ab'[x]}{b - 1}"))
                    A.done(f"prod_{'ab'[x]}{b}", nc.vector.tensor_tensor(prod[0:ext[x], x], aux[0:ext[x], b % 2], ck[0:ext[x], b % 4, x], ALU.mult))
                for x in range(2):
                    dve.wait_ge(A.sem, A.at(f"prod_{'ab'[x]}{b}"))
                    A.done(f"sum_{'ab'[x]}{b}", nc.vector.tensor_reduce(
                        dec_s[0:ext[x], x, b * HEADS:(b + 1) * HEADS], prod[0:ext[x], x].rearrange("p (h d) -> p h d", d=HD), AX.X, ALU.add))
            dve.wait_ge(pe_at.sem, pe_at.at("s_turned"))
            dve.wait_ge(sel_in, 32)
            A.done("dec_max", nc.vector.tensor_tensor_reduce(out=dec_p[0:64], in0=aux[0:64, 2, 0:KEYS], in1=dec_tab[0:64], scale=0.125, scalar=NEG,
                                                             op0=ALU.add, op1=ALU.max, accum_out=dec_col[0:64, 0:1]))
            dve.wait_ge(A.sem, A.at("dec_max"))
            A.done("dec_neg", nc.vector.tensor_scalar(dec_col[0:64, 1:2], dec_col[0:64, 0:1], -1.0, None, ALU.mult))
            dve.wait_ge(act_at.sem, act_at.at("dec_exp"))
            A.done("dec_inv", nc.vector.reciprocal(dec_col[0:64, 3:4], dec_col[0:64, 2:3]))
            dve.wait_ge(A.sem, A.at("dec_inv"))
            A.done("dec_norm", nc.vector.tensor_scalar(dec_p[0:64], dec_p[0:64], dec_col[0:64, 3:4], None, ALU.mult))
            dve.wait_ge(pe_at.sem, pe_at.at("dp_turned"))
            nc.vector.tensor_copy(dec_pT[:, 0], aux[:, 3, 0:64])
            A.done("dec_pT", nc.vector.tensor_copy(dec_pT[0:KEYS_B + 1, 1], aux[0:KEYS_B + 1, 3, 64:128]))
            for r in range(2):
                rows_r = slice(HD * r, HD * r + HD)
                out = aux[rows_r, 0, 0:64].rearrange("p (t b r) -> p t b r", t=4, r=2)[:, :, :, r]
                dve.wait_ge(act_at.sem, act_at.at(f"dec_hi{r}"))
                A.done(f"dec_lo{r}", nc.vector.tensor_tensor(g_lo[rows_r, 0:4, SEQ:T], out, g_hi[rows_r, 0:4, SEQ:T].bitcast(F32), ALU.subtract))
            for n in range(KD):
                convert(N_OUT_A + n + 1, (n + 1) % 2)
                add_to_stream(N_OUT_A + n, n, n % 2)
                norm_tile(1, n)
            ffn(1, N_FFN0, 0)

            R, ppe, pact, ppool = pre["dve"], pre["pe"], pre["act"], pre["pool"]

            def own(steps, name, turn=0):
                dve.wait_ge(steps.sem, steps.at(name, turn))

            dve.wait_ge(rstd_made, 3)
            own(pact, "wab_hi")
            R.done("wab_lo", nc.vector.tensor_tensor(wab_lo[:], wab_pad[:], wab_hi[:].bitcast(F32), ALU.subtract))
            for half in range(2):
                own(ppe, f"chist{half}")
                R.done(f"chist{half}", nc.vector.tensor_copy(chist[:, 12 * half:12 * half + 12].rearrange("p t b i -> p (t b i)"), aux[:, half, 0:288]))
            own(R, "chist1")
            for i in range(CONV - 1):
                dst = cprod if i == 0 else ctmp
                if i == 2:
                    own(R, "sum1")
                R.done(f"prod{i}", nc.vector.tensor_tensor(dst[:], chist[:, :, :, i], wconv[:, i].unsqueeze(2).to_broadcast([P, 3 * GH, NS]), ALU.mult))
                if i:
                    own(R, f"prod{i}")
                    R.done(f"sum{i}", nc.vector.tensor_tensor(cprod[:], cprod[:], ctmp[:], ALU.add))
            own(ppe, "ab")
            R.done("ab", nc.vector.tensor_tensor(halves(ab[0:64]), aux[0:64, 2:4, 0:TH], halves(rstd[0:64]), ALU.mult))
            own(pact, "exp_b")
            R.done("beta1", nc.vector.tensor_scalar(abt[0:8, 0], abt[0:8, 0], 1.0, None, ALU.add))
            own(R, "beta1")
            own(ppool, "rows_zero")
            R.done("beta", nc.vector.reciprocal(rows[0:8], abt[0:8, 0]))
            dve.wait_ge(acol_in, 32)
            R.done("dt", nc.vector.tensor_scalar(abt[32:40, 0], ab[32:40], acol[32:40, 1:2], None, ALU.add))
            own(R, "dt")
            R.done("abs", nc.vector.scalar_tensor_tensor(abt[32:40, 1], abt[32:40, 0], -1.0, abt[32:40, 0], ALU.mult, ALU.min))
            own(pact, "ln_sp")
            R.done("sp", nc.vector.scalar_tensor_tensor(abt[32:40, 2], abt[32:40, 0], 0.0, abt[32:40, 1], ALU.max, ALU.add))
            own(pact, "exp_a")
            R.done("nega", nc.vector.tensor_scalar(acol[32:40, 3:4], acol[32:40, 2:3], -1.0, None, ALU.mult))
            own(R, "nega")
            R.done("g", nc.vector.tensor_scalar(abt[32:40, 0], abt[32:40, 2], acol[32:40, 3:4], None, ALU.mult))
            own(R, "g")
            R.done("cum", nc.vector.tensor_tensor_scan(rows[32:40], delta[32:40, G_KEEP:G_KEEP + T], abt[32:40, 0], 0.0, ALU.mult, ALU.add))
            own(ppe, "rows_turned")
            R.done("tokcols", nc.vector.tensor_copy(tokcols[:].rearrange("p c m -> p (c m)"), aux[:, 0, 0:256]))

            G, A, B = gg["dve"], ga["dve"], gb["dve"]
            identity = ident.unsqueeze(1).to_broadcast([P, QB, P])

            def turn(it, g_on, a_on, b_on):
                ha, hb = it - 1, it - 2
                n0 = N_IN_C + 4 * it

                def wait(steps, name, h):
                    dve.wait_ge(steps.sem, steps.at(name, h))

                def chunk_col(row):
                    return tokcols[:, :, bass.ds(row + ha, 1)].to_broadcast([P, QB, P])

                def chunks(x):
                    return x[:, 0:SEQ].rearrange("p (c m) -> p c m", m=P)

                def conv(stage, name, r, h, zslot):
                    wait(ga["act"] if name == "v" else gg["act"], f"tap_{name}", h)
                    for i in range(CONV - 1):
                        stage.done(f"tap_{name}{i}", nc.vector.scalar_tensor_tensor(
                            y[:, r, 0:SEQ], zc[:, zslot, i:i + SEQ], column(wconv[:, i], r * GH + h), y[:, r, 0:SEQ], ALU.mult, ALU.add))
                        wait(stage, f"tap_{name}{i}", h)
                    stage.done(f"tap_{name}3", nc.vector.tensor_tensor(y[:, r, SEQ:T], y[:, r, SEQ:T], cprod[:, r * GH + h], ALU.add))

                def rows_out(stage, name, r, h, slot):
                    wait(ga["pe"] if name == "v" else gg["pe"], f"tail_{name}", h)
                    stage.done(f"z_{name}", nc.vector.tensor_copy(z_rows[0:11, r], acc[0:11, 2 * slot, TH:TH + P]))

                def one_plus_p(n):
                    if a_on:
                        wait(ga["pe"], f"p{n}", ha)
                        A.done(f"ip{n}", nc.vector.tensor_tensor(ip[:], blocks(aux[:, 0]), identity, ALU.add))

                def to_tT(n):
                    if a_on:
                        wait(ga["pe"], f"u{n}", ha)
                        A.done(f"u{n}", nc.vector.tensor_copy((t_all if n == NL - 1 else tinvT)[:].rearrange("p c m -> p (c m)"), aux[:, 0]))

                def new_state(c):
                    if not b_on:
                        return
                    wait(gb["pe"], f"s{c}", hb)
                    if c == 0:
                        B.done("s0", nc.vector.tensor_copy(state[:], aux[:, 2, 2 * P:3 * P]))
                    else:
                        wait(B, f"s{c - 1}", hb)
                        B.done(f"s{c}", nc.vector.scalar_tensor_tensor(state[:], state[:], sm[:, 6, c:c + 1], aux[:, 2, 2 * P:3 * P], ALU.mult, ALU.add))

                def residue(c):
                    if b_on:
                        wait(gb["pe"], f"ks{c}", hb)
                        B.done(f"r{c}", nc.vector.tensor_tensor(resid[:], vb[:, c], aux[:, 2, 0:P], ALU.subtract))

                if g_on:
                    convert(n0 + 1, 1)
                if a_on:
                    wait(gg["pe"], "tail_q", ha)
                    wait(gg["act"], "tap_q", ha)
                    scaled(zc[:, 0, CONV - 1:], n0 - 1, 1)
                new_state(0)
                if a_on:
                    conv(A, "v", 2, ha, 0)
                    wait(ga["pe"], "beta", ha)
                    A.done("betab", nc.vector.tensor_copy(halves(betab), auxv(0)))
                residue(1)
                if a_on:
                    rows_out(A, "v", 2, ha, 1)
                    wait(ga["act"], "gcb", ha)
                    A.done("diff", nc.vector.tensor_tensor(decay[:], chunks(gcb), chunk_col(32), ALU.subtract))
                    A.done("edk", nc.vector.tensor_tensor(edk[:], chunks(gcb)[:, :, P - 1], tokcols[:, :, bass.ds(32 + ha, 1)].rearrange("p c m -> p (c m)"), ALU.subtract))
                new_state(1)
                if a_on:
                    wait(ga["act"], "rs_q", ha)
                    A.done("qn", nc.vector.tensor_tensor(qn[:], y[:, 0], rqk[:, 0], ALU.mult))
                    wait(ga["act"], "rs_k", ha)
                    A.done("kn", nc.vector.tensor_tensor(kn[:], y[:, 1], rqk[:, 1], ALU.mult))
                residue(2)
                if a_on:
                    wait(ga["act"], "decay", ha)
                    A.done("bdecay", nc.vector.scalar_tensor_tensor(bdecay[:].rearrange("p c m -> p (c m)"), betab[:, 0:SEQ], -1.0,
                                                                    decay[:].rearrange("p c m -> p (c m)"), ALU.mult, ALU.mult))
                if g_on:
                    if a_on:
                        wait(ga["pe"], "tail_v", ha)
                    scaled(zc[:, 0, CONV - 1:], n0, 0)
                if a_on:
                    wait(A, "bdecay", ha)
                    wait(ga["pe"], "kk", ha)
                    A.done("low", nc.vector.tensor_tensor(lowT[:], blocks(aux[:, 0]), bdecay[:], ALU.mult))
                new_state(2)
                if g_on:
                    convert(n0 + 2, 0)
                if a_on:
                    wait(ga["pool"], "lev0", ha)
                    A.done("one", nc.vector.tensor_tensor(tinvT[:], lev[:, 0], identity, ALU.add))
                residue(3)
                if g_on:
                    if a_on:
                        dve.wait_ge(zr_stored, 32 * it)
                    rows_out(G, "q", 0, it, 0)
                    conv(G, "q", 0, it, 0)
                one_plus_p(1)
                new_state(3)
                to_tT(1)
                one_plus_p(2)
                if g_on:
                    scaled(zc[:, 1, CONV - 1:], n0 + 1, 1)
                to_tT(2)
                if g_on:
                    convert(n0 + 3, 1)
                if b_on:
                    wait(gb["pe"], "dk_turned", hb)
                    sx = aux[:, 2, 0:2 * NS].rearrange("p (b r) -> p b r", r=2)
                    B.done("dv", nc.vector.tensor_tensor(sm[:, 2], sm[:, 1], sx[:, :, 0], ALU.subtract))
                    wait(B, "dv", hb)
                    B.done("dqk", nc.vector.tensor_tensor(sm[:, 3], sm[:, 2], aux[:, 2, 2 * NS:3 * NS], ALU.mult))
                    wait(B, "dqk", hb)
                    B.done("do", nc.vector.tensor_tensor(yo[:, SEQ:T], sm[:, 3], sx[:, :, 1], ALU.add))
                if a_on:
                    A.done("qg", nc.vector.tensor_tensor(qg[:], qn[:], egb[:], ALU.mult))
                    A.done("kb", nc.vector.tensor_tensor(kbg[:], kn[:], betab[:], ALU.mult))
                    wait(A, "kb", ha)
                    A.done("kbg", nc.vector.tensor_tensor(kbg[:], kbg[:], egb[:], ALU.mult))
                one_plus_p(3)
                if b_on:
                    wait(gb["pe"], "dv_turned", hb)
                    B.done("d_rows", nc.vector.tensor_copy(kv_rows[0:NS].rearrange("p r m -> p (r m)"), aux[0:NS, 2, P:3 * P]))
                    wait(B, "d_rows", hb)
                    B.done("dvexp", nc.vector.tensor_tensor(dvexp[0:NS].rearrange("p a (c m) -> p (a c) m", m=P), kv_rows[0:NS, 1].unsqueeze(1).to_broadcast([NS, NS, P]),
                                                            ident[0:NS, 0:NS].unsqueeze(2).to_broadcast([NS, NS, P]), ALU.mult))
                to_tT(3)
                if g_on:
                    rows_out(G, "k", 1, it, 1)
                    conv(G, "k", 1, it, 1)
                one_plus_p(4)
                to_tT(4)
                if b_on:
                    wait(gb["pe"], "outer", hb)
                    wait(gb["pool"], "s_decayed", hb)
                    B.done("s_new", nc.vector.tensor_tensor(s_in[:].rearrange("p b m -> p (b m)"), s_in[:].rearrange("p b m -> p (b m)"),
                                                            aux[:, 2:4].rearrange("p a t -> p (a t)"), ALU.add))
                one_plus_p(5)
                to_tT(5)
                if b_on:
                    wait(gb["act"], "o_rs", hb)
                    B.done("on", nc.vector.scalar_tensor_tensor(yo[:], yo[:], par[:, 44:45], ors[:], ALU.mult, ALU.mult))
                    wait(B, "on", hb)
                    B.done("og", nc.vector.tensor_tensor(yo[:], yo[:], gateT[:, hb], ALU.mult))
                if a_on:
                    wait(ga["pe"], "turn_k", ha)
                    wait(ga["act"], "edk", ha)
                    A.done("kdec", nc.vector.tensor_tensor(kdec[:], blocks(aux[:, 3]), edk[:].unsqueeze(2).to_broadcast([P, QB, P]), ALU.mult))
                    A.done("dkq", nc.vector.tensor_tensor(sm[:, 0], qn[:, SEQ:T], kn[:, SEQ:T], ALU.mult))
                    wait(ga["act"], "silu_v", ha)
                    A.done("dvb", nc.vector.tensor_tensor(sm[:, 1], y[:, 2, SEQ:T], betab[:, SEQ:T], ALU.mult))
                    A.done("keep_k", nc.vector.tensor_copy(sm[:, 4], kn[:, SEQ:T]))
                    A.done("keep_e", nc.vector.tensor_copy(sm[:, 5], egb[:, SEQ:T]))
                    A.done("keep_c", nc.vector.tensor_copy(sm[:, 6, 0:QB], chunks(egb)[:, :, P - 1]))
                one_plus_p(6)
                if g_on:
                    scaled(gateT[:, it], n0 + 2, 0)
                if a_on:
                    wait(ga["pe"], "turn_v", ha)
                    A.done("vb", nc.vector.tensor_tensor(vb[:], blocks(aux[:, 2]), chunk_col(0), ALU.mult))
                to_tT(6)
                if g_on:
                    convert(n0 + 4, 0)
                if a_on:
                    wait(ga["pe"], "qk", ha)
                    A.done("attT", nc.vector.tensor_tensor(attT[:], blocks(aux[:, 1]), decay[:], ALU.mult))
                if b_on:
                    wait(gb["act"], "g_hi", hb)
                    B.done("g_lo", nc.vector.tensor_tensor(g_lo[:, hb], yo[:], g_hi[:, hb].bitcast(F32), ALU.subtract))
                    dve.wait_ge(st_stored, 16 * (it - 1))

            turn(0, True, False, False)
            turn(1, True, True, False)
            with dve.Fori(2, GH) as it:
                turn(it, True, True, True)
            turn(GH, False, True, True)
            turn(GH + 1, False, False, True)
            with dve.Fori(0, KD // 2) as i:
                for s in range(2):
                    convert(N_OUT_C + 2 * i + s + 1, 1 - s)
                    add_to_stream(N_OUT_C + 2 * i + s, 2 * i + s, s)
                    norm_tile(3, 2 * i + s)
            ffn(3, N_FFN1, FT)

            Z, pf = fin["dve"], fin["pe"]
            dve.wait_ge(rstd_made, 5)
            dve.wait_ge(acc_read, N_ALL)
            for m in range(KD):
                Z.done(f"y{m}", nc.vector.scalar_tensor_tensor(y_fin[:, m], xT[:, m], par[:, 4 * KD + m:4 * KD + m + 1], rstd[:], ALU.mult, ALU.mult))
            for b in range(QB + 1):
                rows_b = P if b < QB else NS
                dve.wait_ge(pf.sem, pf.at(f"y{b}"))
                Z.done(f"y_tok{b}", nc.vector.tensor_copy(y_tok[0:rows_b, b], acc[0:rows_b, 2 * (b % 2):2 * (b % 2) + 2].rearrange("p a t -> p (a t)")))

        @block.gpsimd
        def _(pool):
            def add_squares(k):
                if k:
                    pool.wait_ge(ss_full, k)
                nc.gpsimd.memset(ssum[:], 0.0).then_inc(ss_clear, 1)
                pool.wait_ge(ss_clear, k + 1)

                def add(i):
                    for s in range(2):
                        before = KD * k + 2 * i + s
                        pool.wait_ge(sq_made, before + 1)
                        if k or s or not isinstance(i, int):
                            pool.wait_ge(ss_added, before)
                        nc.gpsimd.tensor_tensor(ssum[:], ssum[:], sq[:, s], ALU.add).then_inc(ss_added, 1)

                add(0)
                with pool.Fori(1, KD // 2) as i:
                    add(i)

            add_squares(0)
            A, up_dve, pe_at, dve_at, act_at = at["pool"], up["dve"], at["pe"], at["dve"], at["act"]
            pool.wait_ge(up_dve.sem, up_dve.all())
            pool.wait_ge(up["pe"].sem, up["pe"].all())
            pool.dma_start(att_tab[:], a["attention_table"].rearrange("p (r c) -> p r c", r=2)).then_inc(tab_in, 16)
            pool.dma_start(hist_rows[0:120], a["state_pool"][0].rearrange("b j c -> (b j) c")).then_inc(hist_in, 16)
            pool.dma_start(sel8[0:NS], a["select_table"].rearrange("b (c m) -> b c m", m=P)).then_inc(sel_in, 16)
            pool.dma_start(dec_tab[0:64], a["decode_table"]).then_inc(sel_in, 16)
            for t in range(4):
                pool.wait_ge(act_at.sem, act_at.at(f"k_kept{t}"))
                pool.dma_start(o["a_k_prompt"][0, 0].rearrange("(b p) h d -> p b (h d)", p=P)[:, :, t * P:(t + 1) * P],
                               k_stage[:, t % 2]).then_inc(k_stored[t % 2], 16)
            pool.wait_ge(dve_at.sem, dve_at.at("v_kept3"))
            pool.dma_start(o["a_v_prompt"][0, 0].rearrange("(b p) h d -> p b (h d)", p=P), v_tok[:]).then_inc(stored, 16)
            pool.wait_ge(dve_at.sem, dve_at.at("z_kept"))
            pool.dma_start(o["pool_prompt"][0, 0], u_tok[0:POOL_HIST]).then_inc(stored, 16)
            pool.dma_start(o["pool_sample"][0, :, POOL_HIST - 1, :], u_tok[POOL_HIST:POOL_HIST + NS]).then_inc(stored, 16)
            pool.dma_start(o["a_k_sample"][0].rearrange("b t h d -> b t (h d)")[:, PAST], z_tok[0:NS, 1]).then_inc(stored, 16)
            pool.dma_start(o["a_v_sample"][0].rearrange("b t h d -> b t (h d)")[:, PAST], z_tok[0:NS, 2]).then_inc(stored, 16)
            pool.wait_ge(dve_at.sem, dve_at.at("g_lo3"))
            pool.dma_start(cnt[:], a["pool_table"].rearrange("p (g t) -> p g t", g=4)).then_inc(pool_in, 16)
            pool.dma_start(wpool[:], a["w_pool"][0].rearrange("g c d -> c g d")).then_inc(pool_in, 16)
            pool.wait_ge(pool_in, 32)
            for g in range(4):
                src = zT[:, 12 + g]
                for n in range(g + 1):
                    dst, s = run[:, n % 2], 1 << n
                    A.done(f"run{g}{n}a", nc.gpsimd.tensor_tensor(dst[:, s:SEQ], src[:, s:SEQ], src[:, 0:SEQ - s], ALU.add))
                    A.done(f"run{g}{n}b", nc.gpsimd.tensor_copy(dst[:, 0:s], src[:, 0:s]))
                    pool.wait_ge(A.sem, A.at(f"run{g}{n}b"))
                    src = dst
                mean = run[:, (g + 1) % 2]
                A.done(f"mean{g}", nc.gpsimd.tensor_tensor(mean[:, 0:SEQ], src[:, 0:SEQ], cnt[:, g, 0:SEQ], ALU.mult))
                pool.wait_ge(A.sem, A.at(f"mean{g}"))
                if g >= 2:
                    pool.wait_ge(pe_at.sem, pe_at.at(f"pooled{g - 2}"))
                A.done(f"pool{g}", nc.gpsimd.tensor_tensor(pooled[:, g % 2, 0:SEQ], mean[:, 0:SEQ], zT[:, 12 + g, 0:SEQ], ALU.subtract))
                pool.wait_ge(A.sem, A.at(f"pool{g}"))
            add_squares(1)
            R = pre["pool"]
            pool.wait_ge(acc_full, N_OUT_A + 1)
            for q in range(2):
                pool.wait_ge(k_stored[q], 32)
            pool.wait_ge(stored, 16 * 5)
            pool.dma_start(delta[:], a["delta_table"]).then_inc(delta_in, 16)
            pool.dma_start(crow[0:3 * NS], a["state_conv"][0].rearrange("b i c -> (b i) c")).then_inc(crow_in, 16)
            pool.dma_start(wab_raw[:], w_in_c[:, 4 * QK:].rearrange("(k p) m -> p k m", p=P)).then_inc(wab_in, 16)
            pool.dma_start(acol[32:40, 0:1], a["a_log_c"].rearrange("o h -> h o")).then_inc(acol_in, 16)
            pool.dma_start(acol[32:40, 1:2], a["dt_bias_c"].rearrange("o h -> h o")).then_inc(acol_in, 16)
            add_squares(2)
            pool.wait_ge(acc_read, N_IN_C)
            pool.wait_ge(g_lo_made, FT)
            R.done("zc", nc.gpsimd.memset(zc[:, :, 0:CONV - 1], 0.0))
            R.done("wab_zero", nc.gpsimd.memset(wab_pad[:], 0.0))
            pool.wait_ge(wab_in, 16)
            pool.wait_ge(R.sem, R.at("wab_zero"))
            R.done("wab_pad_b", nc.gpsimd.tensor_copy(wab_pad[:, :, 0:GH], wab_raw[:, :, 0:GH]))
            R.done("wab_pad_a", nc.gpsimd.tensor_copy(wab_pad[:, :, 32:32 + GH], wab_raw[:, :, GH:2 * GH]))
            R.done("rows_zero", nc.gpsimd.memset(rows[:], 0.0))
            pool.wait_ge(pre["dve"].sem, pre["dve"].all())

            A, B = ga["pool"], gb["pool"]

            def turn(it, a_on, b_on):
                ha, hb = it - 1, it - 2

                def wait(steps, name, h):
                    pool.wait_ge(steps.sem, steps.at(name, h))

                def level(n):
                    if a_on:
                        mask = delta[:, G_LEVEL + n * P:G_LEVEL + (n + 1) * P].unsqueeze(1).to_broadcast([P, QB, P])
                        A.done(f"lev{n}", nc.gpsimd.tensor_tensor(lev[:, n % 2], lowT[:], mask, ALU.mult))

                if a_on:
                    if b_on:
                        wait(ga["pe"], "beta", hb)
                    A.done("rowsel", nc.gpsimd.tensor_tensor(rowsel[0:64], rows[0:64], delta[0:64, bass.ds(G_SEL + ha, 1)].to_broadcast([64, T]), ALU.mult))
                    wait(ga["dve"], "diff", ha)
                    tri = delta[:, G_TRI:G_TRI + P].unsqueeze(1).to_broadcast([P, QB, P])
                    A.done("mask", nc.gpsimd.tensor_tensor(decay[:], decay[:], tri, ALU.add))
                    wait(ga["dve"], "low", ha)
                    level(0)
                    level(1)
                    wait(ga["dve"], "one", ha)
                    level(2)
                    for n in (3, 4):
                        wait(ga["pe"], f"p{n - 2}", ha)
                        level(n)
                if b_on:
                    pool.wait_ge(s_read, 16 * hb + 16)
                    wait(gb["pe"], "dx", hb)
                    B.done("s_decayed", nc.gpsimd.tensor_tensor(s_in[:], s_in[:], sm[:, 5].unsqueeze(2).to_broadcast([P, NS, P]), ALU.mult))
                if a_on:
                    for n in (5, 6):
                        wait(ga["pe"], f"p{n - 2}", ha)
                        level(n)

            turn(1, True, False)
            with pool.Fori(2, GH) as it:
                turn(it, True, True)
            turn(GH, True, True)
            turn(GH + 1, False, True)
            add_squares(3)
            add_squares(4)


_OUTS = {
    "y_prompt": (1, 512, 1024), "y_sample": (8, 1, 1024),
    "a_k_prompt": (1, 1, 512, 8, 64), "a_v_prompt": (1, 1, 512, 8, 64),
    "pool_prompt": (1, 1, 15, 512), "conv_prompt": (1, 1, 3, 3072), "gdn_prompt": (1, 1, 8, 128, 128),
    "a_k_sample": (1, 8, 513, 8, 64), "a_v_sample": (1, 8, 513, 8, 64),
    "pool_sample": (1, 8, 15, 512), "conv_sample": (1, 8, 3, 3072), "gdn_sample": (1, 8, 8, 128, 128),
}


def kernel(**inputs):
    import numpy as _np
    import concourse.bacc as _bacc
    from concourse import mybir as _mybir
    from concourse.bass_utils import run_bass_kernel_spmd as _run

    arrays = {name: _np.ascontiguousarray(x) for name, x in inputs.items()}
    arrays["par_rows"] = _np.concatenate([arrays[n].reshape(-1, P) for n in (
        "norm_mix", "norm_ffn", "norm_final", "pool_scale", "norm_out_c")], 0)
    arrays["const_table"], arrays["delta_table"] = constant_table(), delta_table()
    arrays["attention_table"], arrays["decode_table"] = attention_table(), decode_table()
    arrays["pool_table"], arrays["select_table"] = pool_table(), select_table()
    used = [n for n in arrays if n not in ("norm_mix", "norm_ffn", "norm_final", "pool_scale", "norm_out_c")]
    nc = _bacc.Bacc("TRN2", target_bir_lowering=False, num_devices=1)
    a = {n: nc.dram_tensor(f"in_{n}", arrays[n].shape, _mybir.dt.from_np(arrays[n].dtype), kind="ExternalInput").ap() for n in used}
    o = {n: nc.dram_tensor(f"out_{n}", shape, F32, kind="ExternalOutput").ap() for n, shape in _OUTS.items()}
    build(nc, a, o)
    r = _run(nc, [{f"in_{n}": arrays[n] for n in used}], core_ids=[0])
    return tuple(r.results[0][f"out_{n}"] for n in _OUTS)
```

```python
import math
from contextlib import ExitStack

import concourse.bass as bass
import numpy as np
from concourse import mybir

F32 = mybir.dt.float32
F32R = mybir.dt.float32r
ALU = mybir.AluOpType
ACT = mybir.ActivationFunctionType
AX = mybir.AxisListType

P = 128
D_MODEL = 1024
SEQ = 512
NS = 8
T = SEQ + NS
TH = T // 2
KD = D_MODEL // P
HEADS = 8
HD = 64
A_W = HEADS * HD
PAST = 512
POOL_HIST = 15
POOL_WINDOWS = (2, 4, 8, 16)
QB = SEQ // P
FFN = 2816
FT = FFN // P
PARTS = (8, 8, 6)
GH = 8
CONV = 4
QK = GH * P
SLOT = 2048
LEVELS = (1, 2, 4, 8, 16, 32, 64)
EPS = 1e-6
NEG = -1e30
KEYS_A = 128
KEYS_B = 96
KEYS = KEYS_A + KEYS_B + 1

N_IN_A = 0
N_OUT_A = N_IN_A + 16
N_FFN0 = N_OUT_A + KD
N_FFN = 2 * FT + KD * len(PARTS)
N_IN_C = N_FFN0 + N_FFN
N_OUT_C = N_IN_C + 4 * GH
N_FFN1 = N_OUT_C + KD
N_ALL = N_FFN1 + N_FFN
BLOCK = KD * P
IN_A_TILES = [4 * r + t for r in (3, 2, 1, 0) for t in range(4)]

C_ID = 0
C_ONE = C_ID + P
C_COL = C_ONE + P
C_END = C_COL + 3
G_LEVEL = 0
G_TRI = G_LEVEL + len(LEVELS) * P
G_HALF = G_TRI + P
G_KEEP = G_HALF + 2 * P
G_SEL = G_KEEP + T
G_END = G_SEL + GH


def multiplicity(d):
    return int(0 <= d <= 128) + int(d >= 0 and d % 4 == 0 and d // 4 <= 128) + int(d >= 0 and d % 16 == 0 and d // 16 <= 128)


def slope(h):
    return 2.0 ** (-8.0 * (h + 1) / HEADS)


def log_count(d):
    c = multiplicity(d)
    return math.log(c) if c else NEG


def constant_table():
    t = np.ones((P, C_END), np.float32)
    t[:, C_ID:C_ID + P] = np.eye(P)
    t[:, C_COL] = EPS
    t[:, C_COL + 1] = -0.5 * math.log(P)
    return t


def delta_table():
    t = np.zeros((P, G_END), np.float32)
    j = np.arange(P)[:, None]
    i = np.arange(P)[None, :]
    for n, s in enumerate(LEVELS):
        t[:, G_LEVEL + n * P:G_LEVEL + (n + 1) * P] = (j // (2 * s) == i // (2 * s)) & (j % (2 * s) < s) & (i % (2 * s) >= s)
    t[:, G_TRI:G_TRI + P] = np.where(i >= j, 0.0, NEG)
    t[0:32, G_HALF:G_HALF + P] = 1.0
    t[32:64, G_HALF + P:G_HALF + 2 * P] = 1.0
    t[:, G_KEEP:G_KEEP + SEQ] = (np.arange(SEQ) % P != 0)[None, :]
    for h in range(GH):
        t[h, G_SEL + h] = t[32 + h, G_SEL + h] = 1.0
    return t


def attention_table():
    d = np.arange(P)[:, None] + 3 * P - np.arange(SEQ)[None, :]
    count = np.vectorize(log_count)(np.arange(-P, SEQ + P + 1))
    lc = count[d + P]
    return np.concatenate([d, np.where(lc < NEG / 2, NEG, 8.0 * lc)], 1).astype(np.float32)


def decode_table():
    dist = [PAST - t for t in range(PAST - KEYS_A, PAST)] + [PAST - 4 * r for r in range(KEYS_B)] + [0]
    rows = [[8.0 * (log_count(d) - slope(h) * d) for d in dist] for _ in range(NS) for h in range(HEADS)]
    return np.asarray(rows, np.float32)


def pool_table():
    rows = [[1.0 / min(t + 1, w) for t in range(SEQ)] + [1.0 / w] * NS for w in POOL_WINDOWS]
    return np.broadcast_to(np.asarray(rows, np.float32).reshape(1, -1), (P, len(rows) * T)).copy()


def select_table():
    return np.repeat(np.eye(NS, dtype=np.float32), P, 1)


IN_C_PART = (0, 1, 3, 2)
NORM_ROWS = (0, 2, 1, 3, 4)


class Steps:

    def __init__(self, sem, names):
        self.sem, self.names, self.n = sem, {x: n for n, x in enumerate(names)}, 0
        assert len(self.names) == len(names)

    def at(self, name, turn=0):
        return turn * len(self.names) + self.names[name] + 1

    def all(self, turn=1):
        return turn * len(self.names)

    def done(self, name, instruction):
        assert self.names[name] == self.n % len(self.names), (name, self.n)
        self.n += 1
        instruction.then_inc(self.sem, 1)


def build(nc, a, o):
    ctx = ExitStack()
    with ctx:
        def sem(name):
            return ctx.enter_context(nc.semaphore(name))

        def sb(name, cols, dt=F32, stack=ctx):
            shape = [P, *cols] if isinstance(cols, (list, tuple)) else [P, cols]
            return stack.enter_context(nc.sbuf_tensor(name, shape, dt))

        NL = len(LEVELS)

        xT = sb("xT", [KD, T])
        const = sb("const", C_END)
        par = sb("par", 48)
        wconv = sb("wconv", [CONV, 3 * GH])
        rstd = sb("rstd", T)
        ssum = sb("ssum", T)
        sq = sb("sq", [2, T])
        w_raw = sb("w_raw", [2, BLOCK])
        w_hi = sb("w_hi", [2, BLOCK], F32R)
        w_lo = sb("w_lo", [2, BLOCK], F32R)
        with ExitStack() as s:
            gateT = sb("gateT", [KD, T], F32, s)
        g_hi = sb("g_hi", [KD, T], F32R)
        g_lo = sb("g_lo", [KD, T], F32R)

        with ExitStack() as s:
            ck = sb("ck", [4, 2, A_W], F32, s)
            cv = sb("cv", [4, 2, A_W], F32, s)
        h_hi = sb("h_hi", [KD, T], F32R)
        h_lo = sb("h_lo", [KD, T], F32R)

        with ExitStack() as s:
            x_tok = sb("x_tok", [QB, D_MODEL], F32, s)
            xs_tok = sb("xs_tok", D_MODEL, F32, s)
            par_rows = sb("par_rows", [2, P], F32, s)
        with ExitStack() as s:
            zT = sb("zT", [16, T], F32, s)
            v_tok = sb("v_tok", [QB, A_W], F32, s)
            k_stage = sb("k_stage", [2, QB, P], F32, s)
            z_tok = sb("z_tok", [3, A_W], F32, s)
            u_tok = sb("u_tok", A_W, F32, s)
            hist_rows = sb("hist_rows", A_W, F32, s)
            sel8 = sb("sel8", [NS, P], F32, s)
            prod = sb("prod", [2, A_W], F32, s)
            dec_s = sb("dec_s", [2, NS * HEADS], F32, s)
            dec_tab = sb("dec_tab", KEYS, F32, s)
            dec_p = sb("dec_p", KEYS, F32, s)
            dec_pT = sb("dec_pT", [2, NS * HEADS], F32, s)
            dec_col = sb("dec_col", 4, F32, s)
            att_tab = sb("att_tab", [2, SEQ], F32, s)
            with ExitStack() as s1:
                bias = sb("bias", SEQ, F32, s1)
                prob = sb("prob", [2, 10 * P], F32, s1)
                probT = sb("probT", [2, SEQ], F32, s1)
                o_tok = sb("o_tok", [QB, P], F32, s1)
                att_col = sb("att_col", [2, 4, QB], F32, s1)
            with ExitStack() as s1:
                histT = sb("histT", [4, NS, POOL_HIST], F32, s1)
                cnt = sb("cnt", [4, T], F32, s1)
                wpool = sb("wpool", [4, P], F32, s1)
                run = sb("run", [2, T], F32, s1)
                tail = sb("tail", NS, F32, s1)
                pooled = sb("pooled", [2, T], F32, s1)
        with ExitStack() as s:
            gate_n = sb("gate_n", T, F32, s)
            gate_s = sb("gate_s", T, F32, s)
            up_n = sb("up_n", T, F32, s)
            gu = sb("gu", T, F32, s)
        with ExitStack() as s:
            zc = sb("zc", [3, CONV - 1 + T], F32, s)
            y = sb("y", [3, T], F32, s)
            delta = sb("delta", G_END, F32, s)
            chist = sb("chist", [3 * GH, NS, CONV - 1], F32, s)
            cprod = sb("cprod", [3 * GH, NS], F32, s)
            rows = sb("rows", T, F32, s)
            acol = sb("acol", 4, F32, s)
            tokcols = sb("tokcols", [QB, 64], F32, s)
            z_rows = sb("z_rows", [3, P], F32, s)
            with ExitStack() as s1:
                wab_hi = sb("wab_hi", [KD, 64], F32R, s1)
                wab_lo = sb("wab_lo", [KD, 64], F32R, s1)
                crow = sb("crow", 3 * GH * P, F32, s1)
                ctmp = sb("ctmp", [3 * GH, NS], F32, s1)
                wab_raw = sb("wab_raw", [KD, 2 * GH], F32, s1)
                wab_pad = sb("wab_pad", [KD, 64], F32, s1)
                ab = sb("ab", T, F32, s1)
                abt = sb("abt", [3, T], F32, s1)
            with ExitStack() as s1:
                qn = sb("qn", T, F32, s1)
                kn = sb("kn", T, F32, s1)
                rowsel = sb("rowsel", T, F32, s1)
                gcb = sb("gcb", T, F32, s1)
                egb = sb("egb", T, F32, s1)
                betab = sb("betab", T, F32, s1)
                decay = sb("decay", [QB, P], F32, s1)
                bdecay = sb("bdecay", [QB, P], F32, s1)
                lowT = sb("lowT", [QB, P], F32, s1)
                ip = sb("ip", [NL - 1, QB, P], F32, s1)
                edk = sb("edk", QB, F32, s1)
                with ExitStack() as s2:
                    sqg = sb("sqg", [2, T], F32, s2)
                    rqk = sb("rqk", [2, T], F32, s2)
                with ExitStack() as s2:
                    lev = sb("lev", [2, QB, P], F32, s2)
                    sb("pad1", 2 * (T - SEQ), F32, s2)
                    tinv = sb("tinv", [QB, P], F32, s2)
                    tinvT = sb("tinvT", [QB, P], F32, s2)
                    sb("pad2", 2 * (T - SEQ), F32, s2)
                    qg = sb("qg", T, F32, s2)
                    kbg = sb("kbg", T, F32, s2)
                    attT = sb("attT", [QB, P], F32, s2)
                    vb = sb("vb", [QB, P], F32, s2)
                    kdec = sb("kdec", [QB, P], F32, s2)
                    t_all = sb("t_all", [QB, P], F32, s2)
                    kq = sb("kq", [NS, 2], F32, s2)
                    sm = sb("sm", [7, NS], F32, s2)
                    state = sb("state", P, F32, s2)
                    resid = sb("resid", P, F32, s2)
                    vnew = sb("vnew", P, F32, s2)
                    yo = sb("yo", T, F32, s2)
                    s_in = sb("s_in", [NS, P], F32, s2)
                    dvexp = sb("dvexp", [2, SEQ], F32, s2)
                    kv_rows = sb("kv_rows", [2, P], F32, s2)
        osq, ors = sq[:, 0], sq[:, 1]
        with ExitStack() as s:
            y_fin = sb("y_fin", [KD, T], F32, s)
            y_tok = sb("y_tok", [QB + 1, D_MODEL], F32, s)
            r_tok = sb("r_tok", 2 * (QB + 1), F32, s)

        acc = ctx.enter_context(nc.psum_tensor("acc", [P, 4, 512], F32))
        aux = ctx.enter_context(nc.psum_tensor("aux", [P, 4, 512], F32))

        def turned_bank(b):
            return acc[:, 2] if b % 2 else aux[:, 2]

        def halves(x):
            return x.rearrange("p (b t) -> p b t", b=2)

        def apart(engine):
            engine.nop()

        def half_cols(x, n, second=False):
            k = x.rearrange("p c (k two s) -> p (c k) two s", two=2, s=1 << n)
            return k[:, :, 1 if second else 0, :]

        def packed(bank, n):
            return aux[:, bank, 0:SEQ // 2].rearrange("p (k s) -> p k s", s=1 << n)

        def blocks(x):
            return x.rearrange("p (c m) -> p c m", m=P)

        def accv(slot):
            return acc[:, 2 * slot:2 * slot + 2, 0:TH]

        def auxv(pair):
            return aux[:, 2 * pair:2 * pair + 2, 0:TH]

        def column(tensor, n):
            return tensor[:, n:n + 1] if isinstance(n, int) else tensor[:, bass.ds(n, 1)]

        ident = const[:, C_ID:C_ID + P]
        ones = const[:, C_ONE:C_ONE + P]
        eps_col = const[:, C_COL:C_COL + 1]
        lnq_col = const[:, C_COL + 1:C_COL + 2]
        one_col = const[:, C_COL + 2:C_COL + 3]

        const_in, par_in, xs_in, tab_in, sel_in, hist_in, pool_in = (
            sem(n) for n in ("const_in", "par_in", "xs_in", "tab_in", "sel_in", "hist_in", "pool_in"))
        x_in = [sem(f"x_in{b}") for b in range(QB)]
        w_loaded = [sem("w_loaded0"), sem("w_loaded1")]
        w_hi_made, w_lo_made = sem("w_hi_made"), sem("w_lo_made")
        acc_full = sem("acc_full")
        acc_read = sem("acc_read")
        h_hi_made, h_lo_made, sq_made, ss_added = (sem(n) for n in ("h_hi_made", "h_lo_made", "sq_made", "ss_added"))
        ss_clear, ss_full, ln_made, rstd_made = (sem(n) for n in ("ss_clear", "ss_full", "ln_made", "rstd_made"))
        silu_made, gu_made, g_hi_made, g_lo_made = (sem(n) for n in ("silu_made", "gu_made", "g_hi_made", "g_lo_made"))
        ck_in, cv_in, ck2_in, cv2_in, self_in, self2_in = (
            sem(n) for n in ("ck_in", "cv_in", "ck2_in", "cv2_in", "self_in", "self2_in"))
        k_stored = [sem("k_stored0"), sem("k_stored1")]
        delta_in, crow_in, wab_in, acol_in, s_read, s_stored, st_stored, zr_stored = (
            sem(n) for n in ("delta_in", "crow_in", "wab_in", "acol_in", "s_read", "s_stored", "st_stored", "zr_stored"))
        stored = sem("stored")
        copied = sem("copied")
        y_stored = sem("y_stored")
        y_fin_made = sem("y_fin_made")

        up = {e: Steps(sem(f"up_{e}"), n) for e, n in {
            "pe": ["par", "xs"] + [f"x{m}" for m in range(KD)],
            "dve": ["par", "wconv", "xs"] + [f"x{m}" for m in range(KD)],
        }.items()}
        in_a_pe = {4: ["u_turned", "hist_turned"], 5: ["v_turned0"], 6: ["v_turned1"], 7: ["v_turned2", "pooled0"],
                   8: ["v_turned3", "pooled1"], 9: ["k_turned0"], 10: ["k_turned1", "pooled2"], 11: ["k_turned2"],
                   12: ["k_turned3", "pooled3"], 15: ["z_turned"]}
        tails = [[f"tail{g}", f"tail_sum{g}", f"tail_p{g}"] for g in range(4)]
        in_a_dve = {4: ["u_kept", "histT"], 5: ["v_kept0"] + tails[0], 6: ["v_kept1"] + tails[1], 7: ["v_kept2"],
                    8: ["v_kept3", "pool_lo0"] + tails[2], 9: ["pool_lo1"] + tails[3], 11: ["pool_lo2"], 13: ["pool_lo3"], 15: ["z_kept"]}
        in_a_act = {7: ["pool_hi0"], 8: ["pool_hi1"], 9: ["k_kept0"], 10: ["k_kept1", "pool_hi2"], 11: ["k_kept2"], 12: ["k_kept3", "pool_hi3"]}
        spread_at = {(1, b): b for b in range(4)} | {(3, b): 4 + b for b in range(4)}
        dec_pe = {x: [f"q_spread{b}"] for x, b in spread_at.items()} | {(4, 0): ["s_turned"], (5, 0): ["dp_turned"], (7, 1): ["dec_out"]}
        dec_dve = {x: [f"{name}{b}" for name in ("prod_a", "prod_b", "sum_a", "sum_b")] for x, b in spread_at.items()} | {
            (4, 0): ["dec_max", "dec_neg"], (4, 2): ["dec_inv", "dec_norm"], (5, 0): ["dec_pT"], (7, 3): ["dec_lo0", "dec_lo1"]}
        dec_act = {(4, 1): ["dec_exp"], (7, 2): ["dec_hi0", "dec_hi1"]}
        pe_att = [x for names in in_a_pe.values() for x in names]
        for h in range(HEADS + 1):
            for b in range(QB):
                if h < HEADS:
                    pe_att.append(f"scores{h}{b}")
                if h:
                    pe_att.append(f"p_turned{h - 1}{b}")
                    pe_att += [f"pv{h - 1}{b - 1}"] if b else []
                pe_att += dec_pe.get((h, b), [])
            if h:
                pe_att.append(f"pv{h - 1}{QB - 1}")
                if h % 2 == 0:
                    pe_att.append(f"o_turned{h // 2 - 1}")
        dve_att = [x for names in in_a_dve.values() for x in names]
        for h in range(HEADS + 1):
            if h < HEADS:
                dve_att.append(f"bias{h}")
            for b in range(QB):
                if h < HEADS:
                    dve_att += [f"max{h}{b}", f"neg{h}{b}"]
                if h and b % 2:
                    dve_att.append(f"pT{h - 1}{b}")
                dve_att += dec_dve.get((h, b), [])
            if h:
                dve_att += [f"inv{h - 1}", f"o{h - 1}"]
                if h % 2 == 0:
                    dve_att.append(f"g_lo{h // 2 - 1}")
        act_att = [x for names in in_a_act.values() for x in names]
        for h in range(HEADS + 1):
            for b in range(QB):
                if h < HEADS:
                    act_att.append(f"exp{h}{b}")
                if h and b % 2 == 0:
                    act_att.append(f"pT{h - 1}{b}")
                act_att += dec_act.get((h, b), [])
            if h and h % 2 == 0:
                act_att.append(f"g_hi{h // 2 - 1}")
        pool_att = []
        for g in range(4):
            pool_att += [f"run{g}{n}{x}" for n in range(g + 1) for x in "ab"] + [f"mean{g}", f"pool{g}"]
        at = {e: Steps(sem(f"mix_{e}"), n) for e, n in
              {"pe": pe_att, "dve": dve_att, "act": act_att, "pool": pool_att}.items()}

        pre = {e: Steps(sem(f"pre_{e}"), n) for e, n in {
            "pe": ["ab", "chist0", "chist1", "rows_turned"],
            "act": ["wab_hi", "exp_b", "exp_sp", "ln_sp", "exp_a"],
            "dve": ["wab_lo", "ab", "beta1", "beta", "dt", "abs", "sp", "nega", "g", "cum",
                    "chist0", "chist1", "prod0", "prod1", "sum1", "prod2", "sum2", "tokcols"],
            "pool": ["wab_zero", "wab_pad_b", "wab_pad_a", "rows_zero", "zc", "ip_ones"],
        }.items()}
        taps = lambda r: [f"tap_{r}{i}" for i in range(4)]
        gg = {e: Steps(sem(f"heads_g_{e}"), n) for e, n in {
            "pe": ["tail_q", "tail_k"],
            "act": ["tap_q", "tap_k", "silu_q", "silu_k", "silu_g"],
            "dve": ["z_q"] + taps("q") + ["z_k"] + taps("k"),
        }.items()}
        ga = {e: Steps(sem(f"heads_a_{e}"), n) for e, n in {
            "pe": ["gc", "beta", "ss_q", "tail_v", "ss_k", "kk", "t_turned", "p1", "t1", "p2", "u1", "t2", "p3", "u2", "t3",
                   "p4", "u3", "t4", "p5", "u4", "t5", "turn_k", "p6", "u5", "turn_v", "u6", "qk"],
            "act": ["tap_v", "gcb", "egb", "sq_q", "sq_k", "ln_q", "rs_q", "ln_k", "rs_k", "decay", "edk", "tinv",
                    "t1", "t2", "t3", "t4", "silu_v", "t5", "kq_k", "kq_q"],
            "dve": ["betab", "z_v", "diff", "edk", "qn", "kn", "bdecay", "diag", "low", "one", "tap_v0", "tap_v1", "ip1", "tap_v2", "tap_v3", "u1", "ip2", "qg", "kb", "kbg",
                                "u2", "ip3", "u3", "ip4", "u4", "ip5", "kdec", "dkq", "dvb", "keep_k", "keep_e", "keep_c",
                                "u5", "ip6", "vb", "t_first", "u6", "attT"],
            "pool": ["rowsel", "mask"] + [f"lev{n}" for n in range(NL)],
        }.items()}
        gb = {e: Steps(sem(f"heads_b_{e}"), n) for e, n in {
            "pe": ["v0", "o0", "s0"] + [f"{x}{c}" for c in range(1, QB) for x in ("ks", "v", "o", "s")] + ["dx", "dqk", "dk_turned", "dv_turned", "osum", "outer"],
            "act": [f"v{c}" for c in range(QB)] + ["oT", "o_sq", "o_ln", "o_rs", "g_hi"],
            "dve": ["s0", "r1", "s1", "r2", "s2", "r3", "s3", "dv", "dqk", "do", "d_rows", "dvexp", "s_new", "on", "og", "g_lo"],
            "pool": ["s_decayed"],
        }.items()}
        fin = {e: Steps(sem(f"fin_{e}"), n) for e, n in {
            "pe": ["y0", "y1", "y2", "sums", "y3", "y4"], "act": ["ln", "ln_s", "rstd", "rstd_s", "y_tok1", "y_tok3"],
            "dve": ["y_tok0", "y_tok2", "y_tok4"]}.items()}

        w_in_a, w_out_a = a["w_in_a"][0], a["w_out_a"][0]
        w_in_c, w_out_c = a["w_in_c"][0], a["w_out_c"][0]

        def column_blocks(w, k0=0, kt=KD, cols=None):
            w = w[k0 * P:(k0 + kt) * P, 0:cols or w.shape[1]]
            return w.rearrange("(k p) (c m) -> c p k m", p=P, m=P)

        block = ctx.enter_context(nc.Block())

        @block.sync
        def _(sp):
            def load(n, slot, src, kt=KD):
                if not isinstance(n, int) or n >= 2:
                    sp.wait_ge(w_lo_made, n - 1)
                sp.dma_start(w_raw[:, slot, 0:kt * P].rearrange("p (k m) -> p k m", m=P), src).then_inc(w_loaded[slot], 16)

            for b in range(QB):
                sp.dma_start(x_tok[:, b], a["x_prompt"][0, b * P:(b + 1) * P, :]).then_inc(x_in[b], 16)
            in_a = column_blocks(w_in_a)
            for n in range(16):
                load(N_IN_A + n, n % 2, in_a[IN_A_TILES[n]])
            out_a = column_blocks(w_out_a)
            load(N_OUT_A, 0, out_a[0])
            load(N_OUT_A + 1, 1, out_a[1])
            sp.wait_ge(acc_full, N_OUT_A)

            sp.dma_start(o["pool_sample"][0, :, 0:POOL_HIST - 1, :], a["state_pool"][0, :, 1:POOL_HIST, :]).then_inc(copied, 16)
            sp.dma_start(o["conv_sample"][0, :, 0:CONV - 2, :], a["state_conv"][0, :, 1:CONV - 1, :]).then_inc(copied, 16)

            def cached(dst, src, b0, signal):
                cache = src[0, b0:b0 + 4].rearrange("b t h d -> t b (h d)")
                sp.dma_start(dst[:, :, 0, :], cache[PAST - KEYS_A:PAST]).then_inc(signal, 16)
                sp.dma_start(dst[0:KEYS_B, :, 1, :], cache[0:PAST - KEYS_A:4]).then_inc(signal, 16)

            def own_row(dst, r, b0, signal):
                for b in range(4):
                    sp.dma_start(dst[KEYS_B:KEYS_B + 1, b, 1, :], z_tok[b0 + b:b0 + b + 1, r, :]).then_inc(signal, 16)

            sp.wait_ge(at["dve"].sem, at["dve"].at("z_kept"))
            cached(ck, a["state_a_k"], 0, ck_in)
            own_row(ck, 1, 0, self_in)
            cached(cv, a["state_a_v"], 0, cv_in)
            own_row(cv, 2, 0, cv_in)
            sp.wait_ge(at["dve"].sem, at["dve"].at("sum_b3"))
            cached(ck, a["state_a_k"], 4, ck2_in)
            own_row(ck, 1, 4, self2_in)
            sp.wait_ge(at["dve"].sem, at["dve"].at(f"sum_b{NS - 1}"))
            cached(ck, a["state_a_v"], 4, cv2_in)
            own_row(ck, 2, 4, cv2_in)
            for n in range(2, KD, 1):
                load(N_OUT_A + n, n % 2, out_a[n])

            def ffn(layer, base):
                gate, upw = column_blocks(a["w_ffn_gate"][layer]), column_blocks(a["w_ffn_up"][layer])
                k0 = 0
                for part, kt in enumerate(PARTS):
                    with sp.Fori(0, kt) as i:
                        load(base + 2 * i, 0, gate[i + k0])
                        load(base + 2 * i + 1, 1, upw[i + k0])
                        if layer == 0 and part < 2:
                            old, new = (("state_a_k", "a_k_sample"), ("state_a_v", "a_v_sample"))[part]
                            sp.dma_start(o[new][0].rearrange("b t h d -> b t (h d)")[:, 0:PAST][i],
                                         a[old][0].rearrange("b t h d -> b t (h d)")[i]).then_inc(copied, 16)
                    base += 2 * kt
                    down = column_blocks(a["w_ffn_down"][layer], k0, kt)
                    with sp.Fori(0, KD // 2) as i:
                        for s in range(2):
                            load(base + 2 * i + s, s, down[2 * i + s], kt)
                    base += KD
                    k0 += kt

            ffn(0, N_FFN0)
            in_c = column_blocks(w_in_c, cols=4 * QK)
            out_c = column_blocks(w_out_c)
            a_dve, b_dve = ga["dve"], gb["dve"]

            def turn(it, ahead=None, a_on=True, b_on=True):
                if a_on:
                    conv_prompt = o["conv_prompt"][0, 0].rearrange("i (r h m) -> h i r m", r=3, m=P)[it - 1]
                    conv_sample = o["conv_sample"][0, :, CONV - 2].rearrange("b (r h m) -> h b r m", r=3, m=P)[it - 1]
                if b_on:
                    gdn_prompt = o["gdn_prompt"][0, 0].rearrange("h k v -> h k v")[it - 2]
                    gdn_sample = o["gdn_sample"][0].rearrange("b h k v -> h k b v")[it - 2]
                    if not isinstance(it, int) or it > 2:
                        sp.wait_ge(s_stored, 16 * (it - 2))
                    sp.dma_start(s_in[:], a["state_gdn"][0].rearrange("b h k v -> h k b v")[it - 2]).then_inc(s_read, 16)
                if ahead:
                    load(N_IN_C + 4 * it + 2, 0, in_c[GH * IN_C_PART[2] + it])
                if a_on:
                    sp.wait_ge(a_dve.sem, a_dve.at("z_v", it - 1))
                    sp.dma_start(conv_prompt, z_rows[0:3]).then_inc(zr_stored, 16)
                    sp.dma_start(conv_sample, z_rows[3:11]).then_inc(zr_stored, 16)
                if ahead:
                    load(N_IN_C + 4 * it + 3, 1, in_c[GH * IN_C_PART[3] + it])
                    load(N_IN_C + 4 * it + 4, 0, ahead[0])
                if b_on:
                    sp.wait_ge(b_dve.sem, b_dve.at(f"s{QB - 1}", it - 2))
                    sp.dma_start(gdn_prompt, state[:]).then_inc(st_stored, 16)
                if ahead:
                    load(N_IN_C + 4 * it + 5, 1, ahead[1])
                if b_on:
                    sp.wait_ge(b_dve.sem, b_dve.at("s_new", it - 2))
                    sp.dma_start(gdn_sample, s_in[:]).then_inc(s_stored, 16)

            for r in range(2):
                load(N_IN_C + r, r, in_c[GH * r])
            turn(0, [in_c[GH * r + 1] for r in range(2)], False, False)
            turn(1, [in_c[GH * r + 2] for r in range(2)], True, False)
            turn(2, [in_c[GH * r + 3] for r in range(2)])
            with sp.Fori(3, GH - 1) as it:
                turn(it, [in_c[GH * r + it + 1] for r in range(2)])
            turn(GH - 1, [out_c[0], out_c[1]])
            turn(GH)
            turn(GH + 1, None, False)
            with sp.Fori(1, KD // 2) as i:
                for s in range(2):
                    load(N_OUT_C + 2 * i + s, s, out_c[2 * i + s])
            ffn(1, N_FFN1)
            for b in range(QB + 1):
                copier = fin["act" if b in (1, 3) else "dve"]
                sp.wait_ge(copier.sem, copier.at(f"y_tok{b}"))
                if b < QB:
                    sp.dma_start(o["y_prompt"][0, b * P:(b + 1) * P, :], y_tok[:, b]).then_inc(y_stored, 16)
                else:
                    sp.dma_start(o["y_sample"].rearrange("b t d -> (b t) d"), y_tok[0:NS, b]).then_inc(y_stored, 16)
            sp.wait_ge(y_stored, 16 * (QB + 1))
            sp.wait_ge(stored, 16 * 5)
            for q in range(2):
                sp.wait_ge(k_stored[q], 32)
            sp.wait_ge(copied, 16 * (2 * NS + 2))
            sp.wait_ge(s_stored, 16 * GH)
            sp.wait_ge(st_stored, 16 * GH)
            sp.wait_ge(zr_stored, 32 * GH)

        @block.tensor
        def _(pe):
            def product(n, slot, kt, xh, xl, hi_at=None, lo_at=None):
                if not isinstance(n, int) or n >= 2:
                    pe.wait_ge(acc_read, n - 1)
                pe.wait_ge(w_hi_made, n + 1)
                for part, (w, x, ready) in enumerate(((w_hi, xh, hi_at), (w_hi, xl, lo_at), (w_lo, xh, None))):
                    if part == 2:
                        pe.wait_ge(w_lo_made, n + 1)
                    for k in range(kt):
                        if ready:
                            pe.wait_ge(*ready(k))
                        for b in range(2):
                            last = nc.tensor.matmul(acc[:, 2 * slot + b, 0:TH], w[:, slot, k * P:(k + 1) * P],
                                                    x[:, k, b * TH:(b + 1) * TH], start=part == 0 and k == 0,
                                                    stop=part == 2 and k == kt - 1)
                last.then_inc(acc_full, 1)

            def norm_sum(k):
                pe.wait_ge(ss_added, KD * (k + 1))
                for b in range(2):
                    mm = nc.tensor.matmul(aux[:, b, 0:TH], ones, ssum[:, b * TH:(b + 1) * TH], start=True, stop=True)
                mm.then_inc(ss_full, 1)

            def normed(k):
                return {"hi_at": lambda kt: (h_hi_made, KD * k + kt + 1), "lo_at": lambda kt: (h_lo_made, KD * k + kt + 1)}

            def ffn(k, base, g_base):
                product(base, 0, KD, h_hi, h_lo, **normed(k))
                norm_sum(k)
                product(base + 1, 1, KD, h_hi, h_lo)
                for part, kt in enumerate(PARTS):
                    with pe.Fori(0 if part else 1, kt) as i:
                        product(base + 2 * i, 0, KD, h_hi, h_lo)
                        product(base + 2 * i + 1, 1, KD, h_hi, h_lo)
                    base += 2 * kt
                    with pe.Fori(0, KD // 2) as i:
                        product(base + 2 * i, 0, kt, g_hi, g_lo, lambda j: (g_hi_made, g_base + j + 1), lambda j: (g_lo_made, g_base + j + 1))
                        product(base + 2 * i + 1, 1, kt, g_hi, g_lo)
                    base += KD
                    g_base += kt

            U = up["pe"]
            pe.wait_ge(const_in, 16)
            pe.wait_ge(par_in, 32)
            nc.tensor.transpose(aux[:, 3, 0:45], par_rows[0:45, 0], ident[0:45, 0:45])
            U.done("par", nc.tensor.transpose(aux[:, 3, 64:64 + 96], par_rows[0:96, 1], ident[0:96, 0:96]))
            pe.wait_ge(xs_in, 16)
            for m in range(KD):
                tr = nc.tensor.transpose(aux[:, 2, m * NS:(m + 1) * NS], xs_tok[0:NS, m * P:(m + 1) * P], ident[0:NS, 0:NS])
            U.done("xs", tr)
            for m in range(KD):
                if m >= 2:
                    pe.wait_ge(up["dve"].sem, up["dve"].at(f"x{m - 2}"))
                for b in range(QB):
                    if m == 0:
                        pe.wait_ge(x_in[b], 16)
                    tr = nc.tensor.transpose(aux[:, m % 2, b * P:(b + 1) * P], x_tok[:, b, m * P:(m + 1) * P], ident)
                U.done(f"x{m}", tr)
            pe.wait_ge(up["dve"].sem, up["dve"].at(f"x{KD - 1}"))
            A, dve_at, act_at = at["pe"], at["dve"], at["act"]

            def turn_v(t):
                pe.wait_ge(acc_read, 5 + t)
                pe.wait_ge(dve_at.sem, dve_at.at(("u_kept", "histT", "v_kept0", "v_kept1")[t]))
                for b in range(QB):
                    tr = nc.tensor.transpose(aux[:, 2 + t % 2, b * P:(b + 1) * P], zT[:, 8 + t, b * P:(b + 1) * P], ident)
                A.done(f"v_turned{t}", tr)

            def turn_k(t):
                pe.wait_ge(acc_read, 9 + t)
                if t < 2:
                    pe.wait_ge(dve_at.sem, dve_at.at(f"v_kept{t + 2}"))
                else:
                    pe.wait_ge(act_at.sem, act_at.at(f"k_kept{t - 2}"))
                for b in range(QB):
                    tr = nc.tensor.transpose(aux[:, 2 + t % 2, b * P:(b + 1) * P], zT[:, 4 + t, b * P:(b + 1) * P], ident)
                A.done(f"k_turned{t}", tr)

            def pool_product(g):
                pe.wait_ge(at["pool"].sem, at["pool"].at(f"pool{g}"))
                pe.wait_ge(dve_at.sem, dve_at.at(f"tail_p{g}"))
                if g == 0:
                    pe.wait_ge(pool_in, 32)
                    pe.wait_ge(rstd_made, 1)
                else:
                    pe.wait_ge(dve_at.sem, dve_at.at(f"pool_lo{g - 1}"))
                for b in range(2):
                    mm = nc.tensor.matmul(auxv(0)[:, b], wpool[:, g], pooled[:, g % 2, b * TH:(b + 1) * TH], start=True, stop=True)
                A.done(f"pooled{g}", mm)

            for n in range(16):
                product(N_IN_A + n, n % 2, KD, h_hi, h_lo, **(normed(0) if n == 0 else {}))
                if n == 0:
                    norm_sum(0)
                if n == 4:
                    pe.wait_ge(acc_read, 4)
                    pe.wait_ge(up["dve"].sem, up["dve"].all())
                    for t in range(4):
                        tr = nc.tensor.transpose(aux[0:POOL_HIST + NS, 2, t * P:(t + 1) * P], zT[:, 12 + t, SEQ - POOL_HIST:T], ident)
                    A.done("u_turned", tr)
                    pe.wait_ge(hist_in, 16)
                    for g in range(4):
                        tr = nc.tensor.transpose(aux[:, 3, g * 120:(g + 1) * 120], hist_rows[0:120, g * P:(g + 1) * P], ident[0:120, 0:120])
                    A.done("hist_turned", tr)
                if 5 <= n < 9:
                    turn_v(n - 5)
                if 9 <= n < 13:
                    turn_k(n - 9)
                if n in (7, 8, 10, 12):
                    pool_product((7, 8, 10, 12).index(n))

            pe.wait_ge(acc_read, 16)
            for r in range(3):
                for t in range(4):
                    tr = nc.tensor.transpose(acc[0:NS, r, t * P:(t + 1) * P], zT[:, 4 * r + t, SEQ:T], ident)
            A.done("z_turned", tr)
            pe.wait_ge(dve_at.sem, dve_at.at("pool_lo3"))
            pe.wait_ge(act_at.sem, act_at.at("k_kept3"))

            def scores(h, b):
                rows_h = slice(HD * (h % 2), HD * (h % 2) + HD)
                if h or b >= 2:
                    hh, bb = (h, b - 2) if b >= 2 else (h - 1, b + 2)
                    pe.wait_ge(dve_at.sem, dve_at.at(f"max{hh}{bb}"))
                A.done(f"scores{h}{b}", nc.tensor.matmul(
                    aux[:, b % 2, 0:(b + 1) * P], zT[rows_h, h // 2, b * P:(b + 1) * P],
                    zT[rows_h, 4 + h // 2, 0:(b + 1) * P], start=True, stop=True))

            def turn_probs(h, b):
                pe.wait_ge(act_at.sem, act_at.at(f"exp{h}{b}"))
                if h or b >= 2:
                    last_at = dve_at if b % 2 else act_at
                    pe.wait_ge(last_at.sem, last_at.at(f"pT{h}{b - 2}" if b >= 2 else f"pT{h - 1}{b + 2}"))
                if h and h % 2 == 0 and b == 0:
                    pe.wait_ge(dve_at.sem, dve_at.at(f"g_lo{h // 2 - 1}"))
                off = P * b * (b + 1) // 2
                for k in range(b + 1):
                    tr = nc.tensor.transpose(turned_bank(b)[:, k * P:(k + 1) * P], prob[:, h % 2, off + k * P:off + (k + 1) * P], ident)
                A.done(f"p_turned{h}{b}", tr)

            def weigh(h, b):
                made = dve_at if b % 2 else act_at
                pe.wait_ge(made.sem, made.at(f"pT{h}{b}"))
                if h and b == 0:
                    pe.wait_ge(dve_at.sem, dve_at.at(f"o{h - 1}"))
                for k in range(b + 1):
                    mm = nc.tensor.matmul(aux[:, 3, b * HD:(b + 1) * HD], probT[:, b % 2, k * P:(k + 1) * P],
                                          v_tok[:, k, h * HD:(h + 1) * HD], start=k == 0, stop=k == b)
                A.done(f"pv{h}{b}", mm)

            def samples(h, b):
                if (h, b) in spread_at:
                    sample = spread_at[h, b]
                    if sample == 0:
                        pe.wait_ge(sel_in, 32)
                        pe.wait_ge(dve_at.sem, dve_at.at("z_kept"))
                    if sample >= 2:
                        pe.wait_ge(dve_at.sem, dve_at.at(f"prod_b{sample - 2}"))
                    A.done(f"q_spread{sample}", nc.tensor.matmul(acc[:, sample % 2, 0:A_W], sel8[0:NS, sample], z_tok[0:NS, 0], start=True, stop=True))
                if (h, b) == (4, 0):
                    pe.wait_ge(dve_at.sem, dve_at.at(f"sum_b{NS - 1}"))
                    nc.tensor.transpose(acc[0:64, 3, 0:KEYS_A], dec_s[:, 0], ident)
                    A.done("s_turned", nc.tensor.transpose(acc[0:64, 3, KEYS_A:KEYS], dec_s[0:KEYS_B + 1, 1], ident[0:KEYS_B + 1, 0:KEYS_B + 1]))
                if (h, b) == (5, 0):
                    pe.wait_ge(dve_at.sem, dve_at.at("dec_norm"))
                    nc.tensor.transpose(acc[:, 3, 0:64], dec_p[0:64, 0:KEYS_A], ident[0:64, 0:64])
                    A.done("dp_turned", nc.tensor.transpose(acc[0:KEYS_B + 1, 3, 64:128], dec_p[0:64, KEYS_A:KEYS], ident[0:64, 0:64]))
                sample = 4 * (h - 5) + b - 2
                if 0 <= sample < NS:
                    if sample == 0:
                        pe.wait_ge(dve_at.sem, dve_at.at("dec_pT"))
                        pe.wait_ge(cv_in, 96)
                    if sample == 4:
                        pe.wait_ge(cv2_in, 96)
                    vals = cv if sample < 4 else ck
                    for t in range(4):
                        c = (t * NS + sample) * 2
                        two = slice(sample * HEADS + 2 * t, sample * HEADS + 2 * t + 2)
                        nc.tensor.matmul(acc[:, 0, c:c + 2], vals[:, sample % 4, 0, t * P:(t + 1) * P], dec_pT[:, 0, two], start=True, stop=False)
                        mm = nc.tensor.matmul(acc[:, 0, c:c + 2], vals[0:KEYS_B + 1, sample % 4, 1, t * P:(t + 1) * P],
                                              dec_pT[0:KEYS_B + 1, 1, two], start=False, stop=True)
                    if sample == NS - 1:
                        A.done("dec_out", mm)

            for h in range(HEADS + 1):
                for b in range(QB):
                    if h < HEADS:
                        scores(h, b)
                    if h:
                        turn_probs(h - 1, b)
                        if b:
                            weigh(h - 1, b - 1)
                    samples(h, b)
                if h:
                    weigh(h - 1, QB - 1)
                    if h % 2 == 0:
                        t = h // 2 - 1
                        pe.wait_ge(dve_at.sem, dve_at.at(f"o{h - 1}"))
                        pe.wait_ge(act_at.sem, act_at.at(f"pT{h - 1}2"))
                        for b in range(QB):
                            tr = nc.tensor.transpose(aux[:, 2, b * P:(b + 1) * P], o_tok[:, b], ident)
                        A.done(f"o_turned{t}", tr)
            pe.wait_ge(act_at.sem, act_at.all())
            pe.wait_ge(dve_at.sem, dve_at.all())
            for n in range(KD):
                product(N_OUT_A + n, n % 2, KD, g_hi, g_lo)
            ffn(1, N_FFN0, 0)

            R = pre["pe"]
            G, A, B = gg["pe"], ga["pe"], gb["pe"]

            def product_sixth(n, slot, j):
                if j == 0:
                    pe.wait_ge(acc_read, n - 1)
                    pe.wait_ge(w_hi_made, n + 1)
                if j == 4:
                    pe.wait_ge(w_lo_made, n + 1)
                w, x = ((w_hi, h_hi), (w_hi, h_lo), (w_lo, h_hi))[j // 2]
                for k in range(4 * (j % 2), 4 * (j % 2) + 4):
                    if isinstance(n, int) and n == N_IN_C and j < 4:
                        pe.wait_ge(*normed(2)["hi_at" if j < 2 else "lo_at"](k))
                    for b in range(2):
                        last = nc.tensor.matmul(acc[:, 2 * slot + b, 0:TH], w[:, slot, k * P:(k + 1) * P],
                                                x[:, k, b * TH:(b + 1) * TH], start=j == 0 and k == 0, stop=j == 5 and k == KD - 1)
                if j == 5:
                    last.then_inc(acc_full, 1)

            for j in range(6):
                product_sixth(N_IN_C, 0, j)
            norm_sum(2)
            pe.wait_ge(pre["dve"].sem, pre["dve"].at("wab_lo"))
            for w, x, part in ((wab_hi, h_hi, 0), (wab_hi, h_lo, 1), (wab_lo, h_hi, 2)):
                pe.wait_ge(h_hi_made, KD * 3)
                pe.wait_ge(h_lo_made, KD * 3)
                for k in range(KD):
                    for b in range(2):
                        mm = nc.tensor.matmul(aux[0:64, 2 + b, 0:TH], w[:, k], x[:, k, b * TH:(b + 1) * TH],
                                              start=part == 0 and k == 0, stop=part == 2 and k == KD - 1)
            R.done("ab", mm)
            pe.wait_ge(rstd_made, 3)
            pe.wait_ge(crow_in, 16)
            for half in range(2):
                for t in range(12):
                    tile = 12 * half + t
                    tr = nc.tensor.transpose(aux[:, half, t * 24:(t + 1) * 24], crow[0:24, tile * P:(tile + 1) * P], ident[0:24, 0:24])
                R.done(f"chist{half}", tr)
            for j in range(6):
                product_sixth(N_IN_C + 1, 1, j)
            pe.wait_ge(pre["dve"].sem, pre["dve"].at("cum"))
            for c in range(QB):
                tr = nc.tensor.transpose(aux[:, 2, c * 64:(c + 1) * 64], rows[0:64, c * P:(c + 1) * P], ident[0:64, 0:64])
            R.done("rows_turned", tr)
            pe.wait_ge(pre["dve"].sem, pre["dve"].at("tokcols"))

            def out_third(m, part, heads):
                if part == 0 and heads[0] == 0:
                    pe.wait_ge(acc_read, N_OUT_C + m - 1)
                    pe.wait_ge(w_hi_made, N_OUT_C + m + 1)
                    for e in ("act", "dve"):
                        pe.wait_ge(gb[e].sem, gb[e].all(GH - 1))
                if part == 2 and heads[0] == 0:
                    pe.wait_ge(w_lo_made, N_OUT_C + m + 1)
                w, x = ((w_hi, g_hi), (w_hi, g_lo), (w_lo, g_hi))[part]
                for k in heads:
                    for b in range(2):
                        last = nc.tensor.matmul(acc[:, 2 * m + b, 0:TH], w[:, m, k * P:(k + 1) * P], x[:, k, b * TH:(b + 1) * TH],
                                                start=part == 0 and k == 0, stop=part == 2 and k == GH - 1)
                return last

            def turn(it, g_on, a_on, b_on):
                ha, hb = it - 1, it - 2

                def wait(steps, name, h):
                    pe.wait_ge(steps.sem, steps.at(name, h))

                def weights_product(j):
                    if g_on and (a_on or j >= 12):
                        if j == 6 and a_on:
                            wait(ga["dve"], "z_v", ha)
                        if j in (12, 18):
                            wait(gg["dve"], "z_q" if j == 12 else "z_k", it)
                        product_sixth(N_IN_C + 4 * it + j // 6, j // 6 % 2, j % 6)
                    if not a_on and not g_on and j < 12:
                        out_third(j // 6, j // 2 % 3, range(4, GH - 1) if j % 2 else range(4))

                def tail_rows(stage, h, name, n, zslot, slot):
                    pe.wait_ge(acc_read, n + 1)
                    stage.done(f"tail_{name}", nc.tensor.transpose(acc[0:11, 2 * slot, TH:TH + P], zc[:, zslot, SEQ:CONV - 1 + T], ident))

                def spread(name, lhs, rhs):
                    for b in range(2):
                        mm = nc.tensor.matmul(aux[:, b, 0:TH], lhs, rhs[:, b * TH:(b + 1) * TH], start=True, stop=True)
                    A.done(name, mm)

                def by_chunk(name, bank, lhs, rhs):
                    for c in range(QB):
                        mm = nc.tensor.matmul(aux[:, bank, c * P:(c + 1) * P], lhs(c), rhs(c), start=True, stop=True)
                    A.done(name, mm)

                def turned(name, bank, src):
                    for c in range(QB):
                        tr = nc.tensor.transpose(aux[:, bank, c * P:(c + 1) * P], src(c), ident)
                    A.done(name, tr)

                def cols(x):
                    return lambda c: x[:, c * P:(c + 1) * P]

                def by_half(name, bank, n, lhs, x, second=False):
                    for c in range(QB):
                        mm = nc.tensor.matmul(aux[:, bank, c * P // 2:(c + 1) * P // 2].rearrange("p (k s) -> p k s", s=1 << n), lhs(c),
                                              half_cols(x[:, c:c + 1], n, second), start=True, stop=True)
                    A.done(name, mm)

                def level_p(n):
                    if not a_on:
                        return
                    wait(ga["act"], "tinv" if n == 1 else f"t{n - 1}", ha)
                    wait(ga["pool"], f"lev{n}", ha)
                    by_half(f"p{n}", 0, n, lambda c: lev[:, n % 2, c], tinv)
                    if n > 1:
                        turned(f"u{n - 1}", 1, lambda c: tinv[:, c])

                def level_t(n):
                    if not a_on:
                        return
                    wait(ga["dve"], f"ip{n}", ha)
                    if n > 1:
                        wait(ga["dve"], f"u{n - 1}", ha)
                    if n < NL - 1:
                        by_half(f"t{n}", 1, n, lambda c: tinvT[:, c], ip[:, n - 1])
                    else:
                        by_half(f"u{n}", 0, n, lambda c: ip[:, n - 1, c], tinvT, True)

                def chunk_k(c):
                    if b_on:
                        wait(gb["dve"], f"s{c - 1}", hb)
                        B.done(f"ks{c}", nc.tensor.matmul(aux[:, 2, 0:P], kbg[:, c * P:(c + 1) * P], state[:], start=True, stop=True))

                def chunk_v(c):
                    if b_on:
                        if c:
                            wait(gb["dve"], f"r{c}", hb)
                        B.done(f"v{c}", nc.tensor.matmul(aux[:, 2, P:2 * P], t_all[:, c], resid[:] if c else vb[:, 0], start=True, stop=True))

                def chunk_o(c):
                    if b_on:
                        wait(gb["act"], f"v{c}", hb)
                        if c:
                            nc.tensor.matmul(aux[:, 3, c * P:(c + 1) * P], state[:], qg[:, c * P:(c + 1) * P], start=True, stop=False)
                        B.done(f"o{c}", nc.tensor.matmul(aux[:, 3, c * P:(c + 1) * P], vnew[:], attT[:, c], start=c == 0, stop=True))
                        B.done(f"s{c}", nc.tensor.matmul(aux[:, 2, 2 * P:3 * P], kdec[:, c], vnew[:], start=True, stop=True))

                weights_product(0)
                weights_product(1)
                if a_on:
                    wait(ga["pool"], "rowsel", ha)
                    if b_on:
                        wait(ga["dve"], "attT", hb)
                    spread("gc", delta[0:64, G_HALF + P:G_HALF + 2 * P], rowsel[0:64])
                if b_on:
                    pe.wait_ge(ga["dve"].sem, ga["dve"].all(it - 1))
                    pe.wait_ge(ga["act"].sem, ga["act"].all(it - 1))
                chunk_v(0)
                weights_product(2)
                if a_on:
                    wait(ga["act"], "egb", ha)
                    spread("beta", delta[0:64, G_HALF:G_HALF + P], rowsel[0:64])
                chunk_o(0)
                weights_product(3)
                if a_on:
                    wait(ga["act"], "sq_q", ha)
                    wait(ga["dve"], "betab", ha)
                    spread("ss_q", ones, sqg[:, 0])
                chunk_k(1)
                if a_on:
                    wait(gg["dve"], "z_k", ha)
                    tail_rows(A, ha, "v", N_IN_C + 4 * ha + 3, 2, 1)
                weights_product(4)
                if a_on:
                    wait(ga["act"], "ln_q", ha)
                    spread("ss_k", ones, sqg[:, 1])
                chunk_v(1)
                weights_product(5)
                chunk_o(1)
                weights_product(6)
                chunk_k(2)
                weights_product(7)
                if a_on:
                    wait(ga["dve"], "kn", ha)
                    by_chunk("kk", 0, cols(kn), cols(kn))
                chunk_v(2)
                if g_on:
                    tail_rows(G, it, "q", N_IN_C + 4 * it, 0, 0)
                weights_product(8)
                chunk_o(2)
                weights_product(9)
                if a_on:
                    wait(ga["dve"], "one", ha)
                    turned("t_turned", 1, lambda c: tinvT[:, c])
                chunk_k(3)
                weights_product(10)
                level_p(1)
                chunk_v(3)
                weights_product(11)
                level_t(1)
                chunk_o(3)
                weights_product(12)
                level_p(2)
                if b_on:
                    pe.wait_ge(s_read, 16 * hb + 16)
                    wait(gb["dve"], f"s{QB - 1}", hb)
                    for b in range(NS):
                        mm = nc.tensor.matmul(aux[:, 2, 2 * b:2 * b + 2], s_in[:, b], kq[:, b], start=True, stop=True)
                    B.done("dx", mm)
                    B.done("dqk", nc.tensor.matmul(aux[:, 2, 2 * NS:3 * NS], ones, sm[:, 0], start=True, stop=True))
                    B.done("dk_turned", nc.tensor.transpose(aux[0:NS, 2, P:2 * P], sm[:, 4], ident))
                weights_product(13)
                level_t(2)
                if g_on:
                    tail_rows(G, it, "k", N_IN_C + 4 * it + 1, 1, 1)
                weights_product(14)
                level_p(3)
                if b_on:
                    wait(gb["dve"], "do", hb)
                    B.done("dv_turned", nc.tensor.transpose(aux[0:NS, 2, 2 * P:3 * P], sm[:, 2], ident))
                weights_product(15)
                level_t(3)
                if b_on:
                    wait(gb["act"], "o_sq", hb)
                    wait(gb["dve"], "d_rows", hb)
                    for b in range(2):
                        mm = nc.tensor.matmul(auxv(1)[:, b], ones, osq[:, b * TH:(b + 1) * TH], start=True, stop=True)
                    B.done("osum", mm)
                weights_product(16)
                level_p(4)
                if b_on:
                    wait(gb["dve"], "dvexp", hb)
                    wait(gb["act"], "o_ln", hb)
                    for b in range(2):
                        mm = nc.tensor.matmul(aux[:, 2 + b], kv_rows[0:NS, 0], dvexp[0:NS, b], start=True, stop=True)
                    B.done("outer", mm)
                weights_product(17)
                level_t(4)
                weights_product(18)
                level_p(5)
                weights_product(19)
                level_t(5)
                if a_on:
                    if b_on:
                        wait(gb["dve"], "s_new", hb)
                    turned("turn_k", 3, cols(kn))
                weights_product(20)
                level_p(6)
                if a_on:
                    wait(ga["act"], "silu_v", ha)
                    turned("turn_v", 2, cols(y[:, 2]))
                weights_product(21)
                level_t(6)
                weights_product(22)
                if a_on:
                    by_chunk("qk", 1, cols(kn), cols(qn))
                weights_product(23)

            turn(0, True, False, False)
            turn(1, True, True, False)
            with pe.Fori(2, GH) as it:
                turn(it, True, True, True)
            turn(GH, False, True, True)
            turn(GH + 1, False, False, True)
            for e in ("dve", "act"):
                pe.wait_ge(gb[e].sem, gb[e].all(GH))
            for m in range(2):
                for part in range(3):
                    last = out_third(m, part, [GH - 1])
                last.then_inc(acc_full, 1)
            with pe.Fori(1, KD // 2) as i:
                for s in range(2):
                    product(N_OUT_C + 2 * i + s, s, KD, g_hi, g_lo)
            ffn(3, N_FFN1, FT)
            Z, fd, fa = fin["pe"], fin["dve"], fin["act"]
            banks = [acc[:, 0:2], acc[:, 2:4], aux[:, 0:2], acc[:, 0:2], acc[:, 2:4]]
            pe.wait_ge(y_fin_made, KD)
            pe.wait_ge(acc_read, N_ALL)
            pe.wait_ge(rstd_made, 4)
            for b in range(QB + 1):
                rows_b = P if b < QB else NS
                if b == 3:
                    pe.wait_ge(ss_added, KD * 5)
                    for c in range(QB + 1):
                        rows_c = P if c < QB else NS
                        mm = nc.tensor.matmul(aux[0:rows_c, 2, 2 * c:2 * c + 2], ssum[:, c * P:c * P + rows_c], ones[:, 0:2], start=True, stop=True)
                    Z.done("sums", mm)
                    pe.wait_ge(fd.sem, fd.at("y_tok0"))
                if b == 4:
                    pe.wait_ge(fa.sem, fa.at("y_tok1"))
                for m in range(KD):
                    tr = nc.tensor.transpose(banks[b][0:rows_b, m // 4, (m % 4) * P:(m % 4 + 1) * P], y_fin[:, m, b * P:b * P + rows_b], ident)
                Z.done(f"y{b}", tr)

        @block.scalar
        def _(act):
            def convert(n, slot, turn):
                act.wait_ge(w_loaded[slot], 16 * turn + 16)
                if not isinstance(n, int) or n >= 2:
                    act.wait_ge(acc_full, n - 1)
                nc.scalar.activation(w_hi[:, slot], w_raw[:, slot], ACT.Copy).then_inc(w_hi_made, 1)

            def gamma(k, m):
                return column(par, KD * NORM_ROWS[k] + m)

            def norm_tile(k, m, slot, x_sem, x_at):
                if k or not isinstance(m, int) or m >= 2:
                    act.wait_ge(ss_added, KD * k + m - 1)
                act.wait_ge(x_sem, x_at)
                apart(act)
                if k < 4:
                    nc.scalar.activation(h_hi[:, m], xT[:, m], ACT.Copy, scale=gamma(k, m)).then_inc(h_hi_made, 1)
                nc.scalar.activation(sq[:, slot], xT[:, m], ACT.Square).then_inc(sq_made, 1)
                if k == 4:
                    nc.scalar.activation(y_fin[:, m], xT[:, m], ACT.Copy, scale=gamma(k, m)).then_inc(y_fin_made, 1)

            def norm_factor(k):
                nc.scalar.preload_act_table_set("natural_log_exp_and_others")
                act.wait_ge(ss_full, k + 1)
                nc.scalar.activation(halves(rstd), auxv(0), ACT.Ln, bias=eps_col, scale=1.0 / D_MODEL).then_inc(ln_made, 1)
                act.wait_ge(ln_made, k + 1)
                nc.scalar.activation(rstd[:], rstd[:], ACT.Exp, scale=-0.5).then_inc(rstd_made, 1)

            def ffn(k, base, g_base):
                convert(base + 1, 1, base // 2)
                norm_factor(k)
                nc.scalar.preload_act_table_set("silu_and_others")
                for part, kt in enumerate(PARTS):
                    def gate_up(i, converted=False):
                        n = base + 2 * i
                        if not converted:
                            convert(n + 1, 1, base // 2 + i)
                        act.wait_ge(acc_read, n + 1)
                        nc.scalar.activation(gate_s[:], gate_n[:], ACT.Silu).then_inc(silu_made, 1)
                        convert(n + 2, 0, base // 2 + i + 1)
                        act.wait_ge(gu_made, g_base + i + 1)
                        apart(act)
                        nc.scalar.activation(g_hi[:, i], gu[:], ACT.Copy).then_inc(g_hi_made, 1)

                    if part == 0:
                        gate_up(0, True)
                    with act.Fori(0 if part else 1, kt) as i:
                        gate_up(i)
                    base += 2 * kt
                    g_base += kt

                    def down(i, last):
                        for s in range(2):
                            n = base + 2 * i + s
                            if not last:
                                convert(n + 1, 1 - s, base // 2 + i + s)
                            if part == 2:
                                norm_tile(k + 1, 2 * i + s, s, acc_read, n + 1)

                    with act.Fori(0, KD // 2 - 1) as i:
                        down(i, False)
                    i = KD // 2 - 1
                    if base + KD < N_ALL:
                        down(i, False)
                    else:
                        convert(base + KD - 1, 1, base // 2 + i)
                        for s in range(2):
                            norm_tile(k + 1, 2 * i + s, s, acc_read, base + 2 * i + s + 1)
                    base += KD

            act.dma_start(const[:], a["const_table"]).then_inc(const_in, 16)
            act.dma_start(par_rows[0:45, 0], a["par_rows"]).then_inc(par_in, 16)
            act.dma_start(par_rows[0:96, 1], a["w_conv_c"][0].rearrange("i (t p) -> (i t) p", p=P)).then_inc(par_in, 16)
            act.dma_start(xs_tok[0:NS, :], a["x_sample"].rearrange("b t d -> (b t) d")).then_inc(xs_in, 16)
            nc.scalar.preload_act_table_set("natural_log_exp_and_others")
            convert(0, 0, 0)
            act.wait_ge(up["dve"].sem, up["dve"].at("par"))
            for m in range(KD):
                norm_tile(0, m, m % 2, up["dve"].sem, up["dve"].at(f"x{m}"))
            convert(N_IN_A + 1, 1, 0)
            norm_factor(0)
            A, pe_at, dve_at = at["act"], at["pe"], at["dve"]
            for n in range(16):
                if n:
                    convert(N_IN_A + n + 1, (n + 1) % 2, (n + 1) // 2)
                for name in in_a_act.get(n - 1, []):
                    x = int(name[-1])
                    if name.startswith("pool_hi"):
                        act.wait_ge(pe_at.sem, pe_at.at(f"pooled{x}"))
                        A.done(name, nc.scalar.activation(halves(g_hi[:, 4 + x]), auxv(0), ACT.Copy, scale=par[:, 40 + x:41 + x]))
                    else:
                        act.wait_ge(pe_at.sem, pe_at.at(f"k_turned{x}"))
                        if x >= 2:
                            act.wait_ge(k_stored[x % 2], 16)
                        A.done(name, nc.scalar.activation(k_stage[:, x % 2].rearrange("p b m -> p (b m)"), aux[:, 2 + x % 2], ACT.Copy))

            for h in range(HEADS + 1):
                for b in range(QB):
                    off = P * b * (b + 1) // 2
                    if h < HEADS:
                        act.wait_ge(dve_at.sem, dve_at.at(f"neg{h}{b}"))
                        pr = prob[:, h % 2, off:off + (b + 1) * P]
                        A.done(f"exp{h}{b}", nc.scalar.activation(pr, pr, ACT.Exp, bias=att_col[:, h % 2, 1, b:b + 1],
                                                                 accum_out=att_col[:, h % 2, 2, b:b + 1]))
                    if h and b % 2 == 0:
                        act.wait_ge(pe_at.sem, pe_at.at(f"p_turned{h - 1}{b}"))
                        if b or h > 1:
                            act.wait_ge(pe_at.sem, pe_at.at(f"pv{h - 1}{b - 2}" if b else f"pv{h - 2}2"))
                        A.done(f"pT{h - 1}{b}", nc.scalar.activation(probT[:, 0, 0:(b + 1) * P], aux[:, 2, 0:(b + 1) * P], ACT.Copy))
                    if (h, b) == (4, 1):
                        act.wait_ge(dve_at.sem, dve_at.at("dec_neg"))
                        A.done("dec_exp", nc.scalar.activation(dec_p[0:64], dec_p[0:64], ACT.Exp, bias=dec_col[0:64, 1:2], accum_out=dec_col[0:64, 2:3]))
                    if (h, b) == (7, 2):
                        act.wait_ge(pe_at.sem, pe_at.at("dec_out"))
                        for r in range(2):
                            rows_r = slice(HD * r, HD * r + HD)
                            out = acc[rows_r, 0, 0:64].rearrange("p (t b r) -> p t b r", t=4, r=2)[:, :, :, r]
                            A.done(f"dec_hi{r}", nc.scalar.activation(g_hi[rows_r, 0:4, SEQ:T], out, ACT.Copy))
                if h and h % 2 == 0:
                    t = h // 2 - 1
                    act.wait_ge(pe_at.sem, pe_at.at(f"o_turned{t}"))
                    A.done(f"g_hi{t}", nc.scalar.activation(g_hi[:, t, 0:SEQ], aux[:, 2], ACT.Copy))
            for n in range(KD):
                convert(N_OUT_A + n + 1, (n + 1) % 2, (N_OUT_A + n + 1) // 2)
                norm_tile(1, n, n % 2, acc_read, N_OUT_A + n + 1)
            ffn(1, N_FFN0, 0)

            R = pre["act"]
            pre_dve = pre["dve"]
            act.wait_ge(pre["pool"].sem, pre["pool"].at("wab_pad_a"))
            R.done("wab_hi", nc.scalar.activation(wab_hi[:], wab_pad[:], ACT.Copy))
            convert(N_IN_C + 1, 1, N_IN_C // 2)
            norm_factor(2)
            act.wait_ge(pre_dve.sem, pre_dve.at("ab"))
            R.done("exp_b", nc.scalar.activation(abt[0:8, 0], ab[0:8], ACT.Exp, scale=-1.0))
            act.wait_ge(pre_dve.sem, pre_dve.at("abs"))
            R.done("exp_sp", nc.scalar.activation(abt[32:40, 1], abt[32:40, 1], ACT.Exp))
            act.wait_ge(R.sem, R.at("exp_sp"))
            R.done("ln_sp", nc.scalar.activation(abt[32:40, 1], abt[32:40, 1], ACT.Ln, bias=one_col[32:40]))
            R.done("exp_a", nc.scalar.activation(acol[32:40, 2:3], acol[32:40, 0:1], ACT.Exp))

            G, A, B = gg["act"], ga["act"], gb["act"]

            def turn(it, g_on, a_on, b_on):
                ha, hb = it - 1, it - 2
                n0 = N_IN_C + 4 * it

                def wait(steps, name, h):
                    act.wait_ge(steps.sem, steps.at(name, h))

                def to_t(n):
                    if a_on:
                        wait(ga["pe"], "t_turned" if n == 0 else f"t{n}", ha)
                        if n == 0:
                            A.done("tinv", nc.scalar.activation(tinv[:].rearrange("p c m -> p (c m)"), aux[:, 1], ACT.Copy))
                        else:
                            A.done(f"t{n}", nc.scalar.activation(half_cols(tinv, n), packed(1, n), ACT.Copy))

                def v_new(c):
                    if b_on:
                        wait(gb["pe"], f"v{c}", hb)
                        if c:
                            wait(gb["pe"], f"s{c - 1}", hb)
                        B.done(f"v{c}", nc.scalar.activation(vnew[:], aux[:, 2, P:2 * P], ACT.Copy))

                def last_tap(stage, name, r, h, zslot, n):
                    act.wait_ge(acc_read, n + 1)
                    apart(act)
                    stage.done(f"tap_{name}", nc.scalar.activation(y[:, r], zc[:, zslot, CONV - 1:], ACT.Copy,
                                                                   scale=column(wconv[:, CONV - 1], r * GH + h)))

                def silu(stage, name, h, out):
                    wait(ga["dve"] if name == "v" else gg["dve"], f"tap_{name}3", h)
                    stage.done(f"silu_{name}", nc.scalar.activation(out, out, ACT.Silu))

                nc.scalar.preload_act_table_set("natural_log_exp_and_others")
                if g_on and a_on:
                    convert(n0 + 1, 1, N_IN_C // 2 + 2 * it)
                if a_on:
                    if b_on:
                        wait(ga["pe"], "turn_v", hb)
                        wait(ga["dve"], "dvb", hb)
                    last_tap(A, "v", 2, ha, 2, n0 - 1)
                    wait(ga["pe"], "gc", ha)
                    A.done("gcb", nc.scalar.activation(halves(gcb), auxv(0), ACT.Copy))
                    A.done("egb", nc.scalar.activation(halves(egb), auxv(0), ACT.Exp))
                v_new(0)
                if a_on:
                    wait(gg["act"], "silu_k", ha)
                    A.done("sq_q", nc.scalar.activation(sqg[:, 0], y[:, 0], ACT.Square))
                    A.done("sq_k", nc.scalar.activation(sqg[:, 1], y[:, 1], ACT.Square))
                    for r, name in enumerate("qk"):
                        wait(ga["pe"], f"ss_{name}", ha)
                        A.done(f"ln_{name}", nc.scalar.activation(halves(rqk[:, r]), auxv(0), ACT.Ln, bias=eps_col))
                        wait(A, f"ln_{name}", ha)
                        A.done(f"rs_{name}", nc.scalar.activation(rqk[:, r], rqk[:, r], ACT.Exp, scale=-0.5, **({"bias": lnq_col} if r == 0 else {})))
                        if r == 0:
                            v_new(1)
                    wait(ga["pool"], "mask", ha)
                    A.done("decay", nc.scalar.activation(decay[:], decay[:], ACT.Exp))
                    wait(ga["dve"], "edk", ha)
                    A.done("edk", nc.scalar.activation(edk[:], edk[:], ACT.Exp))
                else:
                    v_new(1)
                v_new(2)
                if g_on:
                    convert(n0 + 2, 0, N_IN_C // 2 + 2 * it + 1)
                    if a_on:
                        wait(ga["dve"], "qn", ha)
                    last_tap(G, "q", 0, it, 0, n0)
                to_t(0)
                v_new(3)
                to_t(1)
                if b_on:
                    wait(gb["pe"], f"o{QB - 1}", hb)
                    B.done("oT", nc.scalar.activation(yo[:, 0:SEQ], aux[:, 3], ACT.Copy))
                if g_on:
                    convert(n0 + 3, 1, N_IN_C // 2 + 2 * it + 1)
                    if a_on:
                        wait(ga["dve"], "kn", ha)
                    last_tap(G, "k", 1, it, 1, n0 + 1)
                to_t(2)
                if b_on:
                    wait(B, "oT", hb)
                    wait(gb["dve"], "do", hb)
                    B.done("o_sq", nc.scalar.activation(osq, yo[:], ACT.Square))
                to_t(3)
                if b_on:
                    wait(gb["pe"], "osum", hb)
                    B.done("o_ln", nc.scalar.activation(halves(ors), auxv(1), ACT.Ln, bias=eps_col, scale=1.0 / P))
                    wait(B, "o_ln", hb)
                    B.done("o_rs", nc.scalar.activation(ors, ors, ACT.Exp, scale=-0.5))
                to_t(4)
                nc.scalar.preload_act_table_set("silu_and_others")
                if a_on:
                    silu(A, "v", ha, y[:, 2])
                if g_on:
                    silu(G, "q", it, y[:, 0])
                    silu(G, "k", it, y[:, 1])
                to_t(5)
                if a_on:
                    wait(ga["dve"], "kbg", ha)
                    if b_on:
                        wait(gb["pe"], "dx", hb)
                    A.done("kq_k", nc.scalar.activation(kq[:, :, 0], kbg[:, SEQ:T], ACT.Copy))
                    A.done("kq_q", nc.scalar.activation(kq[:, :, 1], qg[:, SEQ:T], ACT.Copy))
                if g_on:
                    convert(n0 + 4, 0, N_IN_C // 2 + 2 * it + 2)
                if b_on:
                    wait(gb["dve"], "og", hb)
                    apart(act)
                    B.done("g_hi", nc.scalar.activation(g_hi[:, hb], yo[:], ACT.Copy))
                if g_on:
                    act.wait_ge(acc_read, n0 + 3)
                    apart(act)
                    G.done("silu_g", nc.scalar.activation(gateT[:, it], gateT[:, it], ACT.Silu))

            turn(0, True, False, False)
            turn(1, True, True, False)
            with act.Fori(2, GH) as it:
                turn(it, True, True, True)
            turn(GH, False, True, True)
            convert(N_OUT_C + 1, 1, N_OUT_C // 2)
            turn(GH + 1, False, False, True)

            def out(i):
                for s in range(2):
                    n = N_OUT_C + 2 * i + s
                    if s or not isinstance(i, int):
                        convert(n + 1, 1 - s, N_OUT_C // 2 + i + s)
                    norm_tile(3, 2 * i + s, s, acc_read, n + 1)

            out(0)
            with act.Fori(1, KD // 2) as i:
                out(i)
            ffn(3, N_FFN1, FT)
            Z, zp = fin["act"], fin["pe"]
            nc.scalar.preload_act_table_set("natural_log_exp_and_others")
            act.wait_ge(zp.sem, zp.at("sums"))
            for name, fn, src_t, kw in (("ln", ACT.Ln, aux[:, 2], dict(bias=eps_col, scale=1.0 / D_MODEL)), ("rstd", ACT.Exp, r_tok, dict(scale=-0.5))):
                if name == "rstd":
                    act.wait_ge(Z.sem, Z.at("ln_s"))
                Z.done(name, nc.scalar.activation(r_tok[:, 0:2 * QB], src_t[:, 0:2 * QB], fn, **kw))
                if name == "ln":
                    kw = dict(bias=eps_col[0:NS], scale=1.0 / D_MODEL)
                Z.done(name + "_s", nc.scalar.activation(r_tok[0:NS, 2 * QB:2 * QB + 2], src_t[0:NS, 2 * QB:2 * QB + 2], fn, **kw))
            act.wait_ge(Z.sem, Z.at("rstd_s"))
            for b in (1, 3):
                act.wait_ge(zp.sem, zp.at(f"y{b}"))
                Z.done(f"y_tok{b}", nc.scalar.activation(y_tok[:, b], (acc[:, 2:4] if b == 1 else acc[:, 0:2]).rearrange("p a t -> p (a t)"),
                                                         ACT.Copy, scale=r_tok[:, 2 * b:2 * b + 1]))

        @block.vector
        def _(dve):
            def convert(n, slot):
                dve.wait_ge(w_hi_made, n + 1)
                nc.vector.tensor_tensor(w_lo[:, slot], w_raw[:, slot], w_hi[:, slot].bitcast(F32), ALU.subtract).then_inc(w_lo_made, 1)

            def norm_tile(k, m, x_sem=None, x_at=None):
                if k == 4:
                    return
                dve.wait_ge(h_hi_made, KD * k + m + 1)
                nc.vector.scalar_tensor_tensor(h_lo[:, m], xT[:, m], column(par, KD * NORM_ROWS[k] + m), h_hi[:, m].bitcast(F32),
                                               ALU.mult, ALU.subtract).then_inc(h_lo_made, 1)

            def add_to_stream(n, m, slot):
                dve.wait_ge(acc_full, n + 1)
                nc.vector.tensor_tensor(halves(xT[:, m]), accv(slot), halves(xT[:, m]), ALU.add).then_inc(acc_read, 1)

            def scaled(out, n, slot):
                dve.wait_ge(acc_full, n + 1)
                nc.vector.tensor_tensor(halves(out), accv(slot), halves(rstd), ALU.mult).then_inc(acc_read, 1)

            def ffn(k, base, g_base):
                convert(base + 1, 1)
                dve.wait_ge(rstd_made, k + 1)
                for part, kt in enumerate(PARTS):
                    def gate_up(i, converted=False):
                        n, g = base + 2 * i, g_base + i
                        if not converted:
                            convert(n + 1, 1)
                        scaled(gate_n, n, 0)
                        convert(n + 2, 0)
                        scaled(up_n, n + 1, 1)
                        dve.wait_ge(silu_made, g + 1)
                        dve.wait_ge(acc_read, n + 2)
                        nc.vector.tensor_tensor(gu[:], up_n[:], gate_s[:], ALU.mult).then_inc(gu_made, 1)
                        dve.wait_ge(g_hi_made, g + 1)
                        nc.vector.tensor_tensor(g_lo[:, i], gu[:], g_hi[:, i].bitcast(F32), ALU.subtract).then_inc(g_lo_made, 1)

                    if part == 0:
                        gate_up(0, True)
                    with dve.Fori(0 if part else 1, kt) as i:
                        gate_up(i)
                    base += 2 * kt
                    g_base += kt
                    with dve.Fori(0, KD // 2 - 1) as i:
                        for s in range(2):
                            convert(base + 2 * i + s + 1, 1 - s)
                            add_to_stream(base + 2 * i + s, 2 * i + s, s)
                            if part == 2:
                                norm_tile(k + 1, 2 * i + s)
                    i = KD // 2 - 1
                    for s in range(2):
                        if base + 2 * i + s + 1 < N_ALL:
                            convert(base + 2 * i + s + 1, 1 - s)
                        add_to_stream(base + 2 * i + s, 2 * i + s, s)
                        if part == 2:
                            norm_tile(k + 1, 2 * i + s)
                    base += KD

            U, upe = up["dve"], up["pe"]
            dve.wait_ge(upe.sem, upe.at("par"))
            U.done("par", nc.vector.tensor_copy(par[:, 0:45], aux[:, 3, 0:45]))
            U.done("wconv", nc.vector.tensor_copy(wconv[:].rearrange("p i t -> p (i t)"), aux[:, 3, 64:160]))
            dve.wait_ge(upe.sem, upe.at("xs"))
            U.done("xs", nc.vector.tensor_copy(xT[:, :, SEQ:T], aux[:, 2, 0:64].rearrange("p (m t) -> p m t", t=NS)))
            for m in range(KD):
                dve.wait_ge(upe.sem, upe.at(f"x{m}"))
                U.done(f"x{m}", nc.vector.tensor_copy(xT[:, m, 0:SEQ], aux[:, m % 2]))
            dve.wait_ge(U.sem, U.all())
            convert(0, 0)
            for m in range(KD):
                norm_tile(0, m)
            convert(N_IN_A + 1, 1)
            dve.wait_ge(rstd_made, 1)
            A, pe_at, act_at, pool_at = at["dve"], at["pe"], at["act"], at["pool"]

            def tail_means(g):
                w = POOL_WINDOWS[g]
                A.done(f"tail{g}", nc.vector.tensor_reduce(tail[:], histT[:, g, :, POOL_HIST - (w - 1):POOL_HIST], AX.X, ALU.add))
                dve.wait_ge(A.sem, A.at(f"tail{g}"))
                A.done(f"tail_sum{g}", nc.vector.tensor_tensor(tail[:], tail[:], zT[:, 12 + g, SEQ:T], ALU.add))
                dve.wait_ge(A.sem, A.at(f"tail_sum{g}"))
                if g >= 2:
                    dve.wait_ge(pe_at.sem, pe_at.at(f"pooled{g - 2}"))
                A.done(f"tail_p{g}", nc.vector.scalar_tensor_tensor(pooled[:, g % 2, SEQ:T], tail[:], 1.0 / w, zT[:, 12 + g, SEQ:T], ALU.mult, ALU.subtract))
                dve.wait_ge(A.sem, A.at(f"tail_p{g}"))

            for n in range(16):
                if n:
                    convert(N_IN_A + n + 1, (n + 1) % 2)
                scaled(zT[:, IN_A_TILES[n]], N_IN_A + n, n % 2)
                if n == 4:
                    dve.wait_ge(pe_at.sem, pe_at.at("u_turned"))
                    A.done("u_kept", nc.vector.tensor_copy(u_tok[0:23], aux[0:23, 2]))
                    dve.wait_ge(pe_at.sem, pe_at.at("hist_turned"))
                    A.done("histT", nc.vector.tensor_copy(histT[:].rearrange("p g b j -> p (g b j)"), aux[:, 3, 0:480]))
                    dve.wait_ge(A.sem, A.at("histT"))
                if 5 <= n < 9:
                    t = n - 5
                    dve.wait_ge(pe_at.sem, pe_at.at(f"v_turned{t}"))
                    A.done(f"v_kept{t}", nc.vector.tensor_copy(v_tok[:, :, t * P:(t + 1) * P], blocks(aux[:, 2 + t % 2])))
                if n in (8, 9, 11, 13):
                    g = (8, 9, 11, 13).index(n)
                    dve.wait_ge(act_at.sem, act_at.at(f"pool_hi{g}"))
                    A.done(f"pool_lo{g}", nc.vector.scalar_tensor_tensor(halves(g_lo[:, 4 + g]), auxv(0), par[:, 40 + g:41 + g],
                                                                        halves(g_hi[:, 4 + g].bitcast(F32)), ALU.mult, ALU.subtract))
                if n in (5, 6, 8, 9):
                    tail_means((5, 6, 8, 9).index(n))
            dve.wait_ge(pe_at.sem, pe_at.at("z_turned"))
            A.done("z_kept", nc.vector.tensor_copy(z_tok[0:NS], acc[0:NS, 0:3]))

            def samples(h, b):
                if (h, b) in spread_at:
                    n = spread_at[h, b]
                    dve.wait_ge(pe_at.sem, pe_at.at(f"q_spread{n}"))
                    if n == 0:
                        dve.wait_ge(ck_in, 32)
                        dve.wait_ge(self_in, 64)
                    if n == 4:
                        dve.wait_ge(ck2_in, 32)
                        dve.wait_ge(self2_in, 64)
                    ext = (P, KEYS_B + 1)
                    for x in range(2):
                        if n:
                            dve.wait_ge(A.sem, A.at(f"sum_{'ab'[x]}{n - 1}"))
                        A.done(f"prod_{'ab'[x]}{n}", nc.vector.tensor_tensor(prod[0:ext[x], x], acc[0:ext[x], n % 2], ck[0:ext[x], n % 4, x], ALU.mult))
                    for x in range(2):
                        dve.wait_ge(A.sem, A.at(f"prod_{'ab'[x]}{n}"))
                        A.done(f"sum_{'ab'[x]}{n}", nc.vector.tensor_reduce(
                            dec_s[0:ext[x], x, n * HEADS:(n + 1) * HEADS], prod[0:ext[x], x].rearrange("p (h d) -> p h d", d=HD), AX.X, ALU.add))
                if (h, b) == (4, 0):
                    dve.wait_ge(pe_at.sem, pe_at.at("s_turned"))
                    dve.wait_ge(sel_in, 32)
                    A.done("dec_max", nc.vector.tensor_tensor_reduce(out=dec_p[0:64], in0=acc[0:64, 3, 0:KEYS], in1=dec_tab[0:64], scale=0.125, scalar=NEG,
                                                                     op0=ALU.add, op1=ALU.max, accum_out=dec_col[0:64, 0:1]))
                    dve.wait_ge(A.sem, A.at("dec_max"))
                    A.done("dec_neg", nc.vector.tensor_scalar(dec_col[0:64, 1:2], dec_col[0:64, 0:1], -1.0, None, ALU.mult))
                if (h, b) == (4, 2):
                    dve.wait_ge(act_at.sem, act_at.at("dec_exp"))
                    A.done("dec_inv", nc.vector.reciprocal(dec_col[0:64, 3:4], dec_col[0:64, 2:3]))
                    dve.wait_ge(A.sem, A.at("dec_inv"))
                    A.done("dec_norm", nc.vector.tensor_scalar(dec_p[0:64], dec_p[0:64], dec_col[0:64, 3:4], None, ALU.mult))
                if (h, b) == (5, 0):
                    dve.wait_ge(pe_at.sem, pe_at.at("dp_turned"))
                    nc.vector.tensor_copy(dec_pT[:, 0], acc[:, 3, 0:64])
                    A.done("dec_pT", nc.vector.tensor_copy(dec_pT[0:KEYS_B + 1, 1], acc[0:KEYS_B + 1, 3, 64:128]))
                if (h, b) == (7, 3):
                    for r in range(2):
                        rows_r = slice(HD * r, HD * r + HD)
                        out = acc[rows_r, 0, 0:64].rearrange("p (t b r) -> p t b r", t=4, r=2)[:, :, :, r]
                        dve.wait_ge(act_at.sem, act_at.at(f"dec_hi{r}"))
                        A.done(f"dec_lo{r}", nc.vector.tensor_tensor(g_lo[rows_r, 0:4, SEQ:T], out, g_hi[rows_r, 0:4, SEQ:T].bitcast(F32), ALU.subtract))

            dve.wait_ge(tab_in, 16)
            for h in range(HEADS + 1):
                if h < HEADS:
                    if h:
                        dve.wait_ge(A.sem, A.at(f"max{h - 1}3"))
                    A.done(f"bias{h}", nc.vector.scalar_tensor_tensor(bias[:], att_tab[:, 0], -8.0 * slope(h), att_tab[:, 1], ALU.mult, ALU.add))
                    dve.wait_ge(A.sem, A.at(f"bias{h}"))
                for b in range(QB):
                    off = P * b * (b + 1) // 2
                    if h < HEADS:
                        dve.wait_ge(pe_at.sem, pe_at.at(f"scores{h}{b}"))
                        if h >= 2:
                            dve.wait_ge(pe_at.sem, pe_at.at(f"p_turned{h - 2}{b}"))
                        A.done(f"max{h}{b}", nc.vector.tensor_tensor_reduce(
                            out=prob[:, h % 2, off:off + (b + 1) * P], in0=aux[:, b % 2, 0:(b + 1) * P],
                            in1=bias[:, (3 - b) * P:SEQ], scale=0.125, scalar=NEG, op0=ALU.add, op1=ALU.max,
                            accum_out=att_col[:, h % 2, 0, b:b + 1]))
                        dve.wait_ge(A.sem, A.at(f"max{h}{b}"))
                        A.done(f"neg{h}{b}", nc.vector.tensor_scalar(att_col[:, h % 2, 1, b:b + 1], att_col[:, h % 2, 0, b:b + 1], -1.0, None, ALU.mult))
                    if h and b % 2:
                        dve.wait_ge(pe_at.sem, pe_at.at(f"p_turned{h - 1}{b}"))
                        if b == 3 or h > 1:
                            dve.wait_ge(pe_at.sem, pe_at.at(f"pv{h - 1}1" if b == 3 else f"pv{h - 2}3"))
                        A.done(f"pT{h - 1}{b}", nc.vector.tensor_copy(probT[:, 1, 0:(b + 1) * P], turned_bank(b)[:, 0:(b + 1) * P]))
                    samples(h, b)
                if h:
                    hp, par_h = h - 1, (h - 1) % 2
                    dve.wait_ge(act_at.sem, act_at.at(f"exp{hp}3"))
                    A.done(f"inv{hp}", nc.vector.reciprocal(att_col[:, par_h, 3], att_col[:, par_h, 2]))
                    dve.wait_ge(A.sem, A.at(f"inv{hp}"))
                    dve.wait_ge(pe_at.sem, pe_at.at(f"pv{hp}3"))
                    if hp % 2 == 0 and hp:
                        dve.wait_ge(pe_at.sem, pe_at.at(f"o_turned{hp // 2 - 1}"))
                    A.done(f"o{hp}", nc.vector.tensor_tensor(
                        o_tok[:, :, HD * par_h:HD * par_h + HD], aux[:, 3, 0:QB * HD].rearrange("p (b d) -> p b d", d=HD),
                        att_col[:, par_h, 3].unsqueeze(2).to_broadcast([P, QB, HD]), ALU.mult))
                    if h % 2 == 0:
                        t = h // 2 - 1
                        dve.wait_ge(act_at.sem, act_at.at(f"g_hi{t}"))
                        A.done(f"g_lo{t}", nc.vector.tensor_tensor(g_lo[:, t, 0:SEQ], aux[:, 2], g_hi[:, t, 0:SEQ].bitcast(F32), ALU.subtract))
            for n in range(KD):
                convert(N_OUT_A + n + 1, (n + 1) % 2)
                add_to_stream(N_OUT_A + n, n, n % 2)
                norm_tile(1, n)
            ffn(1, N_FFN0, 0)

            R, ppe, pact, ppool = pre["dve"], pre["pe"], pre["act"], pre["pool"]

            def own(steps, name, turn=0):
                dve.wait_ge(steps.sem, steps.at(name, turn))

            own(pact, "wab_hi")
            R.done("wab_lo", nc.vector.tensor_tensor(wab_lo[:], wab_pad[:], wab_hi[:].bitcast(F32), ALU.subtract))
            convert(N_IN_C + 1, 1)
            dve.wait_ge(rstd_made, 3)
            own(ppe, "ab")
            R.done("ab", nc.vector.tensor_tensor(halves(ab[0:64]), aux[0:64, 2:4, 0:TH], halves(rstd[0:64]), ALU.mult))
            own(pact, "exp_b")
            R.done("beta1", nc.vector.tensor_scalar(abt[0:8, 0], abt[0:8, 0], 1.0, None, ALU.add))
            own(R, "beta1")
            own(ppool, "rows_zero")
            R.done("beta", nc.vector.reciprocal(rows[0:8], abt[0:8, 0]))
            dve.wait_ge(acol_in, 32)
            R.done("dt", nc.vector.tensor_scalar(abt[32:40, 0], ab[32:40], acol[32:40, 1:2], None, ALU.add))
            own(R, "dt")
            R.done("abs", nc.vector.scalar_tensor_tensor(abt[32:40, 1], abt[32:40, 0], -1.0, abt[32:40, 0], ALU.mult, ALU.min))
            own(pact, "ln_sp")
            R.done("sp", nc.vector.scalar_tensor_tensor(abt[32:40, 2], abt[32:40, 0], 0.0, abt[32:40, 1], ALU.max, ALU.add))
            own(pact, "exp_a")
            R.done("nega", nc.vector.tensor_scalar(acol[32:40, 3:4], acol[32:40, 2:3], -1.0, None, ALU.mult))
            own(R, "nega")
            R.done("g", nc.vector.tensor_scalar(abt[32:40, 0], abt[32:40, 2], acol[32:40, 3:4], None, ALU.mult))
            own(R, "g")
            R.done("cum", nc.vector.tensor_tensor_scan(rows[32:40], delta[32:40, G_KEEP:G_KEEP + T], abt[32:40, 0], 0.0, ALU.mult, ALU.add))
            for half in range(2):
                own(ppe, f"chist{half}")
                R.done(f"chist{half}", nc.vector.tensor_copy(chist[:, 12 * half:12 * half + 12].rearrange("p t b i -> p (t b i)"), aux[:, half, 0:288]))
            own(R, "chist1")
            for i in range(CONV - 1):
                dst = cprod if i == 0 else ctmp
                if i == 2:
                    own(R, "sum1")
                R.done(f"prod{i}", nc.vector.tensor_tensor(dst[:], chist[:, :, :, i], wconv[:, i].unsqueeze(2).to_broadcast([P, 3 * GH, NS]), ALU.mult))
                if i:
                    own(R, f"prod{i}")
                    R.done(f"sum{i}", nc.vector.tensor_tensor(cprod[:], cprod[:], ctmp[:], ALU.add))
            own(ppe, "rows_turned")
            R.done("tokcols", nc.vector.tensor_copy(tokcols[:].rearrange("p c m -> p (c m)"), aux[:, 2, 0:256]))

            G, A, B = gg["dve"], ga["dve"], gb["dve"]
            identity = ident.unsqueeze(1).to_broadcast([P, QB, P])

            def turn(it, g_on, a_on, b_on):
                ha, hb = it - 1, it - 2
                n0 = N_IN_C + 4 * it

                def wait(steps, name, h):
                    dve.wait_ge(steps.sem, steps.at(name, h))

                def chunk_col(row):
                    return tokcols[:, :, bass.ds(row + ha, 1)].to_broadcast([P, QB, P])

                def chunks(x):
                    return x[:, 0:SEQ].rearrange("p (c m) -> p c m", m=P)

                def conv(stage, name, r, h, zslot, taps=range(CONV - 1)):
                    if taps[0] == 0:
                        wait(ga["act"] if name == "v" else gg["act"], f"tap_{name}", h)
                    for i in taps:
                        stage.done(f"tap_{name}{i}", nc.vector.scalar_tensor_tensor(
                            y[:, r, 0:SEQ], zc[:, zslot, i:i + SEQ], column(wconv[:, i], r * GH + h), y[:, r, 0:SEQ], ALU.mult, ALU.add))
                        wait(stage, f"tap_{name}{i}", h)
                    if taps[-1] == CONV - 2:
                        stage.done(f"tap_{name}3", nc.vector.tensor_tensor(y[:, r, SEQ:T], y[:, r, SEQ:T], cprod[:, r * GH + h], ALU.add))

                def rows_out(stage, name, r, h, slot):
                    wait(ga["pe"] if name == "v" else gg["pe"], f"tail_{name}", h)
                    stage.done(f"z_{name}", nc.vector.tensor_copy(z_rows[0:11, r], acc[0:11, 2 * slot, TH:TH + P]))

                def one_plus_p(n):
                    if a_on:
                        wait(ga["pe"], f"p{n}", ha)
                        one = ident.rearrange("p (k two s) -> p k two s", two=2, s=1 << n)[:, :, 0, :]
                        k = P // (2 << n)
                        A.done(f"ip{n}", nc.vector.tensor_tensor(
                            half_cols(ip[:, n - 1], n).rearrange("p (c k) s -> p c k s", c=QB), packed(0, n).rearrange("p (c k) s -> p c k s", c=QB),
                            one.unsqueeze(1).to_broadcast([P, QB, k, 1 << n]), ALU.add))

                def to_tT(n):
                    if a_on:
                        if n == NL - 1:
                            wait(A, f"u{n - 1}", ha)
                            A.done("t_first", nc.vector.tensor_copy(half_cols(t_all, n), half_cols(tinvT, n)))
                        wait(ga["pe"], f"u{n}", ha)
                        if n == NL - 1:
                            A.done(f"u{n}", nc.vector.tensor_copy(half_cols(t_all, n, True), packed(0, n)))
                        else:
                            A.done(f"u{n}", nc.vector.tensor_copy(tinvT[:], blocks(aux[:, 1])))

                def new_state(c):
                    if not b_on:
                        return
                    wait(gb["pe"], f"s{c}", hb)
                    if c == 0:
                        B.done("s0", nc.vector.tensor_copy(state[:], aux[:, 2, 2 * P:3 * P]))
                    else:
                        wait(B, f"s{c - 1}", hb)
                        B.done(f"s{c}", nc.vector.scalar_tensor_tensor(state[:], state[:], sm[:, 6, c:c + 1], aux[:, 2, 2 * P:3 * P], ALU.mult, ALU.add))

                def residue(c):
                    if b_on:
                        wait(gb["pe"], f"ks{c}", hb)
                        B.done(f"r{c}", nc.vector.tensor_tensor(resid[:], vb[:, c], aux[:, 2, 0:P], ALU.subtract))

                if a_on:
                    if b_on:
                        wait(ga["pe"], "tail_v", hb)
                        wait(ga["act"], "tap_v", hb)
                    scaled(zc[:, 2, CONV - 1:], n0 - 1, 1)
                if g_on and a_on:
                    convert(n0 + 1, 1)
                new_state(0)
                if a_on:
                    wait(ga["pe"], "beta", ha)
                    A.done("betab", nc.vector.tensor_copy(halves(betab), auxv(0)))
                residue(1)
                if a_on:
                    rows_out(A, "v", 2, ha, 1)
                    wait(ga["act"], "gcb", ha)
                    A.done("diff", nc.vector.tensor_tensor(decay[:], chunks(gcb), chunk_col(32), ALU.subtract))
                    A.done("edk", nc.vector.tensor_tensor(edk[:], chunks(gcb)[:, :, P - 1], tokcols[:, :, bass.ds(32 + ha, 1)].rearrange("p c m -> p (c m)"), ALU.subtract))
                new_state(1)
                if a_on:
                    wait(ga["act"], "rs_q", ha)
                    A.done("qn", nc.vector.tensor_tensor(qn[:], y[:, 0], rqk[:, 0], ALU.mult))
                    wait(ga["act"], "rs_k", ha)
                    A.done("kn", nc.vector.tensor_tensor(kn[:], y[:, 1], rqk[:, 1], ALU.mult))
                residue(2)
                if a_on:
                    wait(ga["act"], "decay", ha)
                    A.done("bdecay", nc.vector.scalar_tensor_tensor(bdecay[:].rearrange("p c m -> p (c m)"), betab[:, 0:SEQ], -1.0,
                                                                    decay[:].rearrange("p c m -> p (c m)"), ALU.mult, ALU.mult))
                if g_on:
                    if a_on:
                        wait(gg["pe"], "tail_q", ha)
                        wait(gg["act"], "tap_q", ha)
                    scaled(zc[:, 0, CONV - 1:], n0, 0)
                if a_on:
                    wait(A, "bdecay", ha)
                    wait(ga["pe"], "kk", ha)
                    wait(ga["pool"], "lev0", ha)
                    A.done("diag", nc.vector.tensor_tensor(tinvT[:], blocks(aux[:, 0]), lev[:, 0], ALU.mult))
                    A.done("low", nc.vector.tensor_tensor(lowT[:], blocks(aux[:, 0]), bdecay[:], ALU.mult))
                    wait(A, "diag", ha)
                    A.done("one", nc.vector.tensor_tensor(tinvT[:], tinvT[:], identity, ALU.add))
                new_state(2)
                if g_on:
                    convert(n0 + 2, 0)
                residue(3)
                if a_on:
                    conv(A, "v", 2, ha, 2, range(0, 2))
                one_plus_p(1)
                if a_on:
                    conv(A, "v", 2, ha, 2, range(2, 3))
                if g_on:
                    if a_on:
                        dve.wait_ge(zr_stored, 32 * it)
                    rows_out(G, "q", 0, it, 0)
                new_state(3)
                if g_on:
                    conv(G, "q", 0, it, 0)
                to_tT(1)
                one_plus_p(2)
                if g_on:
                    scaled(zc[:, 1, CONV - 1:], n0 + 1, 1)
                if b_on:
                    wait(gb["pe"], "dk_turned", hb)
                    sx = aux[:, 2, 0:2 * NS].rearrange("p (b r) -> p b r", r=2)
                    B.done("dv", nc.vector.tensor_tensor(sm[:, 2], sm[:, 1], sx[:, :, 0], ALU.subtract))
                    wait(B, "dv", hb)
                    B.done("dqk", nc.vector.tensor_tensor(sm[:, 3], sm[:, 2], aux[:, 2, 2 * NS:3 * NS], ALU.mult))
                    wait(B, "dqk", hb)
                    B.done("do", nc.vector.tensor_tensor(yo[:, SEQ:T], sm[:, 3], sx[:, :, 1], ALU.add))
                if a_on:
                    A.done("qg", nc.vector.tensor_tensor(qg[:], qn[:], egb[:], ALU.mult))
                    A.done("kb", nc.vector.tensor_tensor(kbg[:], kn[:], betab[:], ALU.mult))
                    wait(A, "kb", ha)
                    A.done("kbg", nc.vector.tensor_tensor(kbg[:], kbg[:], egb[:], ALU.mult))
                to_tT(2)
                one_plus_p(3)
                if b_on:
                    wait(gb["pe"], "dv_turned", hb)
                    B.done("d_rows", nc.vector.tensor_copy(kv_rows[0:NS].rearrange("p r m -> p (r m)"), aux[0:NS, 2, P:3 * P]))
                if g_on:
                    convert(n0 + 3, 1)
                    rows_out(G, "k", 1, it, 1)
                if b_on:
                    wait(B, "d_rows", hb)
                    B.done("dvexp", nc.vector.tensor_tensor(dvexp[0:NS].rearrange("p a (c m) -> p (a c) m", m=P), kv_rows[0:NS, 1].unsqueeze(1).to_broadcast([NS, NS, P]),
                                                            ident[0:NS, 0:NS].unsqueeze(2).to_broadcast([NS, NS, P]), ALU.mult))
                to_tT(3)
                one_plus_p(4)
                if g_on:
                    conv(G, "k", 1, it, 1)
                to_tT(4)
                one_plus_p(5)
                if b_on:
                    wait(gb["pe"], "outer", hb)
                    wait(gb["pool"], "s_decayed", hb)
                    B.done("s_new", nc.vector.tensor_tensor(s_in[:].rearrange("p b m -> p (b m)"), s_in[:].rearrange("p b m -> p (b m)"),
                                                            aux[:, 2:4].rearrange("p a t -> p (a t)"), ALU.add))
                if b_on:
                    wait(gb["act"], "o_rs", hb)
                    B.done("on", nc.vector.scalar_tensor_tensor(yo[:], yo[:], par[:, 44:45], ors, ALU.mult, ALU.mult))
                    wait(B, "on", hb)
                    B.done("og", nc.vector.tensor_tensor(yo[:], yo[:], gateT[:, hb], ALU.mult))
                if a_on:
                    wait(ga["pe"], "turn_k", ha)
                    wait(ga["act"], "edk", ha)
                    A.done("kdec", nc.vector.tensor_tensor(kdec[:], blocks(aux[:, 3]), edk[:].unsqueeze(2).to_broadcast([P, QB, P]), ALU.mult))
                    A.done("dkq", nc.vector.tensor_tensor(sm[:, 0], qn[:, SEQ:T], kn[:, SEQ:T], ALU.mult))
                    wait(ga["act"], "silu_v", ha)
                    A.done("dvb", nc.vector.tensor_tensor(sm[:, 1], y[:, 2, SEQ:T], betab[:, SEQ:T], ALU.mult))
                    A.done("keep_k", nc.vector.tensor_copy(sm[:, 4], kn[:, SEQ:T]))
                    A.done("keep_e", nc.vector.tensor_copy(sm[:, 5], egb[:, SEQ:T]))
                    A.done("keep_c", nc.vector.tensor_copy(sm[:, 6, 0:QB], chunks(egb)[:, :, P - 1]))
                to_tT(5)
                one_plus_p(6)
                if g_on:
                    scaled(gateT[:, it], n0 + 2, 0)
                if a_on:
                    wait(ga["pe"], "turn_v", ha)
                    A.done("vb", nc.vector.tensor_tensor(vb[:], blocks(aux[:, 2]), chunk_col(0), ALU.mult))
                to_tT(6)
                if a_on:
                    wait(ga["pe"], "qk", ha)
                    A.done("attT", nc.vector.tensor_tensor(attT[:], blocks(aux[:, 1]), decay[:], ALU.mult))
                if g_on:
                    convert(n0 + 4, 0)
                if b_on:
                    wait(gb["act"], "g_hi", hb)
                    B.done("g_lo", nc.vector.tensor_tensor(g_lo[:, hb], yo[:], g_hi[:, hb].bitcast(F32), ALU.subtract))
                    dve.wait_ge(st_stored, 16 * (it - 1))

            own(ppool, "zc")
            turn(0, True, False, False)
            own(ppool, "ip_ones")
            turn(1, True, True, False)
            with dve.Fori(2, GH) as it:
                turn(it, True, True, True)
            turn(GH, False, True, True)
            convert(N_OUT_C + 1, 1)
            turn(GH + 1, False, False, True)

            def out(i):
                for s in range(2):
                    if s or not isinstance(i, int):
                        convert(N_OUT_C + 2 * i + s + 1, 1 - s)
                    add_to_stream(N_OUT_C + 2 * i + s, 2 * i + s, s)
                    norm_tile(3, 2 * i + s)

            out(0)
            with dve.Fori(1, KD // 2) as i:
                out(i)
            ffn(3, N_FFN1, FT)

            Z, zp, za = fin["dve"], fin["pe"], fin["act"]
            dve.wait_ge(za.sem, za.at("rstd_s"))
            for b, bank in ((0, acc[:, 0:2]), (2, aux[:, 0:2]), (4, acc[:, 2:4])):
                rows_b = P if b < QB else NS
                dve.wait_ge(zp.sem, zp.at(f"y{b}"))
                Z.done(f"y_tok{b}", nc.vector.tensor_scalar(y_tok[0:rows_b, b], bank[0:rows_b].rearrange("p a t -> p (a t)"),
                                                            r_tok[0:rows_b, 2 * b:2 * b + 1], None, ALU.mult))

        @block.gpsimd
        def _(pool):
            def add_squares(k):
                if k:
                    pool.wait_ge(ss_full, k)
                nc.gpsimd.memset(ssum[:], 0.0).then_inc(ss_clear, 1)
                pool.wait_ge(ss_clear, k + 1)

                def add(i):
                    for s in range(2):
                        before = KD * k + 2 * i + s
                        pool.wait_ge(sq_made, before + 1)
                        if k or s or not isinstance(i, int):
                            pool.wait_ge(ss_added, before)
                        nc.gpsimd.tensor_tensor(ssum[:], ssum[:], sq[:, s], ALU.add).then_inc(ss_added, 1)

                add(0)
                with pool.Fori(1, KD // 2) as i:
                    add(i)

            add_squares(0)
            A, up_dve, pe_at, dve_at, act_at = at["pool"], up["dve"], at["pe"], at["dve"], at["act"]
            pool.wait_ge(up_dve.sem, up_dve.all())
            pool.wait_ge(up["pe"].sem, up["pe"].all())
            pool.dma_start(cnt[:], a["pool_table"].rearrange("p (g t) -> p g t", g=4)).then_inc(pool_in, 16)
            pool.dma_start(wpool[:], a["w_pool"][0].rearrange("g c d -> c g d")).then_inc(pool_in, 16)
            pool.dma_start(hist_rows[0:120], a["state_pool"][0].rearrange("b j c -> (b j) c")).then_inc(hist_in, 16)
            pool.dma_start(sel8[0:NS], a["select_table"].rearrange("b (c m) -> b c m", m=P)).then_inc(sel_in, 16)
            pool.dma_start(dec_tab[0:64], a["decode_table"]).then_inc(sel_in, 16)
            pool.dma_start(att_tab[:], a["attention_table"].rearrange("p (r c) -> p r c", r=2)).then_inc(tab_in, 16)
            pool.wait_ge(pool_in, 32)
            for g in range(4):
                pool.wait_ge(acc_read, g + 1)
                src = zT[:, 12 + g]
                for n in range(g + 1):
                    dst, s = run[:, n % 2], 1 << n
                    A.done(f"run{g}{n}a", nc.gpsimd.tensor_tensor(dst[:, s:SEQ], src[:, s:SEQ], src[:, 0:SEQ - s], ALU.add))
                    A.done(f"run{g}{n}b", nc.gpsimd.tensor_copy(dst[:, 0:s], src[:, 0:s]))
                    pool.wait_ge(A.sem, A.at(f"run{g}{n}b"))
                    src = dst
                mean = run[:, (g + 1) % 2]
                A.done(f"mean{g}", nc.gpsimd.tensor_tensor(mean[:, 0:SEQ], src[:, 0:SEQ], cnt[:, g, 0:SEQ], ALU.mult))
                pool.wait_ge(A.sem, A.at(f"mean{g}"))
                if g >= 2:
                    pool.wait_ge(pe_at.sem, pe_at.at(f"pooled{g - 2}"))
                A.done(f"pool{g}", nc.gpsimd.tensor_tensor(pooled[:, g % 2, 0:SEQ], mean[:, 0:SEQ], zT[:, 12 + g, 0:SEQ], ALU.subtract))
                pool.wait_ge(A.sem, A.at(f"pool{g}"))
            for t in range(4):
                pool.wait_ge(act_at.sem, act_at.at(f"k_kept{t}"))
                pool.dma_start(o["a_k_prompt"][0, 0].rearrange("(b p) h d -> p b (h d)", p=P)[:, :, t * P:(t + 1) * P],
                               k_stage[:, t % 2]).then_inc(k_stored[t % 2], 16)
            pool.wait_ge(dve_at.sem, dve_at.at("v_kept3"))
            pool.dma_start(o["a_v_prompt"][0, 0].rearrange("(b p) h d -> p b (h d)", p=P), v_tok[:]).then_inc(stored, 16)
            pool.wait_ge(dve_at.sem, dve_at.at("z_kept"))
            pool.dma_start(o["pool_prompt"][0, 0], u_tok[0:POOL_HIST]).then_inc(stored, 16)
            pool.dma_start(o["pool_sample"][0, :, POOL_HIST - 1, :], u_tok[POOL_HIST:POOL_HIST + NS]).then_inc(stored, 16)
            pool.dma_start(o["a_k_sample"][0].rearrange("b t h d -> b t (h d)")[:, PAST], z_tok[0:NS, 1]).then_inc(stored, 16)
            pool.dma_start(o["a_v_sample"][0].rearrange("b t h d -> b t (h d)")[:, PAST], z_tok[0:NS, 2]).then_inc(stored, 16)
            add_squares(1)
            R = pre["pool"]
            pool.wait_ge(acc_full, N_OUT_A + 1)
            for q in range(2):
                pool.wait_ge(k_stored[q], 32)
            pool.wait_ge(stored, 16 * 5)
            pool.dma_start(delta[:], a["delta_table"]).then_inc(delta_in, 16)
            pool.dma_start(crow[0:3 * NS], a["state_conv"][0].rearrange("b i c -> (b i) c")).then_inc(crow_in, 16)
            pool.dma_start(wab_raw[:], w_in_c[:, 4 * QK:].rearrange("(k p) m -> p k m", p=P)).then_inc(wab_in, 16)
            pool.dma_start(acol[32:40, 0:1], a["a_log_c"].rearrange("o h -> h o")).then_inc(acol_in, 16)
            pool.dma_start(acol[32:40, 1:2], a["dt_bias_c"].rearrange("o h -> h o")).then_inc(acol_in, 16)
            R.done("wab_zero", nc.gpsimd.memset(wab_pad[:], 0.0))
            pool.wait_ge(wab_in, 16)
            pool.wait_ge(R.sem, R.at("wab_zero"))
            R.done("wab_pad_b", nc.gpsimd.tensor_copy(wab_pad[:, :, 0:GH], wab_raw[:, :, 0:GH]))
            R.done("wab_pad_a", nc.gpsimd.tensor_copy(wab_pad[:, :, 32:32 + GH], wab_raw[:, :, GH:2 * GH]))
            R.done("rows_zero", nc.gpsimd.memset(rows[:], 0.0))
            add_squares(2)
            pool.wait_ge(acc_read, N_IN_C)
            pool.wait_ge(g_lo_made, FT)
            R.done("zc", nc.gpsimd.memset(zc[:, :, 0:CONV - 1], 0.0))
            pool.wait_ge(pre["dve"].sem, pre["dve"].all())

            R.done("ip_ones", nc.gpsimd.tensor_copy(ip[:].rearrange("p n c m -> p (n c) m"), ident.unsqueeze(1).to_broadcast([P, (NL - 1) * QB, P])))
            A, B = ga["pool"], gb["pool"]

            def turn(it, a_on, b_on):
                ha, hb = it - 1, it - 2

                def wait(steps, name, h):
                    pool.wait_ge(steps.sem, steps.at(name, h))

                def level(n):
                    if a_on:
                        mask = delta[:, G_LEVEL + n * P:G_LEVEL + (n + 1) * P].unsqueeze(1).to_broadcast([P, QB, P])
                        A.done(f"lev{n}", nc.gpsimd.tensor_tensor(lev[:, n % 2], lowT[:], mask, ALU.mult))

                if a_on:
                    if b_on:
                        wait(ga["pe"], "beta", hb)
                    A.done("rowsel", nc.gpsimd.tensor_tensor(rowsel[0:64], rows[0:64], delta[0:64, bass.ds(G_SEL + ha, 1)].to_broadcast([64, T]), ALU.mult))
                    wait(ga["dve"], "diff", ha)
                    tri = delta[:, G_TRI:G_TRI + P].unsqueeze(1).to_broadcast([P, QB, P])
                    A.done("mask", nc.gpsimd.tensor_tensor(decay[:], decay[:], tri, ALU.add))
                    wait(ga["dve"], "bdecay", ha)
                    mask0 = delta[:, G_LEVEL:G_LEVEL + P].unsqueeze(1).to_broadcast([P, QB, P])
                    A.done("lev0", nc.gpsimd.tensor_tensor(lev[:, 0], bdecay[:], mask0, ALU.mult))
                    wait(ga["dve"], "low", ha)
                    level(1)
                    wait(ga["dve"], "one", ha)
                    level(2)
                    for n in (3, 4):
                        wait(ga["pe"], f"p{n - 2}", ha)
                        level(n)
                if b_on:
                    pool.wait_ge(s_read, 16 * hb + 16)
                    wait(gb["pe"], "dx", hb)
                    B.done("s_decayed", nc.gpsimd.tensor_tensor(s_in[:], s_in[:], sm[:, 5].unsqueeze(2).to_broadcast([P, NS, P]), ALU.mult))
                if a_on:
                    for n in (5, 6):
                        wait(ga["pe"], f"p{n - 2}", ha)
                        level(n)

            turn(1, True, False)
            with pool.Fori(2, GH) as it:
                turn(it, True, True)
            turn(GH, True, True)
            turn(GH + 1, False, True)
            add_squares(3)
            add_squares(4)


_OUTS = {
    "y_prompt": (1, 512, 1024), "y_sample": (8, 1, 1024),
    "a_k_prompt": (1, 1, 512, 8, 64), "a_v_prompt": (1, 1, 512, 8, 64),
    "pool_prompt": (1, 1, 15, 512), "conv_prompt": (1, 1, 3, 3072), "gdn_prompt": (1, 1, 8, 128, 128),
    "a_k_sample": (1, 8, 513, 8, 64), "a_v_sample": (1, 8, 513, 8, 64),
    "pool_sample": (1, 8, 15, 512), "conv_sample": (1, 8, 3, 3072), "gdn_sample": (1, 8, 8, 128, 128),
}


def kernel(**inputs):
    import numpy as _np
    import concourse.bacc as _bacc
    from concourse import mybir as _mybir
    from concourse.bass_utils import run_bass_kernel_spmd as _run

    arrays = {name: _np.ascontiguousarray(x) for name, x in inputs.items()}
    arrays["par_rows"] = _np.concatenate([arrays[n].reshape(-1, P) for n in (
        "norm_mix", "norm_ffn", "norm_final", "pool_scale", "norm_out_c")], 0)
    arrays["const_table"], arrays["delta_table"] = constant_table(), delta_table()
    arrays["attention_table"], arrays["decode_table"] = attention_table(), decode_table()
    arrays["pool_table"], arrays["select_table"] = pool_table(), select_table()
    used = [n for n in arrays if n not in ("norm_mix", "norm_ffn", "norm_final", "pool_scale", "norm_out_c")]
    nc = _bacc.Bacc("TRN2", target_bir_lowering=False, num_devices=1)
    a = {n: nc.dram_tensor(f"in_{n}", arrays[n].shape, _mybir.dt.from_np(arrays[n].dtype), kind="ExternalInput").ap() for n in used}
    o = {n: nc.dram_tensor(f"out_{n}", shape, F32, kind="ExternalOutput").ap() for n, shape in _OUTS.items()}
    build(nc, a, o)
    r = _run(nc, [{f"in_{n}": arrays[n] for n in used}], core_ids=[0])
    return tuple(r.results[0][f"out_{n}"] for n in _OUTS)
```
